# Optimizing a Trainium2 kernel written in Bass

```python
import math
import jax, jax.numpy as jnp
from jax import lax
import numpy as np

D_MODEL = 1024
BATCH = 1
SEQ = 256
DEPTH = 2

N_MIXERS = 2
D_FF = 4 * D_MODEL
NORM_EPS = 1e-6
GLA_HEADS = 4
GLA_DK = D_MODEL // 2 // GLA_HEADS
GLA_DV = D_MODEL // GLA_HEADS
GLA_GATE_RANK = 16
GLA_TAU = 16.0
GLA_CHUNK = 64
GLA_IN = 2 * GLA_HEADS * GLA_DK + 2 * D_MODEL + GLA_GATE_RANK
DIFF_HEADS = 8
DIFF_DH = D_MODEL // DIFF_HEADS // 2
DIFF_DV = 2 * DIFF_DH
DIFF_IN = 3 * D_MODEL
ROPE_THETA = 500000.0
ROPE_DIM = DIFF_DH // 4
Q_BLOCK = 128
N_GLA = (DEPTH + 1) // 2
N_DIFF = DEPTH // 2


def rmsnorm(x, g):
    xf = x.astype(jnp.float32)
    y = xf * lax.rsqrt(jnp.mean(xf * xf, axis=-1, keepdims=True) + NORM_EPS)
    return (y * g.astype(jnp.float32)).astype(x.dtype)

def rope_partial(x, cos, sin):
    half = ROPE_DIM // 2
    cos = cos.astype(x.dtype)
    sin = sin.astype(x.dtype)
    x1 = x[..., :half]
    x2 = x[..., half:ROPE_DIM]
    rest = x[..., ROPE_DIM:]
    return jnp.concatenate([x1 * cos - x2 * sin, x2 * cos + x1 * sin, rest], axis=-1)

def gla_mixer(h, w_in, w_a2, b_a, b_r, norm_g, w_o):
    B, T, _ = h.shape
    H, dk, dv, C = GLA_HEADS, GLA_DK, GLA_DV, GLA_CHUNK
    n = T // C
    hk = H * dk
    f32 = jnp.float32
    q, k, v, r, a_lr = jnp.split(h @ w_in, [hk, 2 * hk, 2 * hk + D_MODEL, 2 * hk + 2 * D_MODEL], axis=-1)
    log_a = jax.nn.log_sigmoid((a_lr @ w_a2 + b_a).astype(f32)) / GLA_TAU

    def chunks(t, d):
        return t.reshape(B, n, C, H, d)

    q = chunks(q.astype(f32), dk) * (dk ** -0.5)
    k = chunks(k.astype(f32), dk)
    v = chunks(v.astype(f32), dv)
    b = jnp.cumsum(chunks(log_a, dk), axis=2)
    b_last = b[:, :, -1:]
    q_dec = q * jnp.exp(b)
    k_intra = k * jnp.exp(-b)
    k_state = k * jnp.exp(b_last - b)

    causal = jnp.tril(jnp.ones((C, C), dtype=bool))
    scores = jnp.einsum('bnchk,bnshk->bnhcs', q_dec, k_intra)
    scores = jnp.where(causal, scores, 0.0)
    o_intra = jnp.einsum('bnhcs,bnshv->bnchv', scores, v)

    def step(state, inp):
        q_c, k_c, v_c, decay = inp
        o_c = jnp.einsum('bchk,bhkv->bchv', q_c, state)
        state = state * jnp.exp(decay)[..., None] + jnp.einsum('bchk,bchv->bhkv', k_c, v_c)
        return state, o_c

    xs = (jnp.moveaxis(q_dec, 1, 0), jnp.moveaxis(k_state, 1, 0),
          jnp.moveaxis(v, 1, 0), jnp.moveaxis(b_last[:, :, 0], 1, 0))
    s0 = jnp.zeros((B, H, dk, dv), f32)
    _, o_inter = lax.scan(step, s0, xs)
    o = o_intra + jnp.moveaxis(o_inter, 0, 1)
    o = rmsnorm(o, norm_g).reshape(B, T, D_MODEL)
    o = o * jax.nn.silu((r + b_r).astype(f32))
    return o.astype(h.dtype) @ w_o

def diff_mixer(h, cos, sin, w_in, lam_vecs, subln_g, w_o, lambda_init):
    B, T, _ = h.shape
    H, dh, dv = DIFF_HEADS, DIFF_DH, DIFF_DV
    f32 = jnp.float32
    q, k, v = jnp.split(h @ w_in, 3, axis=-1)
    q = rope_partial(q.reshape(B, T, H, 2, dh), cos, sin) * (dh ** -0.5)
    k = rope_partial(k.reshape(B, T, H, 2, dh), cos, sin)
    q = q.transpose(0, 2, 3, 1, 4)
    k = k.transpose(0, 2, 3, 1, 4)
    v = v.reshape(B, T, H, dv).transpose(0, 2, 1, 3)
    lf = lam_vecs.astype(f32)
    lam = jnp.exp(jnp.sum(lf[0] * lf[1])) - jnp.exp(jnp.sum(lf[2] * lf[3])) + lambda_init
    outs = []
    for i in range(T // Q_BLOCK):
        L = (i + 1) * Q_BLOCK
        qb = q[:, :, :, i * Q_BLOCK:L]
        s = jnp.einsum('bhiqd,bhikd->bhiqk', qb, k[:, :, :, :L]).astype(f32)
        q_idx = i * Q_BLOCK + jnp.arange(Q_BLOCK)
        mask = jnp.arange(L)[None, :] <= q_idx[:, None]
        p = jax.nn.softmax(jnp.where(mask, s, -jnp.inf), axis=-1)
        a = p[:, :, 0] - lam * p[:, :, 1]
        outs.append(jnp.einsum('bhqk,bhkv->bhqv', a.astype(v.dtype), v[:, :, :L]))
    o = jnp.concatenate(outs, axis=2)
    o = rmsnorm(o, subln_g) * (1.0 - lambda_init)
    o = o.transpose(0, 2, 1, 3).reshape(B, T, D_MODEL)
    return o @ w_o

def first_inputs(seed: int = 0) -> dict:
    key = jax.random.key(seed)
    ks = jax.random.split(key, 24)
    D = D_MODEL
    nrm = jax.random.normal
    x = nrm(ks[0], (BATCH, SEQ, D), jnp.float32)
    c = nrm(ks[1], (BATCH, D), jnp.float32)
    offsets = jax.random.randint(ks[2], (BATCH, 1), 0, 4096, dtype=jnp.int32)
    positions = (offsets + jnp.arange(SEQ, dtype=jnp.int32)[None, :]).astype(jnp.int32)
    return {
        "x": x,
        "c": c,
        "positions": positions,
        "ada_w": nrm(ks[3], (DEPTH, D, 6 * D), jnp.float32) * (0.5 * D ** -0.5),
        "ada_b": nrm(ks[4], (DEPTH, 6 * D), jnp.float32) * 0.02,
        "norm_g": 1.0 + 0.05 * nrm(ks[5], (DEPTH, 2, D), jnp.float32),
        "mlp_w1": nrm(ks[6], (DEPTH, D, D_FF), jnp.float32) * D ** -0.5,
        "mlp_w2": nrm(ks[7], (DEPTH, D_FF, D), jnp.float32) * D_FF ** -0.5,
        "gla_w_in": nrm(ks[8], (N_GLA, D, GLA_IN), jnp.float32) * D ** -0.5,
        "gla_w_a2": nrm(ks[9], (N_GLA, GLA_GATE_RANK, GLA_HEADS * GLA_DK), jnp.float32) * GLA_GATE_RANK ** -0.5,
        "gla_b_a": 0.5 + 0.1 * nrm(ks[10], (N_GLA, GLA_HEADS * GLA_DK), jnp.float32),
        "gla_b_r": 0.02 * nrm(ks[11], (N_GLA, D), jnp.float32),
        "gla_norm_g": 1.0 + 0.05 * nrm(ks[12], (N_GLA, GLA_DV), jnp.float32),
        "gla_w_o": nrm(ks[13], (N_GLA, D, D), jnp.float32) * D ** -0.5,
        "diff_w_in": nrm(ks[14], (N_DIFF, D, DIFF_IN), jnp.float32) * D ** -0.5,
        "diff_lambda": 0.1 * nrm(ks[15], (N_DIFF, 4, DIFF_DH), jnp.float32),
        "diff_subln_g": 1.0 + 0.05 * nrm(ks[16], (N_DIFF, DIFF_DV), jnp.float32),
        "diff_w_o": nrm(ks[17], (N_DIFF, D, D), jnp.float32) * D ** -0.5,
        "final_g": 1.0 + 0.05 * nrm(ks[18], (D,), jnp.float32),
    }

def first_block(x, c, positions, ada_w, ada_b, norm_g, mlp_w1, mlp_w2,
              gla_w_in, gla_w_a2, gla_b_a, gla_b_r, gla_norm_g, gla_w_o,
              diff_w_in, diff_lambda, diff_subln_g, diff_w_o, final_g):
    f32 = jnp.float32
    inv_freq = ROPE_THETA ** (-jnp.arange(0, ROPE_DIM, 2, dtype=f32) / ROPE_DIM)
    ang = positions.astype(f32)[..., None] * inv_freq
    cos = jnp.cos(ang)[:, :, None, None, :]
    sin = jnp.sin(ang)[:, :, None, None, :]
    c_act = jax.nn.silu(c)
    for i in range(DEPTH):
        mod = c_act @ ada_w[i] + ada_b[i]
        shift_t, scale_t, gate_t, shift_c, scale_c, gate_c = [
            m[:, None, :] for m in jnp.split(mod, 6, axis=-1)]
        h = rmsnorm(x, norm_g[i, 0]) * (1.0 + scale_t) + shift_t
        j = i // N_MIXERS
        if i % N_MIXERS == 0:
            y = gla_mixer(h, gla_w_in[j], gla_w_a2[j], gla_b_a[j], gla_b_r[j],
                          gla_norm_g[j], gla_w_o[j])
        else:
            lambda_init = 0.8 - 0.6 * math.exp(-0.3 * i)
            y = diff_mixer(h, cos, sin, diff_w_in[j], diff_lambda[j], diff_subln_g[j],
                           diff_w_o[j], lambda_init)
        x = x + gate_t * y
        h = rmsnorm(x, norm_g[i, 1]) * (1.0 + scale_c) + shift_c
        y = jnp.square(jax.nn.relu(h @ mlp_w1[i])) @ mlp_w2[i]
        x = x + gate_c * y
    return rmsnorm(x, final_g)


EPS = 1e-6
BLOCK = 128
RET_HEADS = D_MODEL // 256
RET_DK = 256
RET_DV = 2 * RET_DK
RET_QK = RET_HEADS * RET_DK
RET_V = RET_HEADS * RET_DV
RET_IN = 2 * RET_QK + 2 * RET_V
ROPE_BASE = 10000.0
SB_HEADS = D_MODEL // 64
SB_DH = 64
SB_IN = 3 * SB_HEADS * SB_DH
D_FF_2 = 2816
CONV_W = 3


def _rmsnorm(x, g):
    xf = x.astype(jnp.float32)
    y = xf * lax.rsqrt(jnp.mean(xf * xf, axis=-1, keepdims=True) + EPS)
    return (y * g.astype(jnp.float32)).astype(x.dtype)

def _rotary(x, cos, sin):
    x1, x2 = jnp.split(x, 2, axis=-1)
    c = cos[None, :, None, :]
    s = sin[None, :, None, :]
    return jnp.concatenate([x1 * c - x2 * s, x1 * s + x2 * c], axis=-1)

def _retention(h, w_in, w_out):
    B_, S_, _ = h.shape
    nc = S_ // BLOCK
    proj = h @ w_in
    q, k, v, g = jnp.split(proj, [RET_QK, 2 * RET_QK, 2 * RET_QK + RET_V], axis=-1)
    pos = jnp.arange(S_, dtype=jnp.float32)
    inv_freq = ROPE_BASE ** (-jnp.arange(0, RET_DK, 2, dtype=jnp.float32) / RET_DK)
    ang = pos[:, None] * inv_freq[None, :]
    cos, sin = jnp.cos(ang), jnp.sin(ang)
    q = _rotary(q.reshape(B_, S_, RET_HEADS, RET_DK).astype(jnp.float32), cos, sin)
    k = _rotary(k.reshape(B_, S_, RET_HEADS, RET_DK).astype(jnp.float32), cos, sin) * (RET_DK ** -0.5)
    v = v.reshape(B_, S_, RET_HEADS, RET_DV).astype(jnp.float32)
    qc = q.transpose(0, 2, 1, 3).reshape(B_, RET_HEADS, nc, BLOCK, RET_DK)
    kc = k.transpose(0, 2, 1, 3).reshape(B_, RET_HEADS, nc, BLOCK, RET_DK)
    vc = v.transpose(0, 2, 1, 3).reshape(B_, RET_HEADS, nc, BLOCK, RET_DV)
    log_g = jnp.log(1.0 - 2.0 ** (-5.0 - jnp.arange(RET_HEADS, dtype=jnp.float32)))
    cpos = jnp.arange(BLOCK, dtype=jnp.float32)
    diff = cpos[:, None] - cpos[None, :]
    dmat = jnp.where(diff[None] >= 0,
                     jnp.exp(jnp.maximum(diff, 0.0)[None] * log_g[:, None, None]), 0.0)
    scores = jnp.einsum('bhncd,bhnkd->bhnck', qc, kc) * dmat[None, :, None]
    intra = jnp.einsum('bhnck,bhnke->bhnce', scores, vc)
    q_dec = qc * jnp.exp((cpos + 1.0)[None, :] * log_g[:, None])[None, :, None, :, None]
    k_dec = kc * jnp.exp((BLOCK - 1.0 - cpos)[None, :] * log_g[:, None])[None, :, None, :, None]
    chunk_decay = jnp.exp(BLOCK * log_g)[None, :, None, None]

    def step(state, xs):
        qd, kd, vv = xs
        out = jnp.einsum('bhcd,bhde->bhce', qd, state)
        state = chunk_decay * state + jnp.einsum('bhkd,bhke->bhde', kd, vv)
        return state, out

    state0 = jnp.zeros((B_, RET_HEADS, RET_DK, RET_DV), jnp.float32)
    _, cross = lax.scan(step, state0, (jnp.moveaxis(q_dec, 2, 0), jnp.moveaxis(k_dec, 2, 0),
                                       jnp.moveaxis(vc, 2, 0)))
    o = intra + jnp.moveaxis(cross, 0, 2)
    o = o.reshape(B_, RET_HEADS, S_, RET_DV)
    o = o * lax.rsqrt(jnp.mean(o * o, axis=-1, keepdims=True) + EPS)
    o = o.transpose(0, 2, 1, 3).reshape(B_, S_, RET_V)
    y = jax.nn.silu(g.astype(jnp.float32)) * o
    return y.astype(h.dtype) @ w_out

def _stick_breaking(h, w_in, w_out):
    B_, S_, _ = h.shape
    nb = S_ // BLOCK
    scale = 1.0 / math.sqrt(SB_DH)
    proj = h @ w_in
    q, k, v = jnp.split(proj, 3, axis=-1)
    to_heads = lambda a: a.reshape(B_, S_, SB_HEADS, SB_DH).transpose(0, 2, 1, 3).astype(jnp.float32)
    q, k, v = to_heads(q), to_heads(k), to_heads(v)
    outs = []
    for i in range(nb):
        qb = q[:, :, i * BLOCK:(i + 1) * BLOCK]
        t_pos = i * BLOCK + jnp.arange(BLOCK)
        kp = jnp.moveaxis(k[:, :, :(i + 1) * BLOCK].reshape(B_, SB_HEADS, i + 1, BLOCK, SB_DH), 2, 0)
        vp = jnp.moveaxis(v[:, :, :(i + 1) * BLOCK].reshape(B_, SB_HEADS, i + 1, BLOCK, SB_DH), 2, 0)

        def step(carry, xs, qb=qb, t_pos=t_pos):
            suffix, acc = carry
            kb, vb, j = xs
            z = jnp.einsum('bhqd,bhkd->bhqk', qb, kb) * scale
            s_pos = j * BLOCK + jnp.arange(BLOCK)
            mask = s_pos[None, :] < t_pos[:, None]
            log1m = jnp.where(mask, jax.nn.log_sigmoid(-z), 0.0)
            excl = lax.cumsum(log1m, axis=3, reverse=True) - log1m
            log_a = jax.nn.log_sigmoid(z) + excl + suffix[..., None]
            a = jnp.where(mask, jnp.exp(log_a), 0.0)
            acc = acc + jnp.einsum('bhqk,bhkd->bhqd', a, vb)
            suffix = suffix + jnp.sum(log1m, axis=3)
            return (suffix, acc), None

        init = (jnp.zeros((B_, SB_HEADS, BLOCK), jnp.float32),
                jnp.zeros((B_, SB_HEADS, BLOCK, SB_DH), jnp.float32))
        (_, acc), _ = lax.scan(step, init, (kp, vp, jnp.arange(i + 1)), reverse=True)
        outs.append(acc)
    o = jnp.concatenate(outs, axis=2)
    o = o.transpose(0, 2, 1, 3).reshape(B_, S_, SB_HEADS * SB_DH)
    return o.astype(h.dtype) @ w_out

def _conv_ffn(h, w_up, conv_w, conv_b, w_down):
    u = h @ w_up
    u = lax.conv_general_dilated(u, conv_w[:, None, :].astype(u.dtype), window_strides=(1,),
                                 padding=[(CONV_W - 1, 0)],
                                 dimension_numbers=('NWC', 'WIO', 'NWC'),
                                 feature_group_count=2 * D_FF_2) + conv_b
    gate, val = jnp.split(u, 2, axis=-1)
    return (jax.nn.silu(gate) * val) @ w_down

def second_inputs(seed: int = 0) -> dict:
    key = jax.random.key(seed)
    ks = jax.random.split(key, 16)
    n_ret = (DEPTH + 1) // 2
    n_sb = DEPTH // 2
    nrm = lambda k, shape, fan_in: jax.random.normal(k, shape, jnp.float32) * fan_in ** -0.5
    gain = lambda k, shape: 1.0 + 0.02 * jax.random.normal(k, shape, jnp.float32)
    return {
        "x": jax.random.normal(ks[0], (BATCH, SEQ, D_MODEL), jnp.float32),
        "ret_norm": gain(ks[1], (n_ret, D_MODEL)),
        "ret_w_in": nrm(ks[2], (n_ret, D_MODEL, RET_IN), D_MODEL),
        "ret_w_out": nrm(ks[3], (n_ret, RET_V, D_MODEL), RET_V),
        "sb_norm": gain(ks[4], (n_sb, D_MODEL)),
        "sb_w_in": nrm(ks[5], (n_sb, D_MODEL, SB_IN), D_MODEL),
        "sb_w_out": nrm(ks[6], (n_sb, SB_HEADS * SB_DH, D_MODEL), SB_HEADS * SB_DH),
        "ffn_norm": gain(ks[7], (DEPTH, D_MODEL)),
        "ffn_w_up": nrm(ks[8], (DEPTH, D_MODEL, 2 * D_FF_2), D_MODEL),
        "ffn_conv_w": nrm(ks[9], (DEPTH, CONV_W, 2 * D_FF_2), CONV_W),
        "ffn_conv_b": 0.02 * jax.random.normal(ks[10], (DEPTH, 2 * D_FF_2), jnp.float32),
        "ffn_w_down": nrm(ks[11], (DEPTH, D_FF_2, D_MODEL), D_FF_2),
        "final_norm": gain(ks[12], (D_MODEL,)),
    }

def second_block(x, ret_norm, ret_w_in, ret_w_out, sb_norm, sb_w_in, sb_w_out,
              ffn_norm, ffn_w_up, ffn_conv_w, ffn_conv_b, ffn_w_down, final_norm):
    for i in range(DEPTH):
        j = i // N_MIXERS
        if i % N_MIXERS == 0:
            x = x + _retention(_rmsnorm(x, ret_norm[j]), ret_w_in[j], ret_w_out[j])
        else:
            x = x + _stick_breaking(_rmsnorm(x, sb_norm[j]), sb_w_in[j], sb_w_out[j])
        x = x + _conv_ffn(_rmsnorm(x, ffn_norm[i]), ffn_w_up[i], ffn_conv_w[i],
                          ffn_conv_b[i], ffn_w_down[i])
    return _rmsnorm(x, final_norm)


def setup_inputs(seed=0):
    out = dict(first_inputs(seed))
    for name, value in second_inputs(seed + 1).items():
        if name != "x":
            out[name + "_2"] = value
    return out


def reference(
    x, c, positions, ada_w, ada_b, norm_g, mlp_w1, mlp_w2, gla_w_in, gla_w_a2, gla_b_a, gla_b_r,
    gla_norm_g, gla_w_o, diff_w_in, diff_lambda, diff_subln_g, diff_w_o, final_g, ret_norm_2,
    ret_w_in_2, ret_w_out_2, sb_norm_2, sb_w_in_2, sb_w_out_2, ffn_norm_2, ffn_w_up_2,
    ffn_conv_w_2, ffn_conv_b_2, ffn_w_down_2, final_norm_2,
):
    x = first_block(
        x, c, positions, ada_w, ada_b, norm_g, mlp_w1, mlp_w2, gla_w_in, gla_w_a2, gla_b_a,
        gla_b_r, gla_norm_g, gla_w_o, diff_w_in, diff_lambda, diff_subln_g, diff_w_o, final_g,
    )
    return second_block(
        x, ret_norm_2, ret_w_in_2, ret_w_out_2, sb_norm_2, sb_w_in_2, sb_w_out_2, ffn_norm_2,
        ffn_w_up_2, ffn_conv_w_2, ffn_conv_b_2, ffn_w_down_2, final_norm_2,
    )


_drawn_inputs = setup_inputs


def setup_inputs(seed=0):
    import zlib

    import numpy as np

    out = dict(_drawn_inputs(seed))
    spreads = {}
    factors = {'gla_b_a': 3.28,
     'gla_b_r': 8.0,
     'gla_norm_g': 3.488,
     'diff_subln_g': 3.161,
     'sb_norm_2': 5.107,
     'ffn_norm_2': 3.095,
     'ffn_conv_b_2': 3.135,
     'final_norm_2': 2.82}
    for name, (base, spread) in spreads.items():
        noise = np.random.default_rng([zlib.crc32(name.encode()), seed]).standard_normal(out[name].shape)
        drawn = base * np.exp(spread * noise) if base else spread * noise
        out[name] = __import__('jax').numpy.asarray(drawn.astype(out[name].dtype))
    for name, factor in factors.items():
        out[name] = (out[name] * factor).astype(out[name].dtype)
    return out
```

```python
import math

import numpy as np
import concourse.bass as bass
from concourse import mybir
from contextlib import ExitStack

P = 128
T = 256
TT = T // P
D = 1024
KT = D // P
DEPTH = 2
F_MLP = 4 * D
EPS = 1e-6
GH_, GDK, GDV, GCH = 4, 128, 256, 64
GRANK, GTAU = 16, 16.0
DH_, DDH, DDV = 8, 64, 128
ROPE_DIM, ROPE_THETA = 16, 500000.0
RH_, RDK, RDV = 4, 256, 512
SH_, SDH = 16, 64
F_FFN = 2816
FT = F_FFN // P
CONV = 3
NSLOT = 4
CHUNK = 2048
LAMBDA_INIT = 0.8 - 0.6 * math.exp(-0.3)
NEG = -2.0 ** 100
ROUND = 1.5 * 2.0 ** 23
TURN = (6.28125, 0.0019350051879882812, 3.0199159819e-07)
PI32 = 3.1415925

UNITS = F_MLP // 256
MLP_UNROLL, MLP_BODIES = 4, 3
GROUPS = FT // 2
C_GV, C_GQ, C_GK, C_GR, C_GO = 0, 4, 6, 8, 12
C_M0 = 16
C_DQ = C_M0 + 2 * UNITS
C_DK, C_DV, C_DO = C_DQ + 4, C_DQ + 8, C_DQ + 12
C_M1 = C_DQ + 16
C_RQ = C_M1 + 2 * UNITS
C_RK, C_RV, C_RG, C_RO = C_RQ + 4, C_RQ + 8, C_RQ + 16, C_RQ + 24
C_F0 = C_RQ + 32
C_SQ = C_F0 + 3 * GROUPS
C_SK, C_SV, C_SO = C_SQ + 4, C_SQ + 8, C_SQ + 12
C_F1 = C_SQ + 16
NCHUNK = C_F1 + 3 * GROUPS

SH_T, SC_T, GA_T, SH_C, SC_C, GA_C = range(6)
ADA_PARTS = 6 * DEPTH
ADA_STEPS = ADA_PARTS * KT
ADA_RING = 4

COL_C = 0
COL_ADAB = COL_C + KT
COL_NORM = COL_ADAB + ADA_PARTS * KT
COL_RET = COL_NORM + 4 * KT
COL_FFN = COL_RET + KT
COL_SB = COL_FFN + 2 * KT
COL_BA = COL_SB + KT
COL_CONV = COL_BA + GH_
NCOL = COL_CONV + 2 * 2 * FT * (CONV + 1)

S_ID = 0
S_GLAM = S_ID + P
S_SCAN = S_GLAM + P
S_CAUS = S_SCAN + T
S_SBM = S_CAUS + 2 * P
S_NU = S_SBM + P
S_NO = S_NU + P
S_INVF = S_NO + P
S_ONE = S_INVF + ROPE_DIM // 2
S_HALF = S_ONE + 1
NSHP = S_HALF + 8
NRETC = 2 * T + RH_ * 3 * P


class Count:

    def __init__(self, sem):
        self.sem, self.n = sem, 0

    def inc(self, instruction):
        instruction.then_inc(self.sem, 1)
        self.n = self.n + 1
        return self.n


def build(nc, x_d, pos_d, stream_d, ada_d, cols_d, shp_d, retc_d, wa_d, wa2_d, br_d, gng_d, lam_d, sub_d,
          fg_d, fn_d, out_d):
    f32, f32r, i32 = mybir.dt.float32, mybir.dt.float32r, mybir.dt.int32
    ALU = mybir.AluOpType
    ACT = mybir.ActivationFunctionType
    AX = mybir.AxisListType.X

    ctx = ExitStack()
    with ctx:
        def sb(name, shape, dt=f32):
            return ctx.enter_context(nc.sbuf_tensor(name, shape, dt))

        def sem(name):
            return ctx.enter_context(nc.semaphore(name))

        raw = sb("raw", [P, NSLOT, CHUNK])
        w_hi = sb("w_hi", [P, NSLOT, CHUNK], f32r)
        w_lo = sb("w_lo", [P, NSLOT, CHUNK], f32r)
        x = sb("x", [P, TT, D])
        h_hi = sb("h_hi", [P, KT, T], f32r)
        h_lo = sb("h_lo", [P, KT, T], f32r)
        row = sb("row", [P, D])
        acc = sb("acc", [P, D])
        ada_offset = nc.sbuf_base
        ada = sb("ada", [P, ADA_RING, D])
        cols = sb("cols", [P, NCOL])
        shp = sb("shp", [P, NSHP])
        mod = sb("mod", [P, ADA_PARTS * KT])
        gsc = sb("gsc", [P, 4 * KT])
        csil = sb("csil", [P, KT])
        maskr = sb("maskr", [P, 4 * P], f32r)
        gng = sb("gng", [P, GDV])
        sub = sb("sub", [P, DDV])
        lamc = sb("lamc", [P, 4])
        rope = sb("rope", [P, 2, TT, ROPE_DIM // 2])
        posi = sb("posi", [P, TT], i32)
        ssq = sb("ssq", [P, 16])
        rstd = sb("rstd", [P, 16])
        el = sb("el", [P, GH_ * 4])
        stat = sb("stat", [P, 2, 16])

        arena_offset = nc.sbuf_base
        arena = sb("arena", [P, 12 * 1024])
        A0 = arena_offset

        def at(name, word, shape, dt=f32):
            return nc.alloc_sbuf_tensor_at(name, [P, *shape], dt, offset=A0 + 4 * word)

        xn = at("xn", 0, [TT, D])
        h32 = at("h32", 2048, [KT, T])
        g_eb = at("g_eb", 0, [GH_, T])
        g_en = at("g_en", 1024, [GH_, T])
        g_es = at("g_es", 2048, [GH_, T])
        g_q = at("g_q", 3072, [GH_, TT, 2, P])
        g_ki = at("g_ki", 5120, [GH_, T])
        g_ks = at("g_ks", 6144, [GH_, T])
        g_w2 = at("g_w2", 6144, [GH_ * GDK])
        g_a = at("g_a", 6656, [T])
        g_wa = at("g_wa", 5120, [KT * GRANK])
        g_wah = at("g_wah", 5248, [KT * GRANK], f32r)
        g_wal = at("g_wal", 5376, [KT * GRANK], f32r)
        g_v = at("g_v", 7168, [TT, D])
        g_r = at("g_r", 9216, [TT, D])
        g_z = at("g_z", 9216, [GH_, T])
        g_t = at("g_t", 10240, [GH_, T])
        g_b = at("g_b", 11264, [GH_, T])
        g_kst = at("g_kst", 11264, [GH_, TT, P])
        g_sm = at("g_sm", 0, [GH_, TT, P])
        g_st = at("g_st", 1024, [2, 3, GDV])
        g_o = at("g_o", 5120, [TT, D])
        m_r = at("m_r", 4096, [2, 512])
        m_sq = at("m_sq", 5120, [2, 512])
        hid_hi = at("hid_hi", 7168, [2, 2, T], f32r)
        hid_lo = at("hid_lo", 8192, [2, 2, T], f32r)
        f_cv = at("f_cv", 4096, [2, 2, 2, T])
        f_p = at("f_p", 6144, [2, 2, T])
        diag = at("diag", 9216, [KT, P])
        d_q = at("d_q", 0, [TT, D])
        d_k = at("d_k", 2048, [TT, D])
        d_v = at("d_v", 4096, [TT, D])
        d_qt = at("d_qt", 6144, [KT, T])
        d_kt = at("d_kt", 8192, [KT, T])
        d_rt = at("d_rt", 10240, [4, TT, 16, 8])
        d_p = at("d_p", 0, [3, 2, 3 * P])
        d_a = at("d_a", 2304, [2, 3 * P])
        d_at = at("d_at", 3072, [2, 3 * P])
        d_st = at("d_st", 3840, [3, 3, 4])
        d_sq = at("d_sq", 0, [TT, D])
        d_o = at("d_o", 10240, [TT, D])
        lamv = at("lamv", 10240, [256])
        lamp = at("lamp", 10496, [2, 64])
        ang = at("ang", 10752, [4, TT, 8])
        r_q = at("r_q", 0, [KT, T])
        r_k = at("r_k", 2048, [KT, T])
        r_v = at("r_v", 4096, [TT, RH_ * RDV])
        r_g = at("r_g", 8192, [TT, RH_ * RDV])
        y_hi = at("y_hi", 0, [KT, T], f32r)
        y_lo = at("y_lo", 2048, [KT, T], f32r)
        A1 = ada_offset

        def in_ada(name, word, shape):
            return nc.alloc_sbuf_tensor_at(name, [P, *shape], f32, offset=A1 + 4 * word)

        retc = in_ada("retc", 0, [NRETC])
        r_t = in_ada("r_t", NRETC, [2, 2, T])
        r_sm = in_ada("r_sm", NRETC, [RH_, 3 * P])
        s_q = at("s_q", 0, [KT, T])
        s_k = at("s_k", 2048, [KT, T])
        s_v = at("s_v", 4096, [TT, D])
        s_b = at("s_b", 6144, [3, 2, 2, 3 * P])

        ps = ctx.enter_context(nc.psum_tensor("ps", [P, 8, 512], f32))
        ident = shp[:, S_ID:S_ID + P]

        raw_in = [sem(f"raw_in{i}") for i in range(NSLOT)]
        hi_done = [sem(f"hi_done{i}") for i in range(NSLOT)]
        lo_done = [sem(f"lo_done{i}") for i in range(NSLOT)]
        used = [sem(f"used{i}") for i in range(NSLOT)]
        ada_in = [sem(f"ada_in{i}") for i in range(ADA_RING)]
        ada_more = [sem(f"ada_more{i}") for i in range(ADA_RING)]
        ada_step = sem("ada_step")
        ada_mm = sem("ada_mm")
        mod_done = sem("mod_done")
        cols_in = sem("cols_in")
        shp_in = sem("shp_in")
        x_in = sem("x_in")
        small_in = sem("small_in")
        retc_in = sem("retc_in")
        fg_in = sem("fg_in")
        fn_in = sem("fn_in")
        out_in = sem("out_in")
        csil_done = sem("csil_done")
        ssq_done = sem("ssq_done")
        rstd_done = sem("rstd_done")
        xn0_done = sem("xn0_done")
        xn1_done = sem("xn1_done")
        tr_done = sem("tr_done")
        hh_done = sem("hh_done")
        hl_done = sem("hl_done")
        x_done = sem("x_done")
        y_act = sem("y_act")
        y_dve = sem("y_dve")
        diag_done = sem("diag_done")
        gate_mm = sem("gate_mm")
        gate_done = sem("gate_done")
        act_chain = sem("act_chain")
        dve_chain = sem("dve_chain")
        pool_chain = sem("pool_chain")
        wah_done = sem("wah_done")
        a_mm = sem("a_mm")
        a_done = sem("a_done")
        z_mm = sem("z_mm")
        z_done = sem("z_done")
        abs_done = sem("abs_done")
        ln_done = sem("ln_done")
        rel_done = sem("rel_done")
        eb_done = sem("eb_done")
        qzero = sem("qzero")
        c_dve = sem("c_dve")
        c_act = sem("c_act")
        sc_mm = sem("sc_mm")
        sm_done = sem("sm_done")
        kt_mm = sem("kt_mm")
        kst_done = sem("kst_done")
        kv_mm = sem("kv_mm")
        st_done = sem("st_done")
        go_mm = sem("go_mm")
        gsq_done = sem("gsq_done")
        grs_done = sem("grs_done")
        silu_done = sem("silu_done")
        o_done = sem("o_done")
        relu_done = sem("relu_done")
        sqh_done = sem("sqh_done")
        hid_done = sem("hid_done")
        cg_act = sem("cg_act")
        cv_act = sem("cv_act")
        cg_dve = sem("cg_dve")
        cv_dve = sem("cv_dve")
        fsilu = sem("fsilu")
        rope_q = sem("rope_q")
        rope_k = sem("rope_k")
        dtr = sem("dtr")
        dtr_act = sem("dtr_act")
        ds_mm = sem("ds_mm")
        ds_max = sem("ds_max")
        ds_exp = sem("ds_exp")
        da_done = sem("da_done")
        dat_mm = sem("dat_mm")
        dat_done = sem("dat_done")
        do_mm = sem("do_mm")
        do_act = sem("do_act")
        dsq = sem("dsq")
        dss = sem("dss")
        drs = sem("drs")
        rs_mm = sem("rs_mm")
        rsm_done = sem("rsm_done")
        ro_mm = sem("ro_mm")
        rsq = sem("rsq")
        rrs = sem("rrs")
        ry = sem("ry")
        z_ready = sem("z_ready")
        sln = sem("sln")
        mask_done = sem("mask_done")
        spm = sem("spm")
        e_mm = sem("e_mm")
        sexp = sem("sexp")
        so_mm = sem("so_mm")
        so_hi = sem("so_hi")
        so_lo = sem("so_lo")
        ang_done = sem("ang_done")
        rope_done = sem("rope_done")
        lam_sum = sem("lam_sum")
        lam_exp = sem("lam_exp")
        gsc_done = sem("gsc_done")
        wal_done = sem("wal_done")
        fin_done = sem("fin_done")
        sq_done = sem("sq_done")
        rqk_done = sem("rqk_done")


        block = ctx.enter_context(nc.Block())

        (TR_N0, TR_GO, TR_N1, TR_N2, TR_DO, TR_N3, TR_N4, TR_RA, TR_RB, TR_N5, TR_N6, TR_N7) = range(12)
        (Y_GV, Y_GR, Y_GOUT, Y_M0, Y_DQ, Y_DK, Y_DV, Y_DOUT, Y_M1, Y_RV0, Y_RV1, Y_RG0, Y_RG1, Y_ROUT, Y_F0,
         Y_SV, Y_SOUT, Y_F1) = range(18)
        BY_ACT = [Y_GV, Y_DQ, Y_DK, Y_DV, Y_RV0, Y_RV1, Y_RG0, Y_RG1, Y_SV]
        BY_DVE = [Y_GR, Y_GOUT, Y_M0, Y_DOUT, Y_M1, Y_ROUT, Y_F0, Y_SOUT, Y_F1]
        X_GLA, X_M0, X_DIFF, X_M1, X_FG, X_RET, X_F0, X_SB, X_F1 = 4, 8, 12, 16, 18, 22, 26, 30, 34
        N_C_RET = 4
        Y_LAST = [C_GQ - 1, C_GO - 1, C_M0 - 1, C_DQ - 1, C_DK - 1, C_DV - 1, C_DO - 1, C_M1 - 1, C_RQ - 1,
                  C_RV + 3, C_RG - 1, C_RG + 3, C_RO - 1, C_F0 - 1, C_SQ - 1, C_SO - 1, C_F1 - 1, NCHUNK - 1]

        def y_read(y, bank):
            if y in BY_ACT:
                return y_act, 4 * BY_ACT.index(y) + bank + 1
            return y_dve, 4 * BY_DVE.index(y) + bank + 1

        def slot_visit(c):
            return c if isinstance(c, tuple) else (c % NSLOT, c // NSLOT)

        def multiplied(c):
            s, v = slot_visit(c)
            return used[s], v + 1

        def ffn_chunk(c0, g, part):
            if part == 2:
                return c0 + 3 * GROUPS - 1 if g == GROUPS - 1 else ffn_chunk(c0, g + 1, 1) + 1
            return c0 + (part if g == 0 else 3 * g - 1 + part)

        def d_bank(h):
            return (2, 4, 6)[h % 3]

        def s_bank(p):
            return (2, 4, 6)[p % 3]

        def bcast(ap, n):
            k = ap.shape[1]
            return ap.rearrange("p (o k) -> p o k", o=1).to_broadcast([P, n, k])

        @block.sync
        def _(sp):
            sp.dma_start(cols[:, :], cols_d).then_inc(cols_in, 16)
            sp.dma_start(x[:, :, :], x_d).then_inc(x_in, 16)
            sp.dma_start(shp[:, :], shp_d).then_inc(shp_in, 16)
            for s in range(2 * KT):
                if s >= ADA_RING:
                    sp.wait_ge(ada_step, s - ADA_RING + 1)
                sp.dma_start(ada[:, s % ADA_RING, :], ada_d[s * P:(s + 1) * P, :]).then_inc(ada_in[s % ADA_RING], 16)
            for c in range(NSLOT):
                sp.dma_start(raw[:, c, :], stream_d[c * P:(c + 1) * P, :]).then_inc(raw_in[c], 16)
            with sp.Fori(1, NCHUNK // NSLOT) as i:
                for s in range(NSLOT):
                    sp.wait_ge(lo_done[s], i)
                    sp.dma_start(raw[:, s, :], stream_d[bass.ds((i * NSLOT + s) * P, P), :]).then_inc(raw_in[s], 16)
            for c in range(NCHUNK - NCHUNK % NSLOT, NCHUNK):
                s, v = slot_visit(c)
                sp.wait_ge(lo_done[s], v)
                sp.dma_start(raw[:, s, :], stream_d[c * P:(c + 1) * P, :]).then_inc(raw_in[s], 16)
            for t in range(TT):
                sp.wait_ge(fin_done, 1 + t)
                sp.dma_start(out_d[t * P:(t + 1) * P, :], xn[:, t, :]).then_inc(out_in, 16)
            sp.wait_ge(out_in, 16 * TT)

        @block.gpsimd
        def _(pool):
            pc = Count(pool_chain)
            for dst, src in ((posi[:, :], pos_d), (lamv[:, :], lam_d), (gng[:, :], gng_d), (sub[:, :], sub_d),
                             (g_wa[:, :], wa_d), (g_w2[0:GRANK, :], wa2_d), (row[:, :], br_d)):
                pool.dma_start(dst, src).then_inc(small_in, 16)

            def inverse_rms(out, sums, n, width):
                pc.inc(pool.tensor_scalar(sums, sums, 1.0 / width, EPS, ALU.mult, ALU.add))
                pool.wait_ge(pool_chain, pc.n)
                return pool.tensor_tensor(out, sums, shp[:, S_HALF:S_HALF + n], ALU.pow)

            def norm(k):
                pool.wait_ge(ssq_done, 2 * (k + 1))
                inverse_rms(rstd[:, 0:TT], ssq[:, 0:TT], TT, D).then_inc(rstd_done, 1)

            def ada_load(s):
                pool.wait_ge(ada_step, s - ADA_RING + 1)
                pool.dma_start(ada[:, s % ADA_RING, :], ada_d[s * P:(s + 1) * P, :]).then_inc(ada_more[s % ADA_RING], 16)

            pool.wait_ge(shp_in, 16)
            norm(0)
            for s in range(2 * KT, 2 * KT + ADA_RING):
                ada_load(s)
            pool.wait_ge(hl_done, 4)
            pool.memset(g_q[:, :, :, :, :], 0.0).then_inc(qzero, 1)
            for s in range(2 * KT + ADA_RING, 5 * KT):
                ada_load(s)
            for j in range(GH_ // 2):
                pool.wait_ge(gsq_done, 4 * j + 4)
                inverse_rms(stat[:, 1, 4 * j:4 * j + 4], stat[:, 0, 4 * j:4 * j + 4], 4, GDV).then_inc(grs_done, 1)
            norm(1)
            with pool.Fori(0, MLP_BODIES) as i:
                for k in range(KT):
                    pool.wait_ge(ada_step, i * KT + (5 * KT + k - ADA_RING + 1))
                    pool.dma_start(ada[:, k % ADA_RING, :], ada_d[bass.ds((i * KT + (5 * KT + k)) * P, P), :])\
                        .then_inc(ada_more[k % ADA_RING], 16)
            norm(2)
            for s in range(8 * KT, 11 * KT + ADA_RING):
                ada_load(s)
            pool.wait_ge(dss, 1)
            for j in range(2):
                last = inverse_rms(stat[:, 1, 8 * j:8 * j + 8], stat[:, 0, 8 * j:8 * j + 8], 8, DDV)
            last.then_inc(drs, 1)
            for s in range(11 * KT + ADA_RING, ADA_STEPS):
                ada_load(s)
            norm(3)
            pool.wait_ge(ada_step, ADA_STEPS)
            pool.dma_start(retc[:, :], retc_d).then_inc(retc_in, 16)
            pool.wait_ge(ada_mm, ADA_PARTS)
            pool.dma_start(acc[:, :], fg_d).then_inc(fg_in, 16)
            norm(4)
            norm(5)
            pool.dma_start(acc[:, :], fn_d).then_inc(fn_in, 16)
            for h in range(RH_):
                pool.wait_ge(rsq, 2 * h + 2)
                inverse_rms(stat[:, 1, 2 * h:2 * h + 2], stat[:, 0, 2 * h:2 * h + 2], 2, RDV).then_inc(rrs, 1)
            for k in range(6, 10):
                norm(k)

        @block.scalar
        def _(act):
            ac = Count(act_chain)

            def hi(c):
                if not isinstance(c, tuple) and c >= NCHUNK:
                    return
                s, v = slot_visit(c)
                act.wait_ge(raw_in[s], v * 16 + 16)
                if isinstance(c, tuple) or v:
                    act.wait_ge(used[s], v)
                act.activation(w_hi[:, s, :], raw[:, s, :], ACT.Copy).then_inc(hi_done[s], 1)

            def squares(k, x_count):
                for t in range(TT):
                    if x_count is not None:
                        act.wait_ge(x_done, x_count - (TT - 1 - t) * (1 if x_count == X_FG else 2))
                    act.activation(xn[:, t, :], x[:, t, :], ACT.Square, accum_out=ssq[:, t:t + 1]).then_inc(ssq_done, 1)

            def norm(k, x_count, stage, scale_col, bias_col):
                squares(k, x_count)
                act.wait_ge(rstd_done, k + 1)
                act.activation(xn[:, 1, :], x[:, 1, :], ACT.Copy, scale=rstd[:, 1:2]).then_inc(xn1_done, 1)
                norm_rows(stage, scale_col, bias_col)

            def norm_rows(stage, scale_col, bias_col):
                for b in range(4):
                    act.wait_ge(tr_done, 4 * stage + b + 1)
                    for j in range(2):
                        kt = 2 * b + j
                        last = act.activation(h32[:, kt, :], ps[:, 4 + b, j * T:(j + 1) * T], ACT.Identity,
                                              bias=bias_col(kt) if bias_col else 0.0, scale=scale_col(kt))
                    last.then_inc(hh_done, 1)

            def split_stage(stage, dst):
                for b in range(4):
                    act.wait_ge(tr_done, 4 * stage + b + 1)
                    act.activation(dst[:, 2 * b:2 * b + 2, :].rearrange("p k t -> p (k t)"), ps[:, 4 + b, :],
                                   ACT.Copy).then_inc(hh_done, 1)

            def read_y(y, dst, scale=1.0, func=ACT.Copy):
                act.wait_ge(*multiplied(Y_LAST[y]))
                for b in range(4):
                    act.activation(dst[:, b // 2, (b % 2) * 512:(b % 2 + 1) * 512], ps[:, b, :], func, scale=scale)\
                        .then_inc(y_act, 1)

            def gate_row(g):
                act.wait_ge(gate_mm, g + 1)
                for j in range(2):
                    last = act.activation(row[:, j * 512:(j + 1) * 512], ps[:, 6 + j, :], ACT.Copy, scale=-1.0)
                last.then_inc(gate_done, 1)

            act.wait_ge(cols_in, 16)
            act.activation(csil[:, :], cols[:, COL_C:COL_C + KT], ACT.Silu).then_inc(csil_done, 1)
            act.wait_ge(x_in, 16)
            squares(0, None)
            act.wait_ge(rstd_done, 1)
            act.activation(xn[:, 1, :], x[:, 1, :], ACT.Copy, scale=rstd[:, 1:2]).then_inc(xn1_done, 1)
            act.wait_ge(ang_done, 1)
            act.activation(rope[:, :, :, :].rearrange("p a t k -> p (a t k)"),
                           ang[:, 2:4, :, :].rearrange("p a t k -> p (a t k)"), ACT.Sin).then_inc(rope_done, 1)
            act.activation(maskr[:, 0:P], ident, ACT.Copy)
            act.activation(maskr[:, P:4 * P], shp[:, S_CAUS:S_CAUS + 3 * P], ACT.Copy).then_inc(mask_done, 1)
            act.wait_ge(lam_sum, 1)
            act.activation(lamc[:, 2:4], lamc[:, 0:2], ACT.Exp).then_inc(lam_exp, 1)
            act.activation(g_wah[:, :], g_wa[:, :], ACT.Copy).then_inc(wah_done, 1)
            for c in range(NSLOT):
                hi(c)
            act.wait_ge(gsc_done, 1)
            norm_rows(TR_N0, lambda kt: gsc[:, kt:kt + 1], lambda kt: mod[:, SH_T * KT + kt:SH_T * KT + kt + 1])

            act.wait_ge(abs_done, 1)
            ac.inc(act.activation(g_t[:, :, :], g_t[:, :, :], ACT.Exp, scale=-1.0))
            act.wait_ge(act_chain, ac.n)
            act.activation(g_t[:, :, :], g_t[:, :, :], ACT.Ln, bias=shp[:, S_ONE:S_ONE + 1]).then_inc(ln_done, 1)
            hi(C_GV + 4)
            hi(C_GV + 5)
            act.wait_ge(rel_done, 1)
            act.activation(g_eb[:, :, :], g_b[:, :, :], ACT.Exp, scale=1.0 / GTAU)
            act.activation(g_en[:, :, :], g_b[:, :, :], ACT.Exp, scale=-1.0 / GTAU)
            act.activation(el[:, :], g_b[:, :, :].rearrange("p h (c j) -> p (h c) j", j=GCH)[:, :, GCH - 1],
                           ACT.Exp, scale=1.0 / GTAU)
            act.activation(g_es[:, :, :], g_t[:, :, :], ACT.Exp, scale=1.0 / GTAU).then_inc(eb_done, 1)
            hi(C_GV + 6)
            read_y(Y_GV, g_v)
            for c in range(C_GV + 3, C_GR + 2):
                hi(c + 4)
            for b in range(2):
                act.wait_ge(kt_mm, b + 1)
                act.activation(g_kst[:, 2 * b:2 * b + 2, :, :].rearrange("p h t k -> p (h t k)"), ps[:, 6 + b, :],
                               ACT.Copy).then_inc(kst_done, 1)
            for c in range(C_GR + 2, C_GO):
                hi(c + 4)
            act.wait_ge(*y_read(Y_GR, 3))
            act.activation(g_r[:, :, :], g_r[:, :, :], ACT.Silu).then_inc(silu_done, 1)
            for h in range(GH_):
                act.wait_ge(go_mm, h + 1)
                for t in range(TT):
                    k = 2 * h + t
                    act.activation(h_hi[:, k, :], ps[:, h, t * GDV:(t + 1) * GDV], ACT.Square,
                                   accum_out=stat[:, 0, k:k + 1]).then_inc(gsq_done, 1)
            split_stage(TR_GO, h_hi)
            for c in range(C_GO, C_GO + 3):
                hi(c + 4)
            gate_row(0)
            hi(C_GO + 7)
            act.wait_ge(gsc_done, 2)
            norm(1, X_GLA, TR_N1, lambda kt: gsc[:, KT + kt:KT + kt + 1],
                 lambda kt: mod[:, SH_C * KT + kt:SH_C * KT + kt + 1])

            def mlp(layer, c0):
                B = UNITS * layer

                def unit(u, par, later, c):
                    act.wait_ge(*multiplied(c))
                    if later:
                        act.wait_ge(hid_done, u - 1)
                    act.activation(m_r[:, par, :], ps[:, 4 + par, :], ACT.Relu).then_inc(relu_done, 1)
                    act.wait_ge(relu_done, u + 1)
                    act.activation(hid_hi[:, par, :, :].rearrange("p f t -> p (f t)"), m_r[:, par, :], ACT.Square)\
                        .then_inc(sqh_done, 1)

                unit(B, 0, False, c0)
                hi(c0 + 4)
                unit(B + 1, 1, False, c0 + 1)
                hi(c0 + 5)
                hi(c0 + 6)
                with act.Fori(0, MLP_BODIES) as it:
                    for j in range(MLP_UNROLL):
                        c = c0 + 3 + 2 * j
                        unit(it * MLP_UNROLL + (B + 2 + j), j % 2, True, (c % NSLOT, it * 2 + c // NSLOT))
                        for c in (c + 4, c + 5):
                            hi((c % NSLOT, it * 2 + c // NSLOT))
                c = c0 + 7 + 2 * MLP_UNROLL * MLP_BODIES
                for i in range(2 + MLP_UNROLL * MLP_BODIES, UNITS):
                    unit(B + i, i % 2, True, c - 4)
                    hi(c)
                    hi(c + 1)
                    c += 2
                gate_row(2 * layer + 1)
                hi(c)

            mlp(0, C_M0)
            act.wait_ge(gsc_done, 3)
            norm(2, X_M0, TR_N2, lambda kt: gsc[:, 2 * KT + kt:2 * KT + kt + 1],
                 lambda kt: mod[:, (6 + SH_T) * KT + kt:(6 + SH_T) * KT + kt + 1])

            def d_features(dst, n):
                for b in range(4):
                    act.wait_ge(dtr, n + b + 1)
                    act.activation(dst[:, 2 * b:2 * b + 2, :].rearrange("p k t -> p (k t)"), ps[:, 4 + b, :],
                                   ACT.Copy).then_inc(dtr_act, 1)

            for c in range(C_DQ, C_DQ + 3):
                hi(c + 4)
            read_y(Y_DQ, d_q, DDH ** -0.5)
            for c in range(C_DQ + 3, C_DK + 3):
                hi(c + 4)
            read_y(Y_DK, d_k)
            hi(C_DK + 7)
            d_features(d_qt, 0)
            hi(C_DV + 4)
            hi(C_DV + 5)
            d_features(d_kt, 4)
            hi(C_DV + 6)
            read_y(Y_DV, d_v)
            hi(C_DV + 7)

            def d_exp(h):
                act.wait_ge(ds_max, h + 1)
                r = h % 3
                for i in range(2):
                    for t, first, n in ((1, 0, 2 * P), (0, 2 * P, P)):
                        k = 2 * i + t
                        last = act.activation(d_p[:, r, i, first:first + n], ps[:, d_bank(h) + i, first:first + n],
                                              ACT.Exp, bias=d_st[:, r, 0, k:k + 1], accum_out=d_st[:, r, 1, k:k + 1])
                last.then_inc(ds_exp, 1)

            def d_out(h):
                act.wait_ge(do_mm, h + 1)
                act.activation(d_o[:, :, h * DDV:(h + 1) * DDV],
                               ps[:, 0, (h % 2) * T:(h % 2 + 1) * T].rearrange("p (t k) -> p t k", t=TT), ACT.Copy)\
                    .then_inc(do_act, 1)

            d_exp(0)
            d_exp(1)
            for h in range(DH_):
                if h + 2 < DH_:
                    if h >= 1:
                        act.wait_ge(da_done, h)
                    d_exp(h + 2)
                if h >= 1:
                    d_out(h - 1)
            d_out(DH_ - 1)
            act.wait_ge(do_act, DH_)
            for t in range(TT):
                act.activation(d_sq[:, t, :], d_o[:, t, :], ACT.Square).then_inc(dsq, 1)
            split_stage(TR_DO, h_hi)
            for c in range(C_DO, C_DO + 3):
                hi(c + 4)
            gate_row(2)
            hi(C_DO + 7)
            act.wait_ge(gsc_done, 4)
            norm(3, X_DIFF, TR_N3, lambda kt: gsc[:, 3 * KT + kt:3 * KT + kt + 1],
                 lambda kt: mod[:, (6 + SH_C) * KT + kt:(6 + SH_C) * KT + kt + 1])
            mlp(1, C_M1)
            squares(4, X_M1)
            norm(5, X_FG, TR_N4, lambda kt: cols[:, COL_RET + kt:COL_RET + kt + 1], None)

            for c in range(C_RQ, C_RV + 3):
                hi(c + 4)
            read_y(Y_RV0, r_v[:, :, 0:D])
            for c in range(C_RV + 3, C_RV + 7):
                hi(c + 4)
            read_y(Y_RV1, r_v[:, :, D:2 * D])
            for c in range(C_RV + 7, C_RG + 3):
                hi(c + 4)
            read_y(Y_RG0, r_g[:, :, 0:D], 1.0, ACT.Silu)
            for c in range(C_RG + 3, C_RG + 7):
                hi(c + 4)
            read_y(Y_RG1, r_g[:, :, D:2 * D], 1.0, ACT.Silu)
            hi(C_RG + 11)
            for k in range(TT * RH_):
                act.wait_ge(ro_mm, k + 1)
                junk = (h_hi if k < 4 else h_lo)[:, 2 * (k % 4):2 * (k % 4) + 2, :].rearrange("p k t -> p (k t)")
                act.activation(junk, ps[:, k % 4, :], ACT.Square, accum_out=stat[:, 0, k:k + 1]).then_inc(rsq, 1)
            split_stage(TR_RA, h_hi)
            split_stage(TR_RB, y_hi)
            for c in range(C_RO, C_RO + 8):
                hi(c + 4)
            norm(6, X_RET, TR_N5, lambda kt: cols[:, COL_FFN + kt:COL_FFN + kt + 1], None)

            def ffn(layer, c0):
                def last_tap(g, value):
                    G = GROUPS * layer + g
                    act.wait_ge(*multiplied(ffn_chunk(c0, g, value)))
                    if g >= 2:
                        act.wait_ge(hid_done, 2 * UNITS + G - 1)
                    for f in range(2):
                        k = COL_CONV + ((layer * 2 + value) * FT + 2 * g + f) * (CONV + 1)
                        last = act.activation(f_cv[:, g % 2, value, f, :],
                                              ps[:, 4 + 2 * (g % 2) + value, f * T:(f + 1) * T],
                                              ACT.Identity, bias=cols[:, k + 3:k + 4], scale=cols[:, k + 2:k + 3])
                    last.then_inc(cv_act if value else cg_act, 1)

                c = c0 + 4
                for g in range(GROUPS):
                    last_tap(g, 0)
                    hi(c)
                    act.wait_ge(cg_dve, GROUPS * layer + g + 1)
                    act.activation(f_cv[:, g % 2, 0, :, :], f_cv[:, g % 2, 0, :, :], ACT.Silu).then_inc(fsilu, 1)
                    last_tap(g, 1)
                    hi(c + 1)
                    c += 2
                    if g:
                        hi(c)
                        c += 1
                hi(c)

            ffn(0, C_F0)
            norm(7, X_F0, TR_N6, lambda kt: cols[:, COL_SB + kt:COL_SB + kt + 1], None)

            for n in range(2 * KT // 2):
                act.wait_ge(*multiplied(C_SQ + n))
                dst, m = (s_q, n) if n < 4 else (s_k, n - 4)
                act.activation(dst[:, 2 * m:2 * m + 2, :].rearrange("p k t -> p (k t)"), ps[:, 4 + n % 4, :], ACT.Copy,
                               scale=SDH ** -0.5 if n < 4 else 1.0).then_inc(c_act, 1)
                hi(C_SQ + n + 4)
            for c in range(C_SV, C_SV + 3):
                hi(c + 4)
            read_y(Y_SV, s_v)
            hi(C_SV + 7)

            def s_log(p):
                act.wait_ge(z_ready, p + 1)
                ln = s_b[:, p % 3, 0, :, :]
                if p >= 3:
                    act.wait_ge(so_mm, p - 2)
                ac.inc(act.activation(ln, ps[:, s_bank(p):s_bank(p) + 2, 0:3 * P], ACT.Abs))
                act.wait_ge(act_chain, ac.n)
                ac.inc(act.activation(ln, ln, ACT.Exp, scale=-1.0))
                act.wait_ge(act_chain, ac.n)
                act.activation(ln, ln, ACT.Ln, bias=shp[:, S_ONE:S_ONE + 1]).then_inc(sln, 1)

            def s_exp(p):
                act.wait_ge(e_mm, p + 1)
                act.activation(s_b[:, p % 3, 0, :, :], ps[:, s_bank(p):s_bank(p) + 2, 0:3 * P], ACT.Exp)\
                    .then_inc(sexp, 1)

            def s_out(p):
                act.wait_ge(so_mm, p + 1)
                act.activation(h_hi[:, p, :], ps[:, p % 2, 0:T], ACT.Copy).then_inc(so_hi, 1)

            s_log(0)
            s_log(1)
            for p in range(SH_ // 2):
                s_exp(p)
                if p >= 1:
                    s_out(p - 1)
                if p + 2 < SH_ // 2:
                    s_log(p + 2)
            s_out(SH_ // 2 - 1)
            for c in range(C_SO, C_SO + 4):
                hi(c + 4)
            norm(8, X_SB, TR_N7, lambda kt: cols[:, COL_FFN + KT + kt:COL_FFN + KT + kt + 1], None)
            ffn(1, C_F1)
            squares(9, X_F1)

        @block.vector
        def _(dve):
            dc = Count(dve_chain)

            def link(instruction):
                dc.inc(instruction)
                dve.wait_ge(dve_chain, dc.n)

            def lo(c):
                if not isinstance(c, tuple) and c >= NCHUNK:
                    return
                s, v = slot_visit(c)
                dve.wait_ge(hi_done[s], v + 1)
                dve.tensor_tensor(w_lo[:, s, :], raw[:, s, :], w_hi[:, s, :].bitcast(f32), ALU.subtract)\
                    .then_inc(lo_done[s], 1)

            def add_step(s, k, ring_fill, early=False):
                dve.wait_ge((ada_in if early else ada_more)[k % ADA_RING], ring_fill)
                rows, ck = ada[:, k % ADA_RING, :], csil[:, k:k + 1]
                if k == 0:
                    dve.tensor_scalar(acc[:, :], rows, ck, None, ALU.mult).then_inc(ada_step, 1)
                else:
                    dve.wait_ge(ada_step, s)
                    dve.scalar_tensor_tensor(acc[:, :], rows, ck, acc[:, :], ALU.mult, ALU.add).then_inc(ada_step, 1)

            def steps(first, n):
                for s in range(first, first + n):
                    if s % KT == 0 and s:
                        dve.wait_ge(ada_mm, s // KT)
                    if s < 2 * KT:
                        add_step(s, s % KT, 16 * (s // ADA_RING + 1), True)
                    else:
                        add_step(s, s % KT, 16 * ((s - 2 * KT) // ADA_RING + 1))

            def finish_part(p, bank):
                dve.wait_ge(ada_mm, p + 1)
                dve.tensor_tensor(mod[:, p * KT:(p + 1) * KT], ps[:, bank, 0:KT],
                                  cols[:, COL_ADAB + p * KT:COL_ADAB + (p + 1) * KT], ALU.add).then_inc(mod_done, 1)

            def norm_scale(n, p):
                dve.wait_ge(mod_done, p + 1)
                dve.scalar_tensor_tensor(gsc[:, n * KT:(n + 1) * KT], mod[:, p * KT:(p + 1) * KT], 1.0,
                                         cols[:, COL_NORM + n * KT:COL_NORM + (n + 1) * KT], ALU.add, ALU.mult)\
                    .then_inc(gsc_done, 1)
                dve.wait_ge(gsc_done, n + 1)

            def norm_xn(k):
                dve.wait_ge(rstd_done, k + 1)
                dve.tensor_scalar(xn[:, 0, :], x[:, 0, :], rstd[:, 0:1], None, ALU.mult).then_inc(xn0_done, 1)

            def norm_split(stage):
                for b in range(4):
                    pair = slice(2 * b, 2 * b + 2)
                    dve.wait_ge(hh_done, 4 * stage + b + 1)
                    link(dve.tensor_copy(h_hi[:, pair, :], h32[:, pair, :]))
                    dve.tensor_tensor(h_lo[:, pair, :], h32[:, pair, :], h_hi[:, pair, :].bitcast(f32), ALU.subtract)\
                        .then_inc(hl_done, 1)

            def split_stage(stage, dst, src_hi):
                for b in range(4):
                    dve.wait_ge(hh_done, 4 * stage + b + 1)
                    dve.tensor_tensor(dst[:, 2 * b:2 * b + 2, :].rearrange("p k t -> p (k t)"), ps[:, 4 + b, :],
                                      src_hi[:, 2 * b:2 * b + 2, :].rearrange("p k t -> p (k t)").bitcast(f32),
                                      ALU.subtract).then_inc(hl_done, 1)

            def make_diag(p):
                dve.wait_ge(mod_done, p + 1)
                for kt in range(KT):
                    last = dve.tensor_scalar(diag[:, kt, :], ident, mod[:, p * KT + kt:p * KT + kt + 1], None, ALU.mult)
                last.then_inc(diag_done, 1)

            def add_gated(y, g):
                dve.wait_ge(*multiplied(Y_LAST[y]))
                dve.wait_ge(gate_done, g + 1)
                for b in range(4):
                    half = slice((b % 2) * 512, (b % 2 + 1) * 512)
                    dve.tensor_tensor(xn[:, b // 2, half], ps[:, b, :], row[:, half], ALU.mult).then_inc(y_dve, 1)
                    dve.wait_ge(*y_read(y, b))
                    dve.tensor_tensor(x[:, b // 2, half], x[:, b // 2, half], xn[:, b // 2, half], ALU.add)\
                        .then_inc(x_done, 1)

            dve.wait_ge(small_in, 16 * 7)
            dve.wait_ge(shp_in, 16)
            pf = stat[:, 0, 0:TT]
            link(dve.tensor_copy(pf, posi[:, :]))
            for t in range(TT):
                last = dve.tensor_scalar(ang[:, 0, t, :], shp[:, S_INVF:S_INVF + 8], stat[:, 0, t:t + 1], None, ALU.mult)
            link(last)
            for n, quarter in ((2, 0.25), (3, 0.0)):
                link(dve.tensor_scalar(ang[:, 1, :, :], ang[:, 0, :, :], 1.0 / (2 * math.pi), quarter, ALU.mult, ALU.add))
                link(dve.tensor_scalar(ang[:, 1, :, :], ang[:, 1, :, :], ROUND, -ROUND, ALU.add, ALU.add))
                link(dve.scalar_tensor_tensor(ang[:, n, :, :], ang[:, 1, :, :], -TURN[0], ang[:, 0, :, :], ALU.mult, ALU.add))
                link(dve.scalar_tensor_tensor(ang[:, n, :, :], ang[:, 1, :, :], -TURN[1], ang[:, n, :, :], ALU.mult, ALU.add))
                link(dve.scalar_tensor_tensor(ang[:, n, :, :], ang[:, 1, :, :], -TURN[2], ang[:, n, :, :], ALU.mult, ALU.add))
                if quarter:
                    link(dve.tensor_scalar(ang[:, n, :, :], ang[:, n, :, :], math.pi / 2, None, ALU.add))
            dve.tensor_scalar(ang[:, 2:4, :, :].rearrange("p a t k -> p (a t k)"),
                              ang[:, 2:4, :, :].rearrange("p a t k -> p (a t k)"), PI32, -PI32, ALU.min, ALU.max)\
                .then_inc(ang_done, 1)
            lv = lamv[:, :].rearrange("p (a b k) -> p a b k", a=2, b=2)
            link(dve.tensor_tensor(lamp[:, :, :], lv[:, :, 0, :], lv[:, :, 1, :], ALU.mult))
            dve.tensor_reduce(lamc[:, 0:2], lamp[:, :, :], AX, ALU.add).then_inc(lam_sum, 1)
            dve.tensor_scalar(sub[:, :], sub[:, :], 1.0 - LAMBDA_INIT, None, ALU.mult)
            dve.wait_ge(lam_exp, 1)
            link(dve.tensor_tensor(lamc[:, 0:1], lamc[:, 3:4], lamc[:, 2:3], ALU.subtract))
            link(dve.tensor_scalar(lamc[:, 0:1], lamc[:, 0:1], -LAMBDA_INIT, None, ALU.add))
            dve.wait_ge(wah_done, 1)
            dve.tensor_tensor(g_wal[:, :], g_wa[:, :], g_wah[:, :].bitcast(f32), ALU.subtract).then_inc(wal_done, 1)

            norm_xn(0)
            dve.wait_ge(csil_done, 1)
            steps(0, KT)
            finish_part(0, 0)
            steps(KT, KT)
            finish_part(1, 0)
            norm_scale(0, SC_T)
            norm_split(TR_N0)
            for c in range(NSLOT):
                lo(c)

            dve.wait_ge(a_mm, 1)
            dve.tensor_copy(g_a[0:GRANK, :], ps[0:GRANK, 4, 0:T]).then_inc(a_done, 1)
            dve.wait_ge(z_mm, 1)
            for h in range(GH_):
                last = dve.tensor_scalar(g_z[:, h, :], ps[:, 6 + h // 2, (h % 2) * T:(h % 2 + 1) * T],
                                         cols[:, COL_BA + h:COL_BA + h + 1], None, ALU.add)
            last.then_inc(z_done, 1)
            dve.wait_ge(z_done, 1)
            dve.scalar_tensor_tensor(g_t[:, :, :], g_z[:, :, :], -1.0, g_z[:, :, :], ALU.mult, ALU.max)\
                .then_inc(abs_done, 1)
            dve.wait_ge(abs_done, 1)
            lo(4)
            link(dve.tensor_scalar(g_z[:, :, :], g_z[:, :, :], 0.0, None, ALU.min))
            dve.wait_ge(ln_done, 1)
            link(dve.scalar_tensor_tensor(g_t[:, :, :], g_t[:, :, :], -1.0, g_z[:, :, :], ALU.mult, ALU.add))
            for h in range(GH_):
                last = dve.tensor_tensor_scan(g_b[:, h, :], shp[:, S_SCAN:S_SCAN + T], g_t[:, h, :], 0.0,
                                              ALU.mult, ALU.add)
            link(last)
            bv = g_b[:, :, :].rearrange("p h (c j) -> p (h c) j", j=GCH)
            dve.tensor_tensor(g_t[:, :, :].rearrange("p h (c j) -> p (h c) j", j=GCH),
                              bv[:, :, GCH - 1:GCH].to_broadcast([P, GH_ * 4, GCH]), bv, ALU.subtract)\
                .then_inc(rel_done, 1)
            lo(5)
            steps(2 * KT, 4)
            lo(6)
            lo(7)
            steps(2 * KT + 4, 4)
            dve.wait_ge(eb_done, 1)
            dve.wait_ge(qzero, 1)
            for n in range(2):
                dve.wait_ge(*multiplied(C_GQ + n))
                for f in range(2):
                    h = 2 * n + f
                    src = ps[:, 4 + n, f * T:(f + 1) * T].rearrange("p (t c j) -> p t c j", t=TT, c=2)
                    dec = g_eb[:, h, :].rearrange("p (t c j) -> p t c j", t=TT, c=2)
                    for c in range(2):
                        last = dve.scalar_tensor_tensor(g_q[:, h, :, c, c * GCH:(c + 1) * GCH], src[:, :, c, :],
                                                        GDK ** -0.5, dec[:, :, c, :], ALU.mult, ALU.mult)
                last.then_inc(c_dve, 1)
                lo(C_GQ + n + 4)
                steps(3 * KT + 2 * n, 2)
                if n == 0:
                    finish_part(2, 6)
            for n in range(2):
                dve.wait_ge(*multiplied(C_GK + n))
                flat = lambda a: a[:, 2 * n:2 * n + 2, :].rearrange("p h t -> p (h t)")
                dve.tensor_tensor(flat(g_ki), ps[:, 4 + n, :], flat(g_en), ALU.mult)
                dve.tensor_tensor(flat(g_ks), ps[:, 4 + n, :], flat(g_es), ALU.mult).then_inc(c_dve, 1)
                lo(C_GK + n + 4)
                steps(3 * KT + 4 + 2 * n, 2)
            lo(C_GR + 4)
            finish_part(3, 6)
            steps(4 * KT, 2)
            lo(C_GR + 5)
            for b in range(2):
                dve.wait_ge(sc_mm, b + 1)
                dve.tensor_tensor(g_sm[:, 2 * b:2 * b + 2, :, :].rearrange("p h t k -> p (h t) k"),
                                  ps[:, 4 + b, :].rearrange("p (a k) -> p a k", a=4),
                                  bcast(shp[:, S_GLAM:S_GLAM + P], 4), ALU.mult).then_inc(sm_done, 1)
            steps(4 * KT + 2, 3)
            lo(C_GR + 6)
            steps(4 * KT + 5, 3)
            lo(C_GR + 7)
            dve.wait_ge(*multiplied(Y_LAST[Y_GR]))
            for b in range(4):
                half = slice((b % 2) * 512, (b % 2 + 1) * 512)
                last = dve.tensor_tensor(g_r[:, b // 2, half], ps[:, b, :], row[:, half], ALU.add)
                last.then_inc(y_dve, 1)

            def state(h):
                dve.wait_ge(kv_mm, h + 1)
                if h >= 2:
                    dve.wait_ge(go_mm, h - 1)
                kv = (ps[:, 4 + 2 * (h % 2), 0:GDV], ps[:, 5 + 2 * (h % 2), 0:GDV], ps[:, 4 + 2 * (h % 2), GDV:2 * GDV])
                st = g_st[:, h % 2, :, :]
                link(dve.tensor_copy(st[:, 0, :], kv[0]))
                link(dve.scalar_tensor_tensor(st[:, 1, :], st[:, 0, :], el[:, 4 * h + 1:4 * h + 2], kv[1],
                                              ALU.mult, ALU.add))
                dve.scalar_tensor_tensor(st[:, 2, :], st[:, 1, :], el[:, 4 * h + 2:4 * h + 3], kv[2],
                                         ALU.mult, ALU.add).then_inc(st_done, 1)

            for h in range(GH_):
                state(h)
            for h in range(GH_):
                dve.wait_ge(grs_done, h // 2 + 1)
                for t in range(TT):
                    last = dve.scalar_tensor_tensor(g_o[:, t, h * GDV:(h + 1) * GDV], ps[:, h, t * GDV:(t + 1) * GDV],
                                                    stat[:, 1, 2 * h + t:2 * h + t + 1], gng[:, :], ALU.mult, ALU.mult)
            link(last)
            dve.wait_ge(silu_done, 1)
            for t in range(TT):
                dve.tensor_tensor(g_o[:, t, :], g_o[:, t, :], g_r[:, t, :], ALU.mult).then_inc(o_done, 1)
            dve.wait_ge(o_done, 2)
            make_diag(GA_T)
            split_stage(TR_GO, h_lo, h_hi)
            lo(C_GO + 4)
            finish_part(4, 4)
            norm_scale(1, SC_C)
            for c in range(C_GO + 1, C_GO + 4):
                lo(c + 4)
            add_gated(Y_GOUT, 0)
            norm_xn(1)
            norm_split(TR_N1)

            def mlp(layer, c0, with_ada):
                B = UNITS * layer

                def unit(u, par):
                    dve.wait_ge(relu_done, u + 1)
                    dve.tensor_tensor(m_sq[:, par, :], m_r[:, par, :], m_r[:, par, :], ALU.mult).then_inc(sq_done, 1)
                    dve.wait_ge(sq_done, u + 1)
                    dve.wait_ge(sqh_done, u + 1)
                    dve.tensor_tensor(hid_lo[:, par, :, :].rearrange("p f t -> p (f t)"), m_sq[:, par, :],
                                      hid_hi[:, par, :, :].rearrange("p f t -> p (f t)").bitcast(f32), ALU.subtract)\
                        .then_inc(hid_done, 1)

                unit(B, 0)
                lo(c0 + 4)
                unit(B + 1, 1)
                lo(c0 + 5)
                if layer == 1:
                    finish_part(11, 6)
                lo(c0 + 6)
                with dve.Fori(0, MLP_BODIES) as it:
                    for j in range(MLP_UNROLL):
                        unit(it * MLP_UNROLL + (B + 2 + j), j % 2)
                        for q in range(2):
                            c = c0 + 7 + 2 * j + q
                            lo((c % NSLOT, it * 2 + c // NSLOT))
                            if with_ada and j < 2:
                                for k in (4 * j + 2 * q, 4 * j + 2 * q + 1):
                                    if k == 0:
                                        dve.wait_ge(ada_mm, it + 5)
                                    add_step(it * KT + (5 * KT + k), k,
                                             it * 32 + 16 * ((3 * KT + k) // ADA_RING + 1))
                    if with_ada:
                        dve.wait_ge(ada_mm, it + 6)
                        dve.tensor_tensor(mod[:, bass.ds(it * KT + 5 * KT, KT)], ps[:, 6, 0:KT],
                                          cols[:, bass.ds(it * KT + (COL_ADAB + 5 * KT), KT)], ALU.add)\
                            .then_inc(mod_done, 1)
                c = c0 + 7 + 2 * MLP_UNROLL * MLP_BODIES
                make_diag(6 * layer + GA_C)
                for i in range(2 + MLP_UNROLL * MLP_BODIES, UNITS):
                    unit(B + i, i % 2)
                    lo(c)
                    lo(c + 1)
                    c += 2
                lo(c)

            mlp(0, C_M0, True)
            norm_scale(2, 6 + SC_T)
            add_gated(Y_M0, 1)
            norm_xn(2)
            norm_split(TR_N2)

            def rotate(q, done):
                v = q[:, :, :].rearrange("p t (g k) -> p t g k", k=DDH)
                x1, x2 = v[:, :, :, 0:8], v[:, :, :, 8:16]

                def each(op, out, a, b):
                    for t in range(TT):
                        last = dve.tensor_tensor(out(t), a(t), b(t), op)
                    return last

                cos = lambda t: bcast(rope[:, 0, t, :], 16)
                sin = lambda t: bcast(rope[:, 1, t, :], 16)
                r = [lambda t, n=n: d_rt[:, n, t, :, :] for n in range(4)]
                a1, a2 = (lambda t: x1[:, t]), (lambda t: x2[:, t])
                each(ALU.mult, r[0], a1, cos)
                each(ALU.mult, r[1], a2, sin)
                each(ALU.mult, r[2], a2, cos)
                link(each(ALU.mult, r[3], a1, sin))
                each(ALU.subtract, a1, r[0], r[1])
                each(ALU.add, a2, r[2], r[3]).then_inc(done, 1)
                dve.wait_ge(done, 1)

            for e in range(3):
                lo(C_DQ + e + 4)
                steps(8 * KT + 2 * e, 2)
            lo(C_DQ + 7)
            steps(8 * KT + 6, 2)
            dve.wait_ge(rope_done, 1)
            dve.wait_ge(*(y_read(Y_DQ, 3)))
            rotate(d_q, rope_q)
            for e in range(4):
                lo(C_DK + e + 4)
                if e == 0:
                    finish_part(8, 4)
                steps(9 * KT + 2 * e, 2)
            dve.wait_ge(*(y_read(Y_DK, 3)))
            rotate(d_k, rope_k)
            for e in range(4):
                lo(C_DV + e + 4)
                if e == 0:
                    finish_part(9, 4)
                steps(10 * KT + 2 * e, 2)

            def d_maxima(h):
                dve.wait_ge(ds_mm, h + 1)
                b, r = d_bank(h), h % 3
                m = d_st[:, r, 0, :].rearrange("p (i t) -> p i t", i=2)
                dve.tensor_reduce(m[:, :, 1], ps[:, b:b + 2, 0:2 * P], AX, ALU.max, negate=True)
                dve.tensor_reduce(m[:, :, 0], ps[:, b:b + 2, 2 * P:3 * P], AX, ALU.max, negate=True).then_inc(ds_max, 1)

            def d_combine(h):
                r, par = h % 3, h % 2
                dve.wait_ge(ds_exp, h + 1)
                link(dve.reciprocal(d_st[:, r, 2, :], d_st[:, r, 1, :]))
                link(dve.tensor_scalar(d_st[:, r, 2, 2:4], d_st[:, r, 2, 2:4], lamc[:, 0:1], None, ALU.mult))
                if h >= 2:
                    dve.wait_ge(dat_mm, h - 1)
                parts = ((1, 0, 2 * P), (0, 2 * P, P))
                for t, a, n in parts:
                    last = dve.tensor_scalar(d_a[:, par, a:a + n], d_p[:, r, 0, a:a + n],
                                             d_st[:, r, 2, t:t + 1], None, ALU.mult)
                link(last)
                for t, a, n in parts:
                    last = dve.scalar_tensor_tensor(d_a[:, par, a:a + n], d_p[:, r, 1, a:a + n],
                                                    d_st[:, r, 2, 2 + t:3 + t], d_a[:, par, a:a + n],
                                                    ALU.mult, ALU.add)
                last.then_inc(da_done, 1)

            def d_transposed(h):
                dve.wait_ge(dat_mm, h + 1)
                if h >= 2:
                    dve.wait_ge(do_mm, h - 1)
                dve.tensor_copy(d_at[:, h % 2, :], ps[:, 1, 0:3 * P]).then_inc(dat_done, 1)

            d_maxima(0)
            d_maxima(1)
            for h in range(DH_):
                if h + 2 < DH_:
                    d_maxima(h + 2)
                d_combine(h)
                if h >= 1:
                    d_transposed(h - 1)
            d_transposed(DH_ - 1)
            for t in range(TT):
                dve.wait_ge(dsq, t + 1)
                last = dve.tensor_reduce(stat[:, 0, 8 * t:8 * t + 8],
                                         d_sq[:, t, :].rearrange("p (h k) -> p h k", h=DH_), AX, ALU.add)
            last.then_inc(dss, 1)
            dve.wait_ge(drs, 1)
            for t in range(TT):
                for h in range(DH_):
                    last = dve.scalar_tensor_tensor(d_o[:, t, h * DDV:(h + 1) * DDV],
                                                    d_o[:, t, h * DDV:(h + 1) * DDV],
                                                    stat[:, 1, 8 * t + h:8 * t + h + 1], sub[:, :], ALU.mult, ALU.mult)
                last.then_inc(o_done, 1)
            make_diag(6 + GA_T)
            split_stage(TR_DO, h_lo, h_hi)
            lo(C_DO + 4)
            finish_part(10, 4)
            norm_scale(3, 6 + SC_C)
            steps(11 * KT, 3)
            for e in range(1, 4):
                lo(C_DO + e + 4)
                if e < 3:
                    steps(11 * KT + 3 * e, 3 if e == 1 else 2)
            add_gated(Y_DOUT, 2)
            norm_xn(3)
            norm_split(TR_N3)
            mlp(1, C_M1, False)
            add_gated(Y_M1, 3)
            dve.wait_ge(rstd_done, 5)
            dve.wait_ge(fg_in, 16)
            for t in range(TT):
                dve.scalar_tensor_tensor(x[:, t, :], x[:, t, :], rstd[:, t:t + 1], acc[:, :], ALU.mult, ALU.mult)\
                    .then_inc(x_done, 1)
            norm_xn(5)
            norm_split(TR_N4)

            dve.wait_ge(retc_in, 16)
            for n in range(2 * RH_):
                dst, h = (r_q, n) if n < RH_ else (r_k, n - RH_)
                dve.wait_ge(*multiplied(C_RQ + n))
                src = ps[:, 4 + n % 4, :].rearrange("p (a t) -> p a t", a=2)
                dve.tensor_tensor(r_t[:, 0, :, :], src, bcast(retc[:, 0:T], 2), ALU.mult)
                dve.tensor_tensor(r_t[:, 1, :, :], src, bcast(retc[:, T:2 * T], 2), ALU.mult).then_inc(c_dve, 1)
                dve.wait_ge(c_dve, N_C_RET + n + 1)
                dve.tensor_tensor(dst[:, 2 * h, :], r_t[:, 0, 0, :], r_t[:, 1, 1, :], ALU.subtract)
                dve.tensor_tensor(dst[:, 2 * h + 1, :], r_t[:, 1, 0, :], r_t[:, 0, 1, :], ALU.add)\
                    .then_inc(rqk_done, 1)
                dve.wait_ge(rqk_done, n + 1)
                lo(C_RQ + n + 4)
            for c in range(C_RV, C_RV + 8):
                lo(c + 4)
            for h in range(RH_):
                dve.wait_ge(rs_mm, h + 1)
                dve.tensor_tensor(r_sm[:, h, :], ps[:, 4 + h, 0:3 * P],
                                  retc[:, 2 * T + h * 3 * P:2 * T + (h + 1) * 3 * P], ALU.mult).then_inc(rsm_done, 1)
            for c in range(C_RG, C_RG + 8):
                lo(c + 4)
            for h in range(RH_):
                dve.wait_ge(rrs, h + 1)
                for t in range(TT):
                    k = 2 * h + t
                    g = r_g[:, t, h * RDV:(h + 1) * RDV]
                    dve.scalar_tensor_tensor(g, ps[:, k % 4, :], stat[:, 1, k:k + 1], g, ALU.mult, ALU.mult)\
                        .then_inc(ry, 1)
            split_stage(TR_RA, h_lo, h_hi)
            split_stage(TR_RB, y_lo, y_hi)
            for c in range(C_RO, C_RO + 8):
                lo(c + 4)

            def add_plain(y):
                dve.wait_ge(*multiplied(Y_LAST[y]))
                for b in range(4):
                    half = slice((b % 2) * 512, (b % 2 + 1) * 512)
                    dve.tensor_tensor(x[:, b // 2, half], x[:, b // 2, half], ps[:, b, :], ALU.add).then_inc(x_done, 1)

            add_plain(Y_ROUT)
            norm_xn(6)
            norm_split(TR_N5)

            def ffn(layer, c0):
                def earlier_taps(g, value):
                    G = GROUPS * layer + g
                    dve.wait_ge(cv_act if value else cg_act, G + 1)
                    for back in (1, 2):
                        for f in range(2):
                            k = COL_CONV + ((layer * 2 + value) * FT + 2 * g + f) * (CONV + 1) + CONV - 1 - back
                            v = f_cv[:, g % 2, value, f, back:T]
                            src = ps[:, 4 + 2 * (g % 2) + value, f * T:(f + 1) * T - back]
                            last = dve.scalar_tensor_tensor(v, src, cols[:, k:k + 1], v, ALU.mult, ALU.add)
                        if back == 1:
                            link(last)
                    last.then_inc(cv_dve if value else cg_dve, 1)

                c = c0 + 4
                for g in range(GROUPS):
                    G = GROUPS * layer + g
                    par = g % 2
                    earlier_taps(g, 0)
                    lo(c)
                    earlier_taps(g, 1)
                    dve.wait_ge(cv_dve, G + 1)
                    dve.wait_ge(fsilu, G + 1)
                    link(dve.tensor_tensor(f_p[:, par, :, :], f_cv[:, par, 0, :, :], f_cv[:, par, 1, :, :], ALU.mult))
                    link(dve.tensor_copy(hid_hi[:, par, :, :], f_p[:, par, :, :]))
                    dve.tensor_tensor(hid_lo[:, par, :, :], f_p[:, par, :, :], hid_hi[:, par, :, :].bitcast(f32),
                                      ALU.subtract).then_inc(hid_done, 1)
                    lo(c + 1)
                    c += 2
                    if g:
                        lo(c)
                        c += 1
                lo(c)

            ffn(0, C_F0)
            add_plain(Y_F0)
            norm_xn(7)
            norm_split(TR_N6)

            for c in range(C_SQ, C_SQ + 12):
                lo(c + 4)

            def s_soft(p):
                dve.wait_ge(sln, p + 1)
                if p >= 3:
                    dve.wait_ge(e_mm, p - 2)
                dve.scalar_tensor_tensor(s_b[:, p % 3, 1, :, :], ps[:, s_bank(p):s_bank(p) + 2, 0:3 * P], 0.0,
                                         s_b[:, p % 3, 0, :, :], ALU.max, ALU.add).then_inc(spm, 1)

            def s_lo(p):
                dve.wait_ge(so_hi, p + 1)
                dve.tensor_tensor(h_lo[:, p, :], ps[:, p % 2, 0:T], h_hi[:, p, :].bitcast(f32), ALU.subtract)\
                    .then_inc(so_lo, 1)

            s_soft(0)
            for p in range(SH_ // 2):
                if p + 1 < SH_ // 2:
                    s_soft(p + 1)
                if p >= 1:
                    s_lo(p - 1)
            s_lo(SH_ // 2 - 1)
            for c in range(C_SO, C_SO + 4):
                lo(c + 4)
            add_plain(Y_SOUT)
            norm_xn(8)
            norm_split(TR_N7)
            ffn(1, C_F1)
            add_plain(Y_F1)
            dve.wait_ge(rstd_done, 10)
            dve.wait_ge(fn_in, 16)
            for t in range(TT):
                dve.scalar_tensor_tensor(xn[:, t, :], x[:, t, :], rstd[:, t:t + 1], acc[:, :], ALU.mult, ALU.mult)\
                    .then_inc(fin_done, 1)

        @block.tensor
        def _(pe):
            def chunk_ready(c):
                s, v = slot_visit(c)
                pe.wait_ge(hi_done[s], v + 1)
                pe.wait_ge(lo_done[s], v + 1)
                return s

            def rows(c, lhs_hi, lhs_lo, start, stop, bank_free=None):
                s = chunk_ready(c)
                for k in range(2):
                    for t in range(TT):
                        wh = [w_hi[:, s, k * D + n * 512:k * D + (n + 1) * 512] for n in range(2)]
                        wl = [w_lo[:, s, k * D + n * 512:k * D + (n + 1) * 512] for n in range(2)]
                        for p, (lhs, w) in enumerate(((lhs_hi(k, t), wh), (lhs_hi(k, t), wl), (lhs_lo(k, t), wh))):
                            for n in range(2):
                                first = start and k == 0 and p == 0
                                if first and bank_free:
                                    pe.wait_ge(*bank_free(2 * t + n))
                                last = pe.matmul(ps[:, 2 * t + n, :], lhs, w[n], start=first,
                                                 stop=stop and k == 1 and p == 2)
                last.then_inc(used[s], 1)

            def h_rows(c, i, n, bank_free=None, hb=h_hi, lb=h_lo, start=None, stop=None):
                kt = 2 * (i % 4)
                rows(c, lambda k, t: hb[:, kt + k, t * P:(t + 1) * P], lambda k, t: lb[:, kt + k, t * P:(t + 1) * P],
                     i == 0, i == n - 1, bank_free)

            def cols_chunk(c, bank):
                s = chunk_ready(c)
                for f in range(2):
                    out = ps[:, bank, f * T:(f + 1) * T]
                    for kt in range(KT):
                        first = kt * T + f * P
                        wh, wl = w_hi[:, s, first:first + P], w_lo[:, s, first:first + P]
                        pe.matmul(out, wh, h_hi[:, kt, :], start=kt == 0, stop=False)
                        pe.matmul(out, wh, h_lo[:, kt, :], start=False, stop=False)
                        last = pe.matmul(out, wl, h_hi[:, kt, :], start=False, stop=kt == KT - 1)
                last.then_inc(used[s], 1)

            def transposes(stage, src):
                for b in range(4):
                    if stage == TR_RB:
                        pe.wait_ge(hl_done, 4 * TR_RA + b + 1)
                    for j in range(2):
                        for t in range(TT):
                            kt = 2 * b + j
                            last = pe.transpose(ps[:, 4 + b, j * T + t * P:j * T + (t + 1) * P],
                                                src[:, t, kt * P:(kt + 1) * P], ident)
                    last.then_inc(tr_done, 1)

            def norm(n, stage):
                pe.wait_ge(xn0_done, n + 1)
                pe.wait_ge(xn1_done, n + 1)
                transposes(stage, xn)
                pe.wait_ge(hl_done, 4 * (stage + 1))

            def sum_part(p, bank):
                pe.wait_ge(ada_step, (p + 1) * KT)
                if p:
                    pe.wait_ge(mod_done, p)
                for j in range(KT):
                    last = pe.matmul(ps[:, bank, j:j + 1], acc[:, j * P:(j + 1) * P], shp[:, S_ONE:S_ONE + 1],
                                     start=True, stop=True)
                last.then_inc(ada_mm, 1)

            def gate(g):
                pe.wait_ge(diag_done, g + 1)
                for j in range(2):
                    last = pe.matmul(ps[:, 6 + j, :], shp[:, S_NO:S_NO + P],
                                     diag[:, 4 * j:4 * j + 4, :].rearrange("p k n -> p (k n)"), start=True, stop=True)
                last.then_inc(gate_mm, 1)

            pe.wait_ge(shp_in, 16)
            pe.wait_ge(mask_done, 1)
            sum_part(0, 0)
            sum_part(1, 0)
            norm(0, TR_N0)

            pe.wait_ge(wal_done, 1)
            wa = lambda w, kt: w[:, kt * GRANK:(kt + 1) * GRANK]
            for kt in range(KT):
                out = ps[0:GRANK, 4, 0:T]
                pe.matmul(out, wa(g_wah, kt), h_hi[:, kt, :], start=kt == 0, stop=False)
                pe.matmul(out, wa(g_wah, kt), h_lo[:, kt, :], start=False, stop=False)
                last = pe.matmul(out, wa(g_wal, kt), h_hi[:, kt, :], start=False, stop=kt == KT - 1)
            last.then_inc(a_mm, 1)
            h_rows(C_GV, 0, 4, lambda b: (mod_done, 2))
            pe.wait_ge(a_done, 1)
            for h in range(GH_):
                last = pe.matmul(ps[:, 6 + h // 2, (h % 2) * T:(h % 2 + 1) * T], g_w2[0:GRANK, h * GDK:(h + 1) * GDK],
                                 g_a[0:GRANK, :], start=True, stop=True)
            last.then_inc(z_mm, 1)
            for i in range(1, 4):
                h_rows(C_GV + i, i, 4)
            for n in range(2):
                cols_chunk(C_GQ + n, 4 + n)
                if n == 0:
                    pe.wait_ge(z_done, 1)
                    sum_part(2, 6)
            for n in range(2):
                pe.wait_ge(c_dve, n + 1)
                cols_chunk(C_GK + n, 4 + n)
            h_rows(C_GR, 0, 4, lambda b: y_read(Y_GV, b))
            sum_part(3, 6)
            h_rows(C_GR + 1, 1, 4)
            pe.wait_ge(c_dve, 4)
            pe.wait_ge(mod_done, 4)
            for b in range(2):
                for h in (2 * b, 2 * b + 1):
                    for t in range(TT):
                        for c in range(2):
                            o = ((h % 2) * 2 + t) * P + c * GCH
                            last = pe.matmul(ps[:, 4 + b, o:o + GCH], g_ki[:, h, t * P:(t + 1) * P],
                                             g_q[:, h, t, c, c * GCH:(c + 1) * GCH], start=True, stop=True)
                last.then_inc(sc_mm, 1)
            for b in range(2):
                for h in (2 * b, 2 * b + 1):
                    for t in range(TT):
                        o = ((h % 2) * 2 + t) * P
                        last = pe.transpose(ps[:, 6 + b, o:o + P], g_ks[:, h, t * P:(t + 1) * P], ident)
                last.then_inc(kt_mm, 1)
            h_rows(C_GR + 2, 2, 4)
            h_rows(C_GR + 3, 3, 4)

            def chunk_states(h):
                if h < 2:
                    pe.wait_ge(sm_done, 2)
                    pe.wait_ge(kst_done, 2)
                    pe.wait_ge(*y_read(Y_GV, 3))
                else:
                    pe.wait_ge(st_done, h - 1)
                b = 4 + 2 * (h % 2)
                for c, out in enumerate((ps[:, b, 0:GDV], ps[:, b + 1, 0:GDV], ps[:, b, GDV:2 * GDV])):
                    part = slice((c % 2) * GCH, (c % 2 + 1) * GCH)
                    last = pe.matmul(out, g_kst[part, h, c // 2, :], g_v[part, c // 2, h * GDV:(h + 1) * GDV],
                                     start=True, stop=True)
                last.then_inc(kv_mm, 1)

            def g_output(h):
                pe.wait_ge(st_done, h + 1)
                pe.wait_ge(*y_read(Y_GR, h))
                v = lambda t: g_v[:, t, h * GDV:(h + 1) * GDV]
                o0, o1 = ps[:, h, 0:GDV], ps[:, h, GDV:2 * GDV]
                pe.matmul(o0, g_sm[:, h, 0, :], v(0), start=True, stop=False)
                pe.matmul(o0, g_q[:, h, 0, 1, :], g_st[:, h % 2, 0, :], start=False, stop=True)
                pe.matmul(o1, g_sm[:, h, 1, :], v(1), start=True, stop=False)
                pe.matmul(o1, g_q[:, h, 1, 0, :], g_st[:, h % 2, 1, :], start=False, stop=False)
                pe.matmul(o1, g_q[:, h, 1, 1, :], g_st[:, h % 2, 2, :], start=False, stop=True).then_inc(go_mm, 1)

            chunk_states(0)
            chunk_states(1)
            for h in range(GH_):
                g_output(h)
                if h + 2 < GH_:
                    chunk_states(h + 2)
            pe.wait_ge(o_done, 2)
            transposes(TR_GO, g_o)
            pe.wait_ge(hl_done, 4 * (TR_GO + 1))
            h_rows(C_GO, 0, 4)
            sum_part(4, 4)
            h_rows(C_GO + 1, 1, 4)
            gate(0)
            h_rows(C_GO + 2, 2, 4)
            h_rows(C_GO + 3, 3, 4)
            norm(1, TR_N1)

            def mlp(layer, c0, with_ada):
                B = UNITS * layer

                def up(u, par, c, later):
                    if later:
                        pe.wait_ge(relu_done, u - 1)
                    cols_chunk(c, 4 + par)

                def down(u, par, c, start, stop):
                    pe.wait_ge(hid_done, u + 1)
                    rows(c, lambda k, t: hid_hi[:, par, k, t * P:(t + 1) * P],
                         lambda k, t: hid_lo[:, par, k, t * P:(t + 1) * P], start, stop)

                up(B, 0, c0, False)
                up(B + 1, 1, c0 + 1, False)
                if layer == 1:
                    sum_part(11, 6)
                down(B, 0, c0 + 2, True, False)
                with pe.Fori(0, MLP_BODIES) as it:
                    for j in range(MLP_UNROLL):
                        u = it * MLP_UNROLL + (B + 2 + j)
                        c = c0 + 3 + 2 * j
                        up(u, j % 2, (c % NSLOT, it * 2 + c // NSLOT), True)
                        if with_ada and j == MLP_UNROLL - 1:
                            pe.wait_ge(ada_step, it * KT + 6 * KT)
                            pe.wait_ge(mod_done, it + 5)
                            for k in range(KT):
                                last = pe.matmul(ps[:, 6, k:k + 1], acc[:, k * P:(k + 1) * P],
                                                 shp[:, S_ONE:S_ONE + 1], start=True, stop=True)
                            last.then_inc(ada_mm, 1)
                        down(u + (-1), (j + 1) % 2, ((c + 1) % NSLOT, it * 2 + (c + 1) // NSLOT), False, False)
                c = c0 + 3 + 2 * MLP_UNROLL * MLP_BODIES
                for i in range(2 + MLP_UNROLL * MLP_BODIES, UNITS):
                    up(B + i, i % 2, c, True)
                    if i == UNITS - 1:
                        gate(2 * layer + 1)
                    down(B + i - 1, (i - 1) % 2, c + 1, False, False)
                    c += 2
                down(B + UNITS - 1, (UNITS - 1) % 2, c, False, True)

            mlp(0, C_M0, True)
            norm(2, TR_N2)

            def d_transposes(src, n):
                for b in range(4):
                    if n:
                        pe.wait_ge(dtr_act, b + 1)
                    for j in range(2):
                        for t in range(TT):
                            kt = 2 * b + j
                            last = pe.transpose(ps[:, 4 + b, j * T + t * P:j * T + (t + 1) * P],
                                                src[:, t, kt * P:(kt + 1) * P], ident)
                    last.then_inc(dtr, 1)

            for i in range(4):
                h_rows(C_DQ + i, i, 4)
            for i in range(4):
                h_rows(C_DK + i, i, 4, lambda b: y_read(Y_DQ, b))
                if i == 0:
                    sum_part(8, 4)
            pe.wait_ge(rope_q, 1)
            pe.wait_ge(mod_done, 9)
            d_transposes(d_q, 0)
            h_rows(C_DV, 0, 4, lambda b: y_read(Y_DK, b))
            pe.wait_ge(dtr_act, 1)
            sum_part(9, 4)
            h_rows(C_DV + 1, 1, 4)
            pe.wait_ge(rope_k, 1)
            pe.wait_ge(mod_done, 10)
            d_transposes(d_k, 4)
            h_rows(C_DV + 2, 2, 4)
            h_rows(C_DV + 3, 3, 4)

            def d_scores(h):
                if h >= 3:
                    pe.wait_ge(ds_exp, h - 2)
                for i in range(2):
                    f, b = slice(i * DDH, (i + 1) * DDH), d_bank(h) + i
                    pe.matmul(ps[:, b, 0:T], d_qt[f, h, P:T], d_kt[f, h, :], start=True, stop=True)
                    pe.matmul(ps[:, b, T:T + P], d_qt[f, h, 0:P], d_kt[f, h, 0:P], start=False, stop=True,
                              skip_group_check=True)
                    last = pe.matmul(ps[:, b, P:3 * P], maskr[:, 0:P], maskr[:, P:3 * P], start=False, stop=True,
                                     skip_group_check=True)
                last.then_inc(ds_mm, 1)

            pe.wait_ge(dtr_act, 8)
            pe.wait_ge(*y_read(Y_DV, 3))
            for h in range(3):
                d_scores(h)
            for h in range(DH_):
                par = h % 2
                pe.wait_ge(da_done, h + 1)
                if h:
                    pe.wait_ge(dat_done, h)
                for j in range(3):
                    last = pe.transpose(ps[:, 1, j * P:(j + 1) * P], d_a[:, par, j * P:(j + 1) * P], ident)
                last.then_inc(dat_mm, 1)
                if h + 3 < DH_:
                    d_scores(h + 3)
                pe.wait_ge(dat_done, h + 1)
                if h:
                    pe.wait_ge(do_act, h)
                v = lambda t: d_v[:, t, h * DDV:(h + 1) * DDV]
                o = lambda t: ps[:, 0, par * T + t * P:par * T + (t + 1) * P]
                pe.matmul(o(1), d_at[:, par, 0:P], v(0), start=True, stop=False)
                pe.matmul(o(1), d_at[:, par, P:2 * P], v(1), start=False, stop=True)
                pe.matmul(o(0), d_at[:, par, 2 * P:3 * P], v(0), start=True, stop=True).then_inc(do_mm, 1)
            pe.wait_ge(o_done, 4)
            transposes(TR_DO, d_o)
            pe.wait_ge(hl_done, 4 * (TR_DO + 1))
            h_rows(C_DO, 0, 4)
            sum_part(10, 4)
            h_rows(C_DO + 1, 1, 4)
            gate(2)
            h_rows(C_DO + 2, 2, 4)
            h_rows(C_DO + 3, 3, 4)
            norm(3, TR_N3)
            mlp(1, C_M1, False)
            norm(4, TR_N4)

            for n in range(2 * RH_):
                if n >= 4:
                    pe.wait_ge(c_dve, N_C_RET + n - 3)
                cols_chunk(C_RQ + n, 4 + n % 4)
            for i in range(4):
                h_rows(C_RV + i, i, 4)
            for i in range(4):
                h_rows(C_RV + 4 + i, i, 4, lambda b: y_read(Y_RV0, b))
            pe.wait_ge(rqk_done, 2 * RH_)
            for h in range(RH_):
                for first, keys, queries in ((0, slice(0, P), slice(0, T)), (T, slice(P, T), slice(P, T))):
                    n = queries.stop - queries.start
                    for kk in range(2):
                        last = pe.matmul(ps[:, 4 + h, first:first + n], r_k[:, 2 * h + kk, keys],
                                         r_q[:, 2 * h + kk, queries], start=kk == 0, stop=kk == 1)
                last.then_inc(rs_mm, 1)
            for i in range(4):
                h_rows(C_RG + i, i, 4, lambda b: y_read(Y_RV1, b))
            for i in range(4):
                h_rows(C_RG + 4 + i, i, 4, lambda b: y_read(Y_RG0, b))
            for h in range(RH_):
                pe.wait_ge(rsm_done, h + 1)
                v = lambda t: r_v[:, t, h * RDV:(h + 1) * RDV]
                for t in range(TT):
                    k = 2 * h + t
                    if k < 4:
                        pe.wait_ge(*y_read(Y_RG1, k))
                    else:
                        pe.wait_ge(ry, k - 3)
                    pe.matmul(ps[:, k % 4, :], r_sm[:, h, t * P:(t + 1) * P], v(0), start=True, stop=t == 0)\
                        if t else pe.matmul(ps[:, k % 4, :], r_sm[:, h, 0:P], v(0), start=True, stop=True)\
                        .then_inc(ro_mm, 1)
                    if t:
                        pe.matmul(ps[:, k % 4, :], r_sm[:, h, 2 * P:3 * P], v(1), start=False, stop=True)\
                            .then_inc(ro_mm, 1)
            pe.wait_ge(ry, 4)
            transposes(TR_RA, r_g[:, :, 0:D])
            pe.wait_ge(ry, 8)
            transposes(TR_RB, r_g[:, :, D:2 * D])
            pe.wait_ge(hl_done, 4 * (TR_RA + 1))
            for i in range(4):
                h_rows(C_RO + i, i, 8)
            pe.wait_ge(hl_done, 4 * (TR_RB + 1))
            for i in range(4, 8):
                h_rows(C_RO + i, i, 8, None, y_hi, y_lo)
            norm(5, TR_N5)

            def ffn(layer, c0):
                B = GROUPS * layer

                def up(g, value):
                    if g >= 2:
                        pe.wait_ge(cv_dve if value else cg_dve, B + g - 1)
                    cols_chunk(ffn_chunk(c0, g, value), 4 + 2 * (g % 2) + value)

                def down(g):
                    pe.wait_ge(hid_done, 2 * UNITS + B + g + 1)
                    rows(ffn_chunk(c0, g, 2), lambda k, t: hid_hi[:, g % 2, k, t * P:(t + 1) * P],
                         lambda k, t: hid_lo[:, g % 2, k, t * P:(t + 1) * P], g == 0, g == GROUPS - 1)

                for g in range(GROUPS):
                    up(g, 0)
                    up(g, 1)
                    if g:
                        down(g - 1)
                down(GROUPS - 1)

            ffn(0, C_F0)
            norm(6, TR_N6)

            for n in range(8):
                if n >= 4:
                    pe.wait_ge(c_act, n - 3)
                cols_chunk(C_SQ + n, 4 + n % 4)
            for i in range(4):
                h_rows(C_SV + i, i, 4)

            def s_scores(p):
                if p >= 3:
                    pe.wait_ge(sexp, p - 2)
                for i in range(2):
                    f, b = slice(i * SDH, (i + 1) * SDH), s_bank(p) + i
                    pe.matmul(ps[:, b, 0:T], s_k[f, p, 0:P], s_q[f, p, :], start=True, stop=True)
                    pe.matmul(ps[:, b, T:T + P], s_k[f, p, P:T], s_q[f, p, P:T], start=False, stop=True,
                              skip_group_check=True)
                    for first in (0, T):
                        last = pe.matmul(ps[:, b, first:first + P], maskr[:, 0:P], maskr[:, 3 * P:4 * P],
                                         start=False, stop=True, skip_group_check=True)
                last.then_inc(z_ready, 1)

            def s_weights(p):
                pe.wait_ge(spm, p + 1)
                for i in range(2):
                    sums, b = s_b[:, p % 3, 1, i, :], s_bank(p) + i
                    pe.matmul(ps[:, b, 0:3 * P], shp[:, S_NU:S_NU + P], sums, start=False, stop=True,
                              skip_group_check=True)
                    last = pe.matmul(ps[:, b, P:2 * P], shp[:, S_NO:S_NO + P], sums[:, 2 * P:3 * P], start=False,
                                     stop=True, skip_group_check=True)
                last.then_inc(e_mm, 1)

            def s_output(p):
                pe.wait_ge(sexp, p + 1)
                if p >= 2:
                    pe.wait_ge(so_lo, p - 1)
                for i in range(2):
                    f, h = slice(i * SDH, (i + 1) * SDH), 2 * p + i
                    a = s_b[:, p % 3, 0, i, :]
                    pe.matmul(ps[f, p % 2, 0:T], s_v[:, 0, h * SDH:(h + 1) * SDH], a[:, 0:T], start=True, stop=False)
                    last = pe.matmul(ps[f, p % 2, P:T], s_v[:, 1, h * SDH:(h + 1) * SDH], a[:, T:T + P],
                                     start=False, stop=True)
                last.then_inc(so_mm, 1)

            pe.wait_ge(c_act, 8)
            pe.wait_ge(*y_read(Y_SV, 3))
            for p in range(3):
                s_scores(p)
            s_weights(0)
            for p in range(SH_ // 2):
                if p + 1 < SH_ // 2:
                    s_weights(p + 1)
                s_output(p)
                if p + 3 < SH_ // 2:
                    s_scores(p + 3)
            pe.wait_ge(so_lo, SH_ // 2)
            for i in range(4):
                h_rows(C_SO + i, i, 4)
            norm(7, TR_N7)
            ffn(1, C_F1)


def shape_constants():
    shp = np.zeros((P, NSHP), np.float32)
    r, c = np.arange(P)[:, None], np.arange(P)[None, :]
    shp[:, S_ID:S_ID + P] = r == c
    shp[:, S_GLAM:S_GLAM + P] = (r <= c) & (r // GCH == c // GCH)
    shp[:, S_SCAN:S_SCAN + T] = np.arange(T) % GCH != 0
    shp[:, S_CAUS:S_CAUS + 2 * P] = np.tile(np.where(c <= r, 0.0, NEG), 2)
    shp[:, S_SBM:S_SBM + P] = np.where(r < c, 0.0, NEG)
    shp[:, S_NU:S_NU + P] = np.where(r >= c, -1.0, 0.0)
    shp[:, S_NO:S_NO + P] = -1.0
    shp[:, S_INVF:S_INVF + 8] = np.float32(ROPE_THETA) ** (-np.arange(0, ROPE_DIM, 2, dtype=np.float32) / ROPE_DIM)
    shp[:, S_ONE] = 1.0
    shp[:, S_HALF:S_HALF + 8] = -0.5
    retc = np.zeros((P, NRETC), np.float32)
    inv = np.float32(10000.0) ** (-np.arange(0, RDK, 2, dtype=np.float32) / RDK)
    angle = np.arange(T, dtype=np.float32)[None, :] * inv[:, None]
    retc[:, 0:T], retc[:, T:2 * T] = np.cos(angle), np.sin(angle)
    log_g = np.log(1.0 - 2.0 ** (-5.0 - np.arange(RH_)))
    for h in range(RH_):
        d = retc[:, 2 * T + h * 3 * P:2 * T + (h + 1) * 3 * P]
        now = np.where(c >= r, np.exp(np.maximum(c - r, 0) * log_g[h]), 0.0)
        d[:, 0:P] = now
        d[:, P:2 * P] = np.exp((c + P - r) * log_g[h])
        d[:, 2 * P:3 * P] = now
    retc[:, 2 * T:] *= RDK ** -0.5
    return shp, retc


def stream(inputs):
    def cols(w, first, n):
        w = w[:, first:first + n].reshape(KT, P, n // 256, 256)
        return list(w.transpose(2, 1, 0, 3).reshape(n // 256, P, CHUNK))

    def rows(w, first=0, n=D):
        w = w[:, first:first + n]
        k = w.shape[0] // 256
        return list(w.reshape(k, 2, P, n).transpose(0, 2, 1, 3).reshape(k, P, CHUNK))

    out = []
    g = inputs["gla_w_in"][0]
    hk = GH_ * GDK
    out += rows(g, 2 * hk) + cols(g, 0, hk) + cols(g, hk, hk) + rows(g, 2 * hk + D) + rows(inputs["gla_w_o"][0])

    def mlp(layer):
        up, down = cols(inputs["mlp_w1"][layer], 0, F_MLP), rows(inputs["mlp_w2"][layer])
        res = [up[0]]
        for i in range(1, UNITS):
            res += [up[i], down[i - 1]]
        return res + [down[-1]]

    out += mlp(0)
    d = inputs["diff_w_in"][0]
    out += rows(d, 0) + rows(d, D) + rows(d, 2 * D) + rows(inputs["diff_w_o"][0])
    out += mlp(1)
    r = inputs["ret_w_in_2"][0]
    qk = RH_ * RDK
    out += cols(r, 0, qk) + cols(r, qk, qk)
    for n in range(4):
        out += rows(r, 2 * qk + n * D)
    out += rows(inputs["ret_w_out_2"][0])

    def ffn(layer):
        w = inputs["ffn_w_up_2"][layer]
        gate, value, down = cols(w, 0, F_FFN), cols(w, F_FFN, F_FFN), rows(inputs["ffn_w_down_2"][layer])
        res = [gate[0], value[0]]
        for i in range(1, GROUPS):
            res += [gate[i], value[i], down[i - 1]]
        return res + [down[-1]]

    out += ffn(0)
    s = inputs["sb_w_in_2"][0]
    out += cols(s, 0, D) + cols(s, D, D) + rows(s, 2 * D) + rows(inputs["sb_w_out_2"][0])
    out += ffn(1)
    assert len(out) == NCHUNK
    return np.concatenate(out, axis=0)


def kernel(**inputs):
    import concourse.bacc as bacc
    from concourse.bass_utils import run_bass_kernel_spmd as run

    a = {k: np.asarray(v) for k, v in inputs.items()}
    per_feature = lambda v: v.reshape(-1, P).T
    on_all = lambda v: np.broadcast_to(v.reshape(1, -1), (P, v.size))
    conv = np.concatenate([a["ffn_conv_w_2"], a["ffn_conv_b_2"][:, None, :]], axis=1)
    conv = conv.reshape(DEPTH, CONV + 1, 2 * FT, P).transpose(3, 0, 2, 1).reshape(P, -1)
    cols = np.concatenate([per_feature(a[n]) for n in ("c", "ada_b", "norm_g", "ret_norm_2", "ffn_norm_2", "sb_norm_2",
                                                        "gla_b_a")] + [conv], axis=1)
    assert cols.shape == (P, NCOL)
    ada_w = a["ada_w"].reshape(DEPTH, D, 6, D).transpose(0, 2, 1, 3).reshape(ADA_PARTS * D, D)
    shp, retc = shape_constants()
    w_in = a["gla_w_in"][0]
    arrays = {
        "x": a["x"].reshape(TT, P, D).transpose(1, 0, 2),
        "positions": a["positions"].reshape(TT, P).T,
        "stream": stream(a),
        "ada_w": ada_w,
        "cols": cols,
        "shp": shp,
        "retc": retc,
        "w_a": w_in[:, w_in.shape[1] - GRANK:].reshape(KT, P, GRANK).transpose(1, 0, 2).reshape(P, KT * GRANK),
        "w_a2": a["gla_w_a2"][0],
        "b_r": on_all(a["gla_b_r"]),
        "gla_norm": on_all(a["gla_norm_g"]),
        "lam": on_all(a["diff_lambda"]),
        "subln": on_all(a["diff_subln_g"]),
        "final_g": on_all(a["final_g"]),
        "final_norm": on_all(a["final_norm_2"]),
    }
    nc = bacc.Bacc("TRN2", target_bir_lowering=False, num_devices=1)
    arrays = {f"in_{k}": np.ascontiguousarray(v) for k, v in arrays.items()}
    args = [nc.dram_tensor(k, v.shape, mybir.dt.from_np(v.dtype), kind="ExternalInput").ap() for k, v in arrays.items()]
    out = nc.dram_tensor("out", (T, D), mybir.dt.float32, kind="ExternalOutput").ap()
    build(nc, *args, out)
    r = run(nc, [arrays], core_ids=[0])
    return r.results[0]["out"].reshape(1, T, D)
```

```python
import math

import numpy as np
import concourse.bass as bass
from concourse import mybir
from contextlib import ExitStack

P = 128
T = 256
TT = T // P
D = 1024
KT = D // P
DEPTH = 2
F_MLP = 4 * D
EPS = 1e-6
GH_, GDK, GDV, GCH = 4, 128, 256, 64
GRANK, GTAU = 16, 16.0
DH_, DDH, DDV = 8, 64, 128
ROPE_DIM, ROPE_THETA = 16, 500000.0
RH_, RDK, RDV = 4, 256, 512
SH_, SDH = 16, 64
F_FFN = 2816
FT = F_FFN // P
CONV = 3
NSLOT = 4
CHUNK = 2048
LAMBDA_INIT = 0.8 - 0.6 * math.exp(-0.3)
NEG = -2.0 ** 100
ROUND = 1.5 * 2.0 ** 23
TURN = (6.28125, 0.0019350051879882812, 3.0199159819e-07)
PI32 = 3.1415925

UNITS = F_MLP // 256
MLP_UNROLL, MLP_BODIES = 4, 3
GROUPS = FT // 2
C_GV, C_GQ, C_GK, C_GR, C_GO = 0, 4, 6, 8, 12
C_M0 = 16
C_DQ = C_M0 + 2 * UNITS
C_DK, C_DV, C_DO = C_DQ + 4, C_DQ + 8, C_DQ + 12
C_M1 = C_DQ + 16
C_RQ = C_M1 + 2 * UNITS
C_RK, C_RV, C_RG, C_RO = C_RQ + 4, C_RQ + 8, C_RQ + 16, C_RQ + 24
C_F0 = C_RQ + 32
C_SQ = C_F0 + 3 * GROUPS
C_SK, C_SV, C_SO = C_SQ + 4, C_SQ + 8, C_SQ + 12
C_F1 = C_SQ + 16
NCHUNK = C_F1 + 3 * GROUPS

SH_T, SC_T, GA_T, SH_C, SC_C, GA_C = range(6)
ADA_PARTS = 6 * DEPTH
ADA_STEPS = ADA_PARTS * KT
ADA_RING = 4

COL_C = 0
COL_ADAB = COL_C + KT
COL_NORM = COL_ADAB + ADA_PARTS * KT
COL_RET = COL_NORM + 4 * KT
COL_FFN = COL_RET + KT
COL_SB = COL_FFN + 2 * KT
COL_BA = COL_SB + KT
COL_CONV = COL_BA + GH_
NCOL = COL_CONV + 2 * 2 * FT * (CONV + 1)

S_ID = 0
S_GLAM = S_ID + P
S_SCAN = S_GLAM + P
S_CAUS = S_SCAN + T
S_SBM = S_CAUS + 2 * P
S_NU = S_SBM + P
S_NO = S_NU + P
S_INVF = S_NO + P
S_ONE = S_INVF + ROPE_DIM // 2
S_HALF = S_ONE + 1
NSHP = S_HALF + 8
NRETC = 2 * T + RH_ * 3 * P


class Count:

    def __init__(self, sem):
        self.sem, self.n = sem, 0

    def inc(self, instruction):
        instruction.then_inc(self.sem, 1)
        self.n = self.n + 1
        return self.n


def build(nc, x_d, pos_d, stream_d, ada_d, cols_d, shp_d, retc_d, wa_d, wa2_d, br_d, gng_d, lam_d, sub_d,
          fg_d, fn_d, out_d):
    f32, f32r, i32 = mybir.dt.float32, mybir.dt.float32r, mybir.dt.int32
    ALU = mybir.AluOpType
    ACT = mybir.ActivationFunctionType
    AX = mybir.AxisListType.X

    ctx = ExitStack()
    with ctx:
        def sb(name, shape, dt=f32):
            return ctx.enter_context(nc.sbuf_tensor(name, shape, dt))

        def sem(name):
            return ctx.enter_context(nc.semaphore(name))

        raw = sb("raw", [P, NSLOT, CHUNK])
        w_hi = sb("w_hi", [P, NSLOT, CHUNK], f32r)
        w_lo = sb("w_lo", [P, NSLOT, CHUNK], f32r)
        x = sb("x", [P, TT, D])
        h_hi = sb("h_hi", [P, KT, T], f32r)
        h_lo = sb("h_lo", [P, KT, T], f32r)
        row = sb("row", [P, D])
        acc = sb("acc", [P, D])
        ada_offset = nc.sbuf_base
        ada = sb("ada", [P, ADA_RING, D])
        cols = sb("cols", [P, NCOL])
        shp = sb("shp", [P, NSHP])
        mod = sb("mod", [P, ADA_PARTS * KT])
        gsc = sb("gsc", [P, 4 * KT])
        csil = sb("csil", [P, KT])
        maskr = sb("maskr", [P, 4 * P], f32r)
        gng = sb("gng", [P, GDV])
        sub = sb("sub", [P, DDV])
        lamc = sb("lamc", [P, 4])
        rope = sb("rope", [P, 2, TT, ROPE_DIM // 2])
        posi = sb("posi", [P, TT], i32)
        ssq = sb("ssq", [P, 16])
        rstd = sb("rstd", [P, 16])
        el = sb("el", [P, GH_ * 4])
        stat = sb("stat", [P, 2, 16])

        arena_offset = nc.sbuf_base
        arena = sb("arena", [P, 12 * 1024])
        A0 = arena_offset

        def at(name, word, shape, dt=f32):
            return nc.alloc_sbuf_tensor_at(name, [P, *shape], dt, offset=A0 + 4 * word)

        xn = at("xn", 0, [TT, D])
        h32 = at("h32", 2048, [KT, T])
        nd = at("nd", 4096, [TT, P])
        sq_out = at("sq_out", 4352, [TT, D])
        g_eb = at("g_eb", 0, [GH_, T])
        g_en = at("g_en", 1024, [GH_, T])
        g_es = at("g_es", 2048, [GH_, T])
        g_q = at("g_q", 3072, [GH_, TT, 2, P])
        g_ki = at("g_ki", 5120, [GH_, T])
        g_ks = at("g_ks", 6144, [GH_, T])
        g_w2 = at("g_w2", 6144, [GH_ * GDK])
        g_a = at("g_a", 6656, [T])
        g_wa = at("g_wa", 5120, [KT * GRANK])
        g_wah = at("g_wah", 5248, [KT * GRANK], f32r)
        g_wal = at("g_wal", 5376, [KT * GRANK], f32r)
        g_v = at("g_v", 7168, [TT, D])
        g_r = at("g_r", 9216, [TT, D])
        g_z = at("g_z", 9216, [GH_, T])
        g_t = at("g_t", 10240, [GH_, T])
        g_b = at("g_b", 11264, [GH_, T])
        g_kst = at("g_kst", 11264, [GH_, TT, P])
        g_sm = at("g_sm", 0, [GH_, TT, P])
        g_st = at("g_st", 1024, [2, 3, GDV])
        g_o = at("g_o", 5120, [TT, D])
        m_r = at("m_r", 4096, [2, 512])
        m_sq = at("m_sq", 5120, [2, 512])
        hid_hi = at("hid_hi", 7168, [2, 2, T], f32r)
        hid_lo = at("hid_lo", 8192, [2, 2, T], f32r)
        f_cv = at("f_cv", 4096, [2, 2, 2, T])
        f_p = at("f_p", 6144, [2, 2, T])
        diag = at("diag", 9216, [KT, P])
        d_q = at("d_q", 0, [TT, D])
        d_k = at("d_k", 2048, [TT, D])
        d_v = at("d_v", 4096, [TT, D])
        d_qt = at("d_qt", 6144, [KT, T])
        d_kt = at("d_kt", 8192, [KT, T])
        d_rt = at("d_rt", 10240, [4, TT, 16, 8])
        d_p = at("d_p", 0, [3, 2, 3 * P])
        d_a = at("d_a", 2304, [2, 3 * P])
        d_at = at("d_at", 3072, [2, 3 * P])
        d_st = at("d_st", 3840, [3, 3, 4])
        d_o = at("d_o", 10240, [TT, D])
        lamv = at("lamv", 10240, [256])
        lamp = at("lamp", 10496, [2, 64])
        ang = at("ang", 10752, [4, TT, 8])
        r_q = at("r_q", 0, [KT, T])
        r_k = at("r_k", 2048, [KT, T])
        r_v = at("r_v", 4096, [TT, RH_ * RDV])
        r_g = at("r_g", 8192, [TT, RH_ * RDV])
        y_hi = at("y_hi", 0, [KT, T], f32r)
        y_lo = at("y_lo", 2048, [KT, T], f32r)
        A1 = ada_offset

        def in_ada(name, word, shape):
            return nc.alloc_sbuf_tensor_at(name, [P, *shape], f32, offset=A1 + 4 * word)

        retc = in_ada("retc", 0, [NRETC])
        r_t = in_ada("r_t", NRETC, [2, 2, T])
        r_sm = in_ada("r_sm", NRETC, [RH_, 3 * P])
        s_q = at("s_q", 0, [KT, T])
        s_k = at("s_k", 2048, [KT, T])
        s_v = at("s_v", 4096, [TT, D])
        s_b = at("s_b", 6144, [3, 2, 2, 3 * P])

        ps = ctx.enter_context(nc.psum_tensor("ps", [P, 8, 512], f32))
        ident = shp[:, S_ID:S_ID + P]

        raw_in = [sem(f"raw_in{i}") for i in range(NSLOT)]
        hi_done = [sem(f"hi_done{i}") for i in range(NSLOT)]
        lo_done = [sem(f"lo_done{i}") for i in range(NSLOT)]
        used = [sem(f"used{i}") for i in range(NSLOT)]
        ada_in = [sem(f"ada_in{i}") for i in range(ADA_RING)]
        ada_more = [sem(f"ada_more{i}") for i in range(ADA_RING)]
        ada_step = sem("ada_step")
        ada_mm = sem("ada_mm")
        mod_done = sem("mod_done")
        cols_in = sem("cols_in")
        shp_in = sem("shp_in")
        x_in = sem("x_in")
        small_in = sem("small_in")
        retc_in = sem("retc_in")
        fg_in = sem("fg_in")
        fn_in = sem("fn_in")
        out_in = sem("out_in")
        csil_done = sem("csil_done")
        ssq_done = sem("ssq_done")
        mean_done = sem("mean_done")
        rstd_done = sem("rstd_done")
        nd_done = sem("nd_done")
        y_part = sem("y_part")
        tr_done = sem("tr_done")
        hh_done = sem("hh_done")
        hl_done = sem("hl_done")
        x_done = sem("x_done")
        y_act = sem("y_act")
        y_dve = sem("y_dve")
        diag_done = sem("diag_done")
        gate_mm = sem("gate_mm")
        gate_done = sem("gate_done")
        act_chain = sem("act_chain")
        dve_chain = sem("dve_chain")
        pool_chain = sem("pool_chain")
        wah_done = sem("wah_done")
        a_mm = sem("a_mm")
        a_done = sem("a_done")
        z_mm = sem("z_mm")
        z_done = sem("z_done")
        abs_done = sem("abs_done")
        ln_done = sem("ln_done")
        rel_done = sem("rel_done")
        eb_done = sem("eb_done")
        qzero = sem("qzero")
        c_dve = sem("c_dve")
        c_act = sem("c_act")
        sc_mm = sem("sc_mm")
        sm_done = sem("sm_done")
        kt_mm = sem("kt_mm")
        kst_done = sem("kst_done")
        kv_mm = sem("kv_mm")
        st_done = sem("st_done")
        go_mm = sem("go_mm")
        gsq_done = sem("gsq_done")
        grs_done = sem("grs_done")
        silu_done = sem("silu_done")
        o_done = sem("o_done")
        relu_done = sem("relu_done")
        sqh_done = sem("sqh_done")
        hid_done = sem("hid_done")
        cg_act = sem("cg_act")
        cv_act = sem("cv_act")
        cg_dve = sem("cg_dve")
        cv_dve = sem("cv_dve")
        fsilu = sem("fsilu")
        rope_q = sem("rope_q")
        rope_k = sem("rope_k")
        dtr = sem("dtr")
        dtr_act = sem("dtr_act")
        ds_mm = sem("ds_mm")
        ds_max = sem("ds_max")
        ds_exp = sem("ds_exp")
        da_done = sem("da_done")
        dat_mm = sem("dat_mm")
        dat_done = sem("dat_done")
        do_mm = sem("do_mm")
        do_act = sem("do_act")
        drs = sem("drs")
        rs_mm = sem("rs_mm")
        rsm_done = sem("rsm_done")
        ro_mm = sem("ro_mm")
        rsq = sem("rsq")
        rrs = sem("rrs")
        ry = sem("ry")
        z_ready = sem("z_ready")
        sln = sem("sln")
        mask_done = sem("mask_done")
        spm = sem("spm")
        e_mm = sem("e_mm")
        sexp = sem("sexp")
        so_mm = sem("so_mm")
        so_hi = sem("so_hi")
        so_lo = sem("so_lo")
        ang_done = sem("ang_done")
        rope_done = sem("rope_done")
        lam_sum = sem("lam_sum")
        lam_exp = sem("lam_exp")
        gsc_done = sem("gsc_done")
        wal_done = sem("wal_done")
        fin_done = sem("fin_done")
        sq_done = sem("sq_done")
        rqk_done = sem("rqk_done")


        block = ctx.enter_context(nc.Block())

        (TR_N0, TR_GO, TR_N1, TR_N2, TR_DO, TR_N3, TR_N4, TR_RA, TR_RB, TR_N5, TR_N6, TR_N7) = range(12)
        (Y_GV, Y_GR, Y_GOUT, Y_M0, Y_DQ, Y_DK, Y_DV, Y_DOUT, Y_M1, Y_RV0, Y_RV1, Y_RG0, Y_RG1, Y_ROUT, Y_F0,
         Y_SV, Y_SOUT, Y_F1) = range(18)
        BY_ACT = [Y_GV, Y_DQ, Y_DK, Y_DV, Y_RV0, Y_RV1, Y_RG0, Y_RG1, Y_SV]
        BY_DVE = [Y_GR, Y_GOUT, Y_M0, Y_DOUT, Y_M1, Y_ROUT, Y_F0, Y_SOUT, Y_F1]
        X_GLA, X_M0, X_DIFF, X_M1, X_FG, X_RET, X_F0, X_SB, X_F1 = 4, 8, 12, 16, 18, 22, 26, 30, 34
        N_C_RET = 4
        Y_LAST = [C_GQ - 1, C_GO - 1, C_M0 - 1, C_DQ - 1, C_DK - 1, C_DV - 1, C_DO - 1, C_M1 - 1, C_RQ - 1,
                  C_RV + 3, C_RG - 1, C_RG + 3, C_RO - 1, C_F0 - 1, C_SQ - 1, C_SO - 1, C_F1 - 1, NCHUNK - 1]

        def y_read(y, bank):
            if y in BY_ACT:
                return y_act, 4 * BY_ACT.index(y) + bank + 1
            return y_dve, 4 * BY_DVE.index(y) + bank + 1

        def y_written(y, bank):
            return (y_part, 3 * y + bank + 1) if bank < 3 else multiplied(Y_LAST[y])

        def so_bank(p):
            return p if p >= 6 else p % 2

        def slot_visit(c):
            return c if isinstance(c, tuple) else (c % NSLOT, c // NSLOT)

        def multiplied(c):
            s, v = slot_visit(c)
            return used[s], v + 1

        def ffn_chunk(c0, g, part):
            if part == 2:
                return c0 + 3 * GROUPS - 1 if g == GROUPS - 1 else ffn_chunk(c0, g + 1, 1) + 1
            return c0 + (part if g == 0 else 3 * g - 1 + part)

        def d_bank(h):
            return (2, 4, 6)[h % 3]

        def s_bank(p):
            return (2, 4, 6)[p % 3]

        def bcast(ap, n):
            k = ap.shape[1]
            return ap.rearrange("p (o k) -> p o k", o=1).to_broadcast([P, n, k])

        @block.sync
        def _(sp):
            sp.dma_start(cols[:, :], cols_d).then_inc(cols_in, 16)
            sp.dma_start(x[:, :, :], x_d).then_inc(x_in, 16)
            sp.dma_start(shp[:, :], shp_d).then_inc(shp_in, 16)
            for s in range(2 * KT):
                if s >= ADA_RING:
                    sp.wait_ge(ada_step, s - ADA_RING + 1)
                sp.dma_start(ada[:, s % ADA_RING, :], ada_d[s * P:(s + 1) * P, :]).then_inc(ada_in[s % ADA_RING], 16)
            for c in range(NSLOT):
                sp.dma_start(raw[:, c, :], stream_d[c * P:(c + 1) * P, :]).then_inc(raw_in[c], 16)
            with sp.Fori(1, NCHUNK // NSLOT) as i:
                for s in range(NSLOT):
                    sp.wait_ge(lo_done[s], i)
                    sp.dma_start(raw[:, s, :], stream_d[bass.ds((i * NSLOT + s) * P, P), :]).then_inc(raw_in[s], 16)
            for c in range(NCHUNK - NCHUNK % NSLOT, NCHUNK):
                s, v = slot_visit(c)
                sp.wait_ge(lo_done[s], v)
                sp.dma_start(raw[:, s, :], stream_d[c * P:(c + 1) * P, :]).then_inc(raw_in[s], 16)
            for t in range(TT):
                sp.wait_ge(fin_done, 1 + t)
                sp.dma_start(out_d[t * P:(t + 1) * P, :], xn[:, t, :]).then_inc(out_in, 16)
            sp.wait_ge(out_in, 16 * TT)

        @block.gpsimd
        def _(pool):
            pc = Count(pool_chain)
            for dst, src in ((posi[:, :], pos_d), (lamv[:, :], lam_d), (gng[:, :], gng_d), (sub[:, :], sub_d),
                             (g_wa[:, :], wa_d), (g_w2[0:GRANK, :], wa2_d), (row[:, :], br_d)):
                pool.dma_start(dst, src).then_inc(small_in, 16)

            def inverse_rms(out, sums, n, width):
                pc.inc(pool.tensor_scalar(sums, sums, 1.0 / width, EPS, ALU.mult, ALU.add))
                pool.wait_ge(pool_chain, pc.n)
                return pool.tensor_tensor(out, sums, shp[:, S_HALF:S_HALF + n], ALU.pow)

            def norm(k):
                pool.wait_ge(mean_done, k + 1)
                pool.tensor_tensor(rstd[:, 0:TT], ssq[:, 4:6], shp[:, S_HALF:S_HALF + TT], ALU.pow)\
                    .then_inc(rstd_done, 1)

            def ada_load(s):
                pool.wait_ge(ada_step, s - ADA_RING + 1)
                pool.dma_start(ada[:, s % ADA_RING, :], ada_d[s * P:(s + 1) * P, :]).then_inc(ada_more[s % ADA_RING], 16)

            pool.wait_ge(shp_in, 16)
            norm(0)
            for s in range(2 * KT, 2 * KT + ADA_RING):
                ada_load(s)
            pool.wait_ge(hl_done, 4)
            pool.memset(g_q[:, :, :, :, :], 0.0).then_inc(qzero, 1)
            for s in range(2 * KT + ADA_RING, 5 * KT):
                ada_load(s)
            for h in range(GH_):
                pool.wait_ge(gsq_done, 2 * h + 2)
                inverse_rms(stat[:, 1, 2 * h:2 * h + 2], stat[:, 0, 2 * h:2 * h + 2], 2, GDV).then_inc(grs_done, 1)
            norm(1)
            with pool.Fori(0, MLP_BODIES) as i:
                for k in range(KT):
                    pool.wait_ge(ada_step, i * KT + (5 * KT + k - ADA_RING + 1))
                    pool.dma_start(ada[:, k % ADA_RING, :], ada_d[bass.ds((i * KT + (5 * KT + k)) * P, P), :])\
                        .then_inc(ada_more[k % ADA_RING], 16)
            norm(2)
            for s in range(8 * KT, 11 * KT + ADA_RING):
                ada_load(s)
            for h in range(DH_):
                pool.wait_ge(do_act, h + 1)
                inverse_rms(stat[:, 1, 2 * h:2 * h + 2], stat[:, 0, 2 * h:2 * h + 2], 2, DDV).then_inc(drs, 1)
            for s in range(11 * KT + ADA_RING, ADA_STEPS):
                ada_load(s)
            norm(3)
            pool.wait_ge(ada_step, ADA_STEPS)
            pool.dma_start(retc[:, :], retc_d).then_inc(retc_in, 16)
            pool.wait_ge(ada_mm, ADA_PARTS)
            pool.dma_start(acc[:, :], fg_d).then_inc(fg_in, 16)
            norm(4)
            norm(5)
            pool.dma_start(acc[:, :], fn_d).then_inc(fn_in, 16)
            for h in range(RH_):
                pool.wait_ge(rsq, 2 * h + 2)
                inverse_rms(stat[:, 1, 2 * h:2 * h + 2], stat[:, 0, 2 * h:2 * h + 2], 2, RDV).then_inc(rrs, 1)
            for k in range(6, 10):
                norm(k)

        @block.scalar
        def _(act):
            ac = Count(act_chain)

            def hi(c):
                if not isinstance(c, tuple) and c >= NCHUNK:
                    return
                s, v = slot_visit(c)
                act.wait_ge(raw_in[s], v * 16 + 16)
                if isinstance(c, tuple) or v:
                    act.wait_ge(used[s], v)
                act.activation(w_hi[:, s, :], raw[:, s, :], ACT.Copy).then_inc(hi_done[s], 1)

            def squares(k, x_count, dst=sq_out):
                for n in range(4):
                    t, half = n // 2, n % 2
                    if x_count == X_FG:
                        act.wait_ge(x_done, X_FG - 1 + t)
                    elif x_count is not None:
                        act.wait_ge(x_done, x_count - 3 + n)
                    part = slice(half * 512, (half + 1) * 512)
                    act.activation(dst[:, t, part], x[:, t, part], ACT.Square, scale=D ** -0.5,
                                   accum_out=ssq[:, 2 * half + t:2 * half + t + 1]).then_inc(ssq_done, 1)

            def norm(k, x_count, stage, late, scale_col, bias_col):
                squares(k, x_count)
                hi(late)
                norm_rows(stage, scale_col, bias_col)

            def norm_rows(stage, scale_col, bias_col):
                for b in range(4):
                    act.wait_ge(tr_done, 4 * stage + b + 1)
                    for j in range(2):
                        kt = 2 * b + j
                        last = act.activation(h32[:, kt, :], ps[:, 4 + b, j * T:(j + 1) * T], ACT.Identity,
                                              bias=bias_col(kt) if bias_col else 0.0, scale=scale_col(kt))
                    last.then_inc(hh_done, 1)

            def split_stage(stage, dst):
                for b in range(4):
                    act.wait_ge(tr_done, 4 * stage + b + 1)
                    act.activation(dst[:, 2 * b:2 * b + 2, :].rearrange("p k t -> p (k t)"), ps[:, 4 + b, :],
                                   ACT.Copy).then_inc(hh_done, 1)

            def read_y(y, dst, scale=1.0, func=ACT.Copy):
                for b in range(4):
                    act.wait_ge(*y_written(y, b))
                    act.activation(dst[:, b // 2, (b % 2) * 512:(b % 2 + 1) * 512], ps[:, b, :], func, scale=scale)\
                        .then_inc(y_act, 1)

            def gate_row(g):
                act.wait_ge(gate_mm, g + 1)
                for j in range(2):
                    last = act.activation(row[:, j * 512:(j + 1) * 512], ps[:, 6 + j, :], ACT.Copy, scale=-1.0)
                last.then_inc(gate_done, 1)

            act.wait_ge(cols_in, 16)
            act.activation(csil[:, :], cols[:, COL_C:COL_C + KT], ACT.Silu).then_inc(csil_done, 1)
            act.wait_ge(x_in, 16)
            squares(0, None, xn)
            act.wait_ge(ang_done, 1)
            act.activation(rope[:, :, :, :].rearrange("p a t k -> p (a t k)"),
                           ang[:, 2:4, :, :].rearrange("p a t k -> p (a t k)"), ACT.Sin).then_inc(rope_done, 1)
            act.activation(maskr[:, 0:P], ident, ACT.Copy)
            act.activation(maskr[:, P:4 * P], shp[:, S_CAUS:S_CAUS + 3 * P], ACT.Copy).then_inc(mask_done, 1)
            act.wait_ge(lam_sum, 1)
            act.activation(lamc[:, 2:4], lamc[:, 0:2], ACT.Exp).then_inc(lam_exp, 1)
            act.activation(g_wah[:, :], g_wa[:, :], ACT.Copy).then_inc(wah_done, 1)
            for c in range(NSLOT):
                hi(c)
            act.wait_ge(gsc_done, 1)
            norm_rows(TR_N0, lambda kt: gsc[:, kt:kt + 1], lambda kt: mod[:, SH_T * KT + kt:SH_T * KT + kt + 1])

            act.wait_ge(abs_done, 1)
            ac.inc(act.activation(g_t[:, :, :], g_t[:, :, :], ACT.Exp, scale=-1.0))
            act.wait_ge(act_chain, ac.n)
            act.activation(g_t[:, :, :], g_t[:, :, :], ACT.Ln, bias=shp[:, S_ONE:S_ONE + 1]).then_inc(ln_done, 1)
            hi(C_GV + 4)
            hi(C_GV + 5)
            act.wait_ge(rel_done, 1)
            act.activation(g_eb[:, :, :], g_b[:, :, :], ACT.Exp, scale=1.0 / GTAU)
            act.activation(g_en[:, :, :], g_b[:, :, :], ACT.Exp, scale=-1.0 / GTAU)
            act.activation(el[:, :], g_b[:, :, :].rearrange("p h (c j) -> p (h c) j", j=GCH)[:, :, GCH - 1],
                           ACT.Exp, scale=1.0 / GTAU)
            act.activation(g_es[:, :, :], g_t[:, :, :], ACT.Exp, scale=1.0 / GTAU).then_inc(eb_done, 1)
            hi(C_GV + 6)
            read_y(Y_GV, g_v)
            for c in range(C_GV + 3, C_GR + 2):
                hi(c + 4)
            for b in range(2):
                act.wait_ge(kt_mm, b + 1)
                act.activation(g_kst[:, 2 * b:2 * b + 2, :, :].rearrange("p h t k -> p (h t k)"), ps[:, 6 + b, :],
                               ACT.Copy).then_inc(kst_done, 1)
            for c in range(C_GR + 2, C_GO):
                hi(c + 4)
            for b in range(4):
                act.wait_ge(*y_read(Y_GR, b))
                g = g_r[:, b // 2, (b % 2) * 512:(b % 2 + 1) * 512]
                act.activation(g, g, ACT.Silu).then_inc(silu_done, 1)
            for h in range(GH_):
                act.wait_ge(go_mm, h + 1)
                for t in range(TT):
                    k = 2 * h + t
                    act.activation(h_hi[:, k, :], ps[:, h, t * GDV:(t + 1) * GDV], ACT.Square,
                                   accum_out=stat[:, 0, k:k + 1]).then_inc(gsq_done, 1)
            split_stage(TR_GO, h_hi)
            for c in range(C_GO, C_GO + 3):
                hi(c + 4)
            gate_row(0)
            act.wait_ge(gsc_done, 2)
            norm(1, X_GLA, TR_N1, C_GO + 7, lambda kt: gsc[:, KT + kt:KT + kt + 1],
                 lambda kt: mod[:, SH_C * KT + kt:SH_C * KT + kt + 1])

            def mlp(layer, c0):
                B = UNITS * layer

                def unit(u, par, later, c):
                    act.wait_ge(*multiplied(c))
                    if later:
                        act.wait_ge(hid_done, u - 1)
                    act.activation(m_r[:, par, :], ps[:, 4 + par, :], ACT.Relu).then_inc(relu_done, 1)
                    act.wait_ge(relu_done, u + 1)
                    act.activation(hid_hi[:, par, :, :].rearrange("p f t -> p (f t)"), m_r[:, par, :], ACT.Square)\
                        .then_inc(sqh_done, 1)

                unit(B, 0, False, c0)
                hi(c0 + 4)
                unit(B + 1, 1, False, c0 + 1)
                hi(c0 + 5)
                hi(c0 + 6)
                with act.Fori(0, MLP_BODIES) as it:
                    for j in range(MLP_UNROLL):
                        c = c0 + 3 + 2 * j
                        unit(it * MLP_UNROLL + (B + 2 + j), j % 2, True, (c % NSLOT, it * 2 + c // NSLOT))
                        for c in (c + 4, c + 5):
                            hi((c % NSLOT, it * 2 + c // NSLOT))
                c = c0 + 7 + 2 * MLP_UNROLL * MLP_BODIES
                for i in range(2 + MLP_UNROLL * MLP_BODIES, UNITS):
                    unit(B + i, i % 2, True, c - 4)
                    hi(c)
                    hi(c + 1)
                    c += 2
                gate_row(2 * layer + 1)

            mlp(0, C_M0)
            act.wait_ge(gsc_done, 3)
            norm(2, X_M0, TR_N2, C_DQ + 3, lambda kt: gsc[:, 2 * KT + kt:2 * KT + kt + 1],
                 lambda kt: mod[:, (6 + SH_T) * KT + kt:(6 + SH_T) * KT + kt + 1])

            def d_features(dst, n):
                for b in range(4):
                    act.wait_ge(dtr, n + b + 1)
                    act.activation(dst[:, 2 * b:2 * b + 2, :].rearrange("p k t -> p (k t)"), ps[:, 4 + b, :],
                                   ACT.Copy).then_inc(dtr_act, 1)

            for c in range(C_DQ, C_DQ + 3):
                hi(c + 4)
            read_y(Y_DQ, d_q, DDH ** -0.5)
            for c in range(C_DQ + 3, C_DK + 3):
                hi(c + 4)
            read_y(Y_DK, d_k)
            hi(C_DK + 7)
            d_features(d_qt, 0)
            hi(C_DV + 4)
            hi(C_DV + 5)
            d_features(d_kt, 4)
            hi(C_DV + 6)
            read_y(Y_DV, d_v)
            hi(C_DV + 7)

            def d_exp(h):
                act.wait_ge(ds_max, h + 1)
                r = h % 3
                for i in range(2):
                    for t, first, n in ((1, 0, 2 * P), (0, 2 * P, P)):
                        k = 2 * i + t
                        last = act.activation(d_p[:, r, i, first:first + n], ps[:, d_bank(h) + i, first:first + n],
                                              ACT.Exp, bias=d_st[:, r, 0, k:k + 1], accum_out=d_st[:, r, 1, k:k + 1])
                last.then_inc(ds_exp, 1)

            def d_out(h):
                act.wait_ge(do_mm, h + 1)
                out = ps[:, 0, (h % 2) * T:(h % 2 + 1) * T].rearrange("p (t k) -> p t k", t=TT)
                for t in range(TT):
                    act.activation(h_lo[:, 2 * (h % 2) + t, 0:DDV], out[:, t, :], ACT.Square,
                                   accum_out=stat[:, 0, 2 * h + t:2 * h + t + 1])
                act.activation(d_o[:, :, h * DDV:(h + 1) * DDV], out, ACT.Copy).then_inc(do_act, 1)

            for h in range(3):
                d_exp(h)
            for h in range(DH_):
                d_out(h)
                if h + 3 < DH_:
                    act.wait_ge(da_done, h + 1)
                    d_exp(h + 3)
            split_stage(TR_DO, h_hi)
            for c in range(C_DO, C_DO + 3):
                hi(c + 4)
            gate_row(2)
            act.wait_ge(gsc_done, 4)
            norm(3, X_DIFF, TR_N3, C_DO + 7, lambda kt: gsc[:, 3 * KT + kt:3 * KT + kt + 1],
                 lambda kt: mod[:, (6 + SH_C) * KT + kt:(6 + SH_C) * KT + kt + 1])
            mlp(1, C_M1)
            squares(4, X_M1)
            norm(5, X_FG, TR_N4, C_RQ + 3, lambda kt: cols[:, COL_RET + kt:COL_RET + kt + 1], None)

            for c in range(C_RQ, C_RV + 3):
                hi(c + 4)
            read_y(Y_RV0, r_v[:, :, 0:D])
            for c in range(C_RV + 3, C_RV + 7):
                hi(c + 4)
            read_y(Y_RV1, r_v[:, :, D:2 * D])
            for c in range(C_RV + 7, C_RG + 3):
                hi(c + 4)
            read_y(Y_RG0, r_g[:, :, 0:D], 1.0, ACT.Silu)
            for c in range(C_RG + 3, C_RG + 7):
                hi(c + 4)
            read_y(Y_RG1, r_g[:, :, D:2 * D], 1.0, ACT.Silu)
            hi(C_RG + 11)
            for k in range(TT * RH_):
                act.wait_ge(ro_mm, k + 1)
                junk = (h_hi if k < 4 else h_lo)[:, 2 * (k % 4):2 * (k % 4) + 2, :].rearrange("p k t -> p (k t)")
                act.activation(junk, ps[:, k % 4, :], ACT.Square, accum_out=stat[:, 0, k:k + 1]).then_inc(rsq, 1)
            split_stage(TR_RA, h_hi)
            split_stage(TR_RB, y_hi)
            for c in range(C_RO, C_RO + 7):
                hi(c + 4)
            norm(6, X_RET, TR_N5, C_RO + 11, lambda kt: cols[:, COL_FFN + kt:COL_FFN + kt + 1], None)

            def ffn(layer, c0):
                def last_tap(g, value):
                    G = GROUPS * layer + g
                    act.wait_ge(*multiplied(ffn_chunk(c0, g, value)))
                    if g >= 2:
                        act.wait_ge(hid_done, 2 * UNITS + G - 1)
                    for f in range(2):
                        k = COL_CONV + ((layer * 2 + value) * FT + 2 * g + f) * (CONV + 1)
                        last = act.activation(f_cv[:, g % 2, value, f, :],
                                              ps[:, 4 + 2 * (g % 2) + value, f * T:(f + 1) * T],
                                              ACT.Identity, bias=cols[:, k + 3:k + 4], scale=cols[:, k + 2:k + 3])
                    last.then_inc(cv_act if value else cg_act, 1)

                c = c0 + 4
                for g in range(GROUPS):
                    last_tap(g, 0)
                    hi(c)
                    act.wait_ge(cg_dve, GROUPS * layer + g + 1)
                    act.activation(f_cv[:, g % 2, 0, :, :], f_cv[:, g % 2, 0, :, :], ACT.Silu).then_inc(fsilu, 1)
                    last_tap(g, 1)
                    hi(c + 1)
                    c += 2
                    if g:
                        hi(c)
                        c += 1

            ffn(0, C_F0)
            norm(7, X_F0, TR_N6, C_SQ + 3, lambda kt: cols[:, COL_SB + kt:COL_SB + kt + 1], None)

            for n in range(2 * KT // 2):
                act.wait_ge(*multiplied(C_SQ + n))
                dst, m = (s_q, n) if n < 4 else (s_k, n - 4)
                act.activation(dst[:, 2 * m:2 * m + 2, :].rearrange("p k t -> p (k t)"), ps[:, 4 + n % 4, :], ACT.Copy,
                               scale=SDH ** -0.5 if n < 4 else 1.0).then_inc(c_act, 1)
                hi(C_SQ + n + 4)
            for c in range(C_SV, C_SV + 3):
                hi(c + 4)
            read_y(Y_SV, s_v)
            hi(C_SV + 7)

            def s_log(p):
                act.wait_ge(z_ready, p + 1)
                ln = s_b[:, p % 3, 0, :, :]
                if p >= 3:
                    act.wait_ge(so_mm, p - 2)
                ac.inc(act.activation(ln, ps[:, s_bank(p):s_bank(p) + 2, 0:3 * P], ACT.Abs))
                act.wait_ge(act_chain, ac.n)
                ac.inc(act.activation(ln, ln, ACT.Exp, scale=-1.0))
                act.wait_ge(act_chain, ac.n)
                act.activation(ln, ln, ACT.Ln, bias=shp[:, S_ONE:S_ONE + 1]).then_inc(sln, 1)

            def s_exp(p):
                act.wait_ge(e_mm, p + 1)
                act.activation(s_b[:, p % 3, 0, :, :], ps[:, s_bank(p):s_bank(p) + 2, 0:3 * P], ACT.Exp)\
                    .then_inc(sexp, 1)

            def s_out(p):
                act.wait_ge(so_mm, p + 1)
                act.activation(h_hi[:, p, :], ps[:, so_bank(p), 0:T], ACT.Copy).then_inc(so_hi, 1)

            s_log(0)
            s_log(1)
            for p in range(SH_ // 2):
                s_exp(p)
                if p >= 1:
                    s_out(p - 1)
                if p + 2 < SH_ // 2:
                    s_log(p + 2)
            s_out(SH_ // 2 - 1)
            for c in range(C_SO, C_SO + 3):
                hi(c + 4)
            norm(8, X_SB, TR_N7, C_SO + 7, lambda kt: cols[:, COL_FFN + KT + kt:COL_FFN + KT + kt + 1], None)
            ffn(1, C_F1)
            squares(9, X_F1)

        @block.vector
        def _(dve):
            dc = Count(dve_chain)

            def link(instruction):
                dc.inc(instruction)
                dve.wait_ge(dve_chain, dc.n)

            def lo(c):
                if not isinstance(c, tuple) and c >= NCHUNK:
                    return
                s, v = slot_visit(c)
                dve.wait_ge(hi_done[s], v + 1)
                dve.tensor_tensor(w_lo[:, s, :], raw[:, s, :], w_hi[:, s, :].bitcast(f32), ALU.subtract)\
                    .then_inc(lo_done[s], 1)

            def add_step(s, k, ring_fill, early=False):
                dve.wait_ge((ada_in if early else ada_more)[k % ADA_RING], ring_fill)
                rows, ck = ada[:, k % ADA_RING, :], csil[:, k:k + 1]
                if k == 0:
                    dve.tensor_scalar(acc[:, :], rows, ck, None, ALU.mult).then_inc(ada_step, 1)
                else:
                    dve.wait_ge(ada_step, s)
                    dve.scalar_tensor_tensor(acc[:, :], rows, ck, acc[:, :], ALU.mult, ALU.add).then_inc(ada_step, 1)

            def steps(first, n):
                for s in range(first, first + n):
                    if s % KT == 0 and s:
                        dve.wait_ge(ada_mm, s // KT)
                    if s < 2 * KT:
                        add_step(s, s % KT, 16 * (s // ADA_RING + 1), True)
                    else:
                        add_step(s, s % KT, 16 * ((s - 2 * KT) // ADA_RING + 1))

            def finish_part(p, bank):
                dve.wait_ge(ada_mm, p + 1)
                dve.tensor_tensor(mod[:, p * KT:(p + 1) * KT], ps[:, bank, 0:KT],
                                  cols[:, COL_ADAB + p * KT:COL_ADAB + (p + 1) * KT], ALU.add).then_inc(mod_done, 1)

            def norm_scale(n, p):
                dve.wait_ge(mod_done, p + 1)
                dve.scalar_tensor_tensor(gsc[:, n * KT:(n + 1) * KT], mod[:, p * KT:(p + 1) * KT], 1.0,
                                         cols[:, COL_NORM + n * KT:COL_NORM + (n + 1) * KT], ALU.add, ALU.mult)\
                    .then_inc(gsc_done, 1)
                dve.wait_ge(gsc_done, n + 1)

            def norm_mean(k):
                dve.wait_ge(ssq_done, 4 * (k + 1))
                dve.scalar_tensor_tensor(ssq[:, 4:6], ssq[:, 0:2], EPS, ssq[:, 2:4], ALU.add, ALU.add)\
                    .then_inc(mean_done, 1)

            def norm_diag(k):
                norm_mean(k)
                dve.wait_ge(rstd_done, k + 1)
                for t in range(TT):
                    last = dve.tensor_scalar(nd[:, t, :], ident, rstd[:, t:t + 1], None, ALU.mult)
                last.then_inc(nd_done, 1)

            def norm_split(stage):
                for b in range(4):
                    pair = slice(2 * b, 2 * b + 2)
                    dve.wait_ge(hh_done, 4 * stage + b + 1)
                    link(dve.tensor_copy(h_hi[:, pair, :], h32[:, pair, :]))
                    dve.tensor_tensor(h_lo[:, pair, :], h32[:, pair, :], h_hi[:, pair, :].bitcast(f32), ALU.subtract)\
                        .then_inc(hl_done, 1)

            def split_stage(stage, dst, src_hi):
                for b in range(4):
                    dve.wait_ge(hh_done, 4 * stage + b + 1)
                    dve.tensor_tensor(dst[:, 2 * b:2 * b + 2, :].rearrange("p k t -> p (k t)"), ps[:, 4 + b, :],
                                      src_hi[:, 2 * b:2 * b + 2, :].rearrange("p k t -> p (k t)").bitcast(f32),
                                      ALU.subtract).then_inc(hl_done, 1)

            def make_diag(p):
                dve.wait_ge(mod_done, p + 1)
                for kt in range(KT):
                    last = dve.tensor_scalar(diag[:, kt, :], ident, mod[:, p * KT + kt:p * KT + kt + 1], None, ALU.mult)
                last.then_inc(diag_done, 1)

            def add_gated(y, g):
                dve.wait_ge(gate_done, g + 1)
                for b in range(4):
                    dve.wait_ge(*y_written(y, b))
                    half = slice((b % 2) * 512, (b % 2 + 1) * 512)
                    dve.tensor_tensor(xn[:, b // 2, half], ps[:, b, :], row[:, half], ALU.mult).then_inc(y_dve, 1)
                    dve.wait_ge(*y_read(y, b))
                    dve.tensor_tensor(x[:, b // 2, half], x[:, b // 2, half], xn[:, b // 2, half], ALU.add)\
                        .then_inc(x_done, 1)

            dve.wait_ge(small_in, 16 * 7)
            dve.wait_ge(shp_in, 16)
            pf = stat[:, 0, 0:TT]
            link(dve.tensor_copy(pf, posi[:, :]))
            for t in range(TT):
                last = dve.tensor_scalar(ang[:, 0, t, :], shp[:, S_INVF:S_INVF + 8], stat[:, 0, t:t + 1], None, ALU.mult)
            link(last)
            for n, quarter in ((2, 0.25), (3, 0.0)):
                link(dve.tensor_scalar(ang[:, 1, :, :], ang[:, 0, :, :], 1.0 / (2 * math.pi), quarter, ALU.mult, ALU.add))
                link(dve.tensor_scalar(ang[:, 1, :, :], ang[:, 1, :, :], ROUND, -ROUND, ALU.add, ALU.add))
                link(dve.scalar_tensor_tensor(ang[:, n, :, :], ang[:, 1, :, :], -TURN[0], ang[:, 0, :, :], ALU.mult, ALU.add))
                link(dve.scalar_tensor_tensor(ang[:, n, :, :], ang[:, 1, :, :], -TURN[1], ang[:, n, :, :], ALU.mult, ALU.add))
                link(dve.scalar_tensor_tensor(ang[:, n, :, :], ang[:, 1, :, :], -TURN[2], ang[:, n, :, :], ALU.mult, ALU.add))
                if quarter:
                    link(dve.tensor_scalar(ang[:, n, :, :], ang[:, n, :, :], math.pi / 2, None, ALU.add))
            dve.tensor_scalar(ang[:, 2:4, :, :].rearrange("p a t k -> p (a t k)"),
                              ang[:, 2:4, :, :].rearrange("p a t k -> p (a t k)"), PI32, -PI32, ALU.min, ALU.max)\
                .then_inc(ang_done, 1)
            lv = lamv[:, :].rearrange("p (a b k) -> p a b k", a=2, b=2)
            link(dve.tensor_tensor(lamp[:, :, :], lv[:, :, 0, :], lv[:, :, 1, :], ALU.mult))
            dve.tensor_reduce(lamc[:, 0:2], lamp[:, :, :], AX, ALU.add).then_inc(lam_sum, 1)
            dve.tensor_scalar(sub[:, :], sub[:, :], 1.0 - LAMBDA_INIT, None, ALU.mult)
            dve.wait_ge(lam_exp, 1)
            link(dve.tensor_tensor(lamc[:, 0:1], lamc[:, 3:4], lamc[:, 2:3], ALU.subtract))
            link(dve.tensor_scalar(lamc[:, 0:1], lamc[:, 0:1], -LAMBDA_INIT, None, ALU.add))
            dve.wait_ge(wah_done, 1)
            dve.tensor_tensor(g_wal[:, :], g_wa[:, :], g_wah[:, :].bitcast(f32), ALU.subtract).then_inc(wal_done, 1)

            norm_diag(0)
            dve.wait_ge(csil_done, 1)
            steps(0, KT)
            finish_part(0, 0)
            steps(KT, KT)
            finish_part(1, 0)
            norm_scale(0, SC_T)
            norm_split(TR_N0)
            for c in range(NSLOT):
                lo(c)

            dve.wait_ge(a_mm, 1)
            dve.tensor_copy(g_a[0:GRANK, :], ps[0:GRANK, 4, 0:T]).then_inc(a_done, 1)
            dve.wait_ge(z_mm, 1)
            for h in range(GH_):
                last = dve.tensor_scalar(g_z[:, h, :], ps[:, 6 + h // 2, (h % 2) * T:(h % 2 + 1) * T],
                                         cols[:, COL_BA + h:COL_BA + h + 1], None, ALU.add)
            last.then_inc(z_done, 1)
            dve.wait_ge(z_done, 1)
            dve.scalar_tensor_tensor(g_t[:, :, :], g_z[:, :, :], -1.0, g_z[:, :, :], ALU.mult, ALU.max)\
                .then_inc(abs_done, 1)
            dve.wait_ge(abs_done, 1)
            lo(4)
            link(dve.tensor_scalar(g_z[:, :, :], g_z[:, :, :], 0.0, None, ALU.min))
            dve.wait_ge(ln_done, 1)
            link(dve.scalar_tensor_tensor(g_t[:, :, :], g_t[:, :, :], -1.0, g_z[:, :, :], ALU.mult, ALU.add))
            for h in range(GH_):
                last = dve.tensor_tensor_scan(g_b[:, h, :], shp[:, S_SCAN:S_SCAN + T], g_t[:, h, :], 0.0,
                                              ALU.mult, ALU.add)
            link(last)
            bv = g_b[:, :, :].rearrange("p h (c j) -> p (h c) j", j=GCH)
            dve.tensor_tensor(g_t[:, :, :].rearrange("p h (c j) -> p (h c) j", j=GCH),
                              bv[:, :, GCH - 1:GCH].to_broadcast([P, GH_ * 4, GCH]), bv, ALU.subtract)\
                .then_inc(rel_done, 1)
            lo(5)
            steps(2 * KT, 4)
            lo(6)
            lo(7)
            steps(2 * KT + 4, 4)
            dve.wait_ge(eb_done, 1)
            dve.wait_ge(qzero, 1)
            for n in range(2):
                dve.wait_ge(*multiplied(C_GQ + n))
                for f in range(2):
                    h = 2 * n + f
                    src = ps[:, 4 + n, f * T:(f + 1) * T].rearrange("p (t c j) -> p t c j", t=TT, c=2)
                    dec = g_eb[:, h, :].rearrange("p (t c j) -> p t c j", t=TT, c=2)
                    for c in range(2):
                        last = dve.scalar_tensor_tensor(g_q[:, h, :, c, c * GCH:(c + 1) * GCH], src[:, :, c, :],
                                                        GDK ** -0.5, dec[:, :, c, :], ALU.mult, ALU.mult)
                last.then_inc(c_dve, 1)
                lo(C_GQ + n + 4)
                steps(3 * KT + 2 * n, 2)
                if n == 0:
                    finish_part(2, 6)
            for n in range(2):
                dve.wait_ge(*multiplied(C_GK + n))
                flat = lambda a: a[:, 2 * n:2 * n + 2, :].rearrange("p h t -> p (h t)")
                dve.tensor_tensor(flat(g_ki), ps[:, 4 + n, :], flat(g_en), ALU.mult)
                dve.tensor_tensor(flat(g_ks), ps[:, 4 + n, :], flat(g_es), ALU.mult).then_inc(c_dve, 1)
                lo(C_GK + n + 4)
                steps(3 * KT + 4 + 2 * n, 2)
            lo(C_GR + 4)
            finish_part(3, 6)
            steps(4 * KT, 2)
            lo(C_GR + 5)
            for b in range(2):
                dve.wait_ge(sc_mm, b + 1)
                dve.tensor_tensor(g_sm[:, 2 * b:2 * b + 2, :, :].rearrange("p h t k -> p (h t) k"),
                                  ps[:, 4 + b, :].rearrange("p (a k) -> p a k", a=4),
                                  bcast(shp[:, S_GLAM:S_GLAM + P], 4), ALU.mult).then_inc(sm_done, 1)
            def state(h):
                dve.wait_ge(kv_mm, h + 1)
                if h >= 2:
                    dve.wait_ge(go_mm, h - 1)
                kv = (ps[:, 4 + 2 * (h % 2), 0:GDV], ps[:, 5 + 2 * (h % 2), 0:GDV], ps[:, 4 + 2 * (h % 2), GDV:2 * GDV])
                st = g_st[:, h % 2, :, :]
                link(dve.tensor_copy(st[:, 0, :], kv[0]))
                link(dve.scalar_tensor_tensor(st[:, 1, :], st[:, 0, :], el[:, 4 * h + 1:4 * h + 2], kv[1],
                                              ALU.mult, ALU.add))
                dve.scalar_tensor_tensor(st[:, 2, :], st[:, 1, :], el[:, 4 * h + 2:4 * h + 3], kv[2],
                                         ALU.mult, ALU.add).then_inc(st_done, 1)

            steps(4 * KT + 2, 3)
            lo(C_GR + 6)
            state(0)
            state(1)
            steps(4 * KT + 5, 3)
            lo(C_GR + 7)
            for b in range(4):
                dve.wait_ge(*y_written(Y_GR, b))
                half = slice((b % 2) * 512, (b % 2 + 1) * 512)
                dve.tensor_tensor(g_r[:, b // 2, half], ps[:, b, :], row[:, half], ALU.add).then_inc(y_dve, 1)
            for b in range(4):
                dve.wait_ge(silu_done, b + 1)
                g = g_r[:, b // 2, (b % 2) * 512:(b % 2 + 1) * 512].rearrange("p (h k) -> p h k", k=GDV)
                last = dve.tensor_tensor(g, g, bcast(gng[:, :], 2), ALU.mult)
            link(last)
            for h in range(GH_):
                if h + 2 < GH_:
                    state(h + 2)
                dve.wait_ge(grs_done, h + 1)
                for t in range(TT):
                    last = dve.scalar_tensor_tensor(g_o[:, t, h * GDV:(h + 1) * GDV], ps[:, h, t * GDV:(t + 1) * GDV],
                                                    stat[:, 1, 2 * h + t:2 * h + t + 1],
                                                    g_r[:, t, h * GDV:(h + 1) * GDV], ALU.mult, ALU.mult)
                last.then_inc(o_done, 1)
            split_stage(TR_GO, h_lo, h_hi)
            lo(C_GO + 4)
            make_diag(GA_T)
            finish_part(4, 4)
            norm_scale(1, SC_C)
            for c in range(C_GO + 1, C_GO + 3):
                lo(c + 4)
            add_gated(Y_GOUT, 0)
            norm_diag(1)
            norm_split(TR_N1)
            lo(C_GO + 7)

            def mlp(layer, c0, with_ada):
                B = UNITS * layer

                def unit(u, par):
                    dve.wait_ge(relu_done, u + 1)
                    dve.tensor_tensor(m_sq[:, par, :], m_r[:, par, :], m_r[:, par, :], ALU.mult).then_inc(sq_done, 1)
                    dve.wait_ge(sq_done, u + 1)
                    dve.wait_ge(sqh_done, u + 1)
                    dve.tensor_tensor(hid_lo[:, par, :, :].rearrange("p f t -> p (f t)"), m_sq[:, par, :],
                                      hid_hi[:, par, :, :].rearrange("p f t -> p (f t)").bitcast(f32), ALU.subtract)\
                        .then_inc(hid_done, 1)

                unit(B, 0)
                lo(c0 + 4)
                unit(B + 1, 1)
                lo(c0 + 5)
                if layer == 1:
                    finish_part(11, 6)
                lo(c0 + 6)
                with dve.Fori(0, MLP_BODIES) as it:
                    for j in range(MLP_UNROLL):
                        unit(it * MLP_UNROLL + (B + 2 + j), j % 2)
                        for q in range(2):
                            c = c0 + 7 + 2 * j + q
                            lo((c % NSLOT, it * 2 + c // NSLOT))
                            if with_ada and j < 2:
                                for k in (4 * j + 2 * q, 4 * j + 2 * q + 1):
                                    if k == 0:
                                        dve.wait_ge(ada_mm, it + 5)
                                    add_step(it * KT + (5 * KT + k), k,
                                             it * 32 + 16 * ((3 * KT + k) // ADA_RING + 1))
                    if with_ada:
                        dve.wait_ge(ada_mm, it + 6)
                        dve.tensor_tensor(mod[:, bass.ds(it * KT + 5 * KT, KT)], ps[:, 6, 0:KT],
                                          cols[:, bass.ds(it * KT + (COL_ADAB + 5 * KT), KT)], ALU.add)\
                            .then_inc(mod_done, 1)
                c = c0 + 7 + 2 * MLP_UNROLL * MLP_BODIES
                make_diag(6 * layer + GA_C)
                for i in range(2 + MLP_UNROLL * MLP_BODIES, UNITS):
                    unit(B + i, i % 2)
                    lo(c)
                    lo(c + 1)
                    c += 2

            mlp(0, C_M0, True)
            norm_scale(2, 6 + SC_T)
            add_gated(Y_M0, 1)
            norm_diag(2)
            norm_split(TR_N2)
            lo(C_DQ + 3)

            def rotate(q, done):
                v = q[:, :, :].rearrange("p t (g k) -> p t g k", k=DDH)
                x1, x2 = v[:, :, :, 0:8], v[:, :, :, 8:16]

                def each(op, out, a, b):
                    for t in range(TT):
                        last = dve.tensor_tensor(out(t), a(t), b(t), op)
                    return last

                cos = lambda t: bcast(rope[:, 0, t, :], 16)
                sin = lambda t: bcast(rope[:, 1, t, :], 16)
                r = [lambda t, n=n: d_rt[:, n, t, :, :] for n in range(4)]
                a1, a2 = (lambda t: x1[:, t]), (lambda t: x2[:, t])
                each(ALU.mult, r[0], a1, cos)
                each(ALU.mult, r[1], a2, sin)
                each(ALU.mult, r[2], a2, cos)
                link(each(ALU.mult, r[3], a1, sin))
                each(ALU.subtract, a1, r[0], r[1])
                each(ALU.add, a2, r[2], r[3]).then_inc(done, 1)
                dve.wait_ge(done, 1)

            for e in range(3):
                lo(C_DQ + e + 4)
                steps(8 * KT + 2 * e, 2)
            lo(C_DQ + 7)
            steps(8 * KT + 6, 2)
            dve.wait_ge(rope_done, 1)
            dve.wait_ge(*(y_read(Y_DQ, 3)))
            rotate(d_q, rope_q)
            for e in range(4):
                lo(C_DK + e + 4)
                if e == 0:
                    finish_part(8, 4)
                steps(9 * KT + 2 * e, 2)
            dve.wait_ge(*(y_read(Y_DK, 3)))
            rotate(d_k, rope_k)
            for e in range(4):
                lo(C_DV + e + 4)
                if e == 0:
                    finish_part(9, 4)
                steps(10 * KT + 2 * e, 2)

            def d_maxima(h):
                dve.wait_ge(ds_mm, h + 1)
                b, r = d_bank(h), h % 3
                m = d_st[:, r, 0, :].rearrange("p (i t) -> p i t", i=2)
                dve.tensor_reduce(m[:, :, 1], ps[:, b:b + 2, 0:2 * P], AX, ALU.max, negate=True)
                dve.tensor_reduce(m[:, :, 0], ps[:, b:b + 2, 2 * P:3 * P], AX, ALU.max, negate=True).then_inc(ds_max, 1)

            def d_combine(h):
                r, par = h % 3, h % 2
                dve.wait_ge(ds_exp, h + 1)
                link(dve.reciprocal(d_st[:, r, 2, :], d_st[:, r, 1, :]))
                link(dve.tensor_scalar(d_st[:, r, 2, 2:4], d_st[:, r, 2, 2:4], lamc[:, 0:1], None, ALU.mult))
                if h >= 2:
                    dve.wait_ge(dat_mm, h - 1)
                parts = ((1, 0, 2 * P), (0, 2 * P, P))
                for t, a, n in parts:
                    last = dve.tensor_scalar(d_a[:, par, a:a + n], d_p[:, r, 0, a:a + n],
                                             d_st[:, r, 2, t:t + 1], None, ALU.mult)
                link(last)
                for t, a, n in parts:
                    last = dve.scalar_tensor_tensor(d_a[:, par, a:a + n], d_p[:, r, 1, a:a + n],
                                                    d_st[:, r, 2, 2 + t:3 + t], d_a[:, par, a:a + n],
                                                    ALU.mult, ALU.add)
                last.then_inc(da_done, 1)

            def d_transposed(h):
                dve.wait_ge(dat_mm, h + 1)
                if h >= 2:
                    dve.wait_ge(do_mm, h - 1)
                dve.tensor_copy(d_at[:, h % 2, :], ps[:, 1, 0:3 * P]).then_inc(dat_done, 1)

            def d_scale(h):
                dve.wait_ge(drs, h + 1)
                for t in range(TT):
                    o = d_o[:, t, h * DDV:(h + 1) * DDV]
                    last = dve.scalar_tensor_tensor(o, o, stat[:, 1, 2 * h + t:2 * h + t + 1], sub[:, :],
                                                    ALU.mult, ALU.mult)
                last.then_inc(o_done, 1)

            d_maxima(0)
            d_maxima(1)
            d_combine(0)
            d_maxima(2)
            for h in range(DH_):
                d_transposed(h)
                if h + 1 < DH_:
                    d_combine(h + 1)
                if h + 3 < DH_:
                    d_maxima(h + 3)
                if h >= 1:
                    d_scale(h - 1)
            make_diag(6 + GA_T)
            d_scale(DH_ - 1)
            split_stage(TR_DO, h_lo, h_hi)
            lo(C_DO + 4)
            finish_part(10, 4)
            norm_scale(3, 6 + SC_C)
            steps(11 * KT, 3)
            for e in range(1, 3):
                lo(C_DO + e + 4)
                steps(11 * KT + 3 * e, 3 if e == 1 else 2)
            add_gated(Y_DOUT, 2)
            norm_diag(3)
            norm_split(TR_N3)
            lo(C_DO + 7)
            mlp(1, C_M1, False)
            add_gated(Y_M1, 3)
            norm_mean(4)
            dve.wait_ge(rstd_done, 5)
            dve.wait_ge(fg_in, 16)
            for t in range(TT):
                dve.scalar_tensor_tensor(x[:, t, :], x[:, t, :], rstd[:, t:t + 1], acc[:, :], ALU.mult, ALU.mult)\
                    .then_inc(x_done, 1)
            norm_diag(5)
            norm_split(TR_N4)
            lo(C_RQ + 3)

            dve.wait_ge(retc_in, 16)
            for n in range(2 * RH_):
                dst, h = (r_q, n) if n < RH_ else (r_k, n - RH_)
                dve.wait_ge(*multiplied(C_RQ + n))
                src = ps[:, 4 + n % 4, :].rearrange("p (a t) -> p a t", a=2)
                dve.tensor_tensor(r_t[:, 0, :, :], src, bcast(retc[:, 0:T], 2), ALU.mult)
                dve.tensor_tensor(r_t[:, 1, :, :], src, bcast(retc[:, T:2 * T], 2), ALU.mult).then_inc(c_dve, 1)
                dve.wait_ge(c_dve, N_C_RET + n + 1)
                dve.tensor_tensor(dst[:, 2 * h, :], r_t[:, 0, 0, :], r_t[:, 1, 1, :], ALU.subtract)
                dve.tensor_tensor(dst[:, 2 * h + 1, :], r_t[:, 1, 0, :], r_t[:, 0, 1, :], ALU.add)\
                    .then_inc(rqk_done, 1)
                dve.wait_ge(rqk_done, n + 1)
                lo(C_RQ + n + 4)
            for c in range(C_RV, C_RV + 8):
                lo(c + 4)
            for h in range(RH_):
                dve.wait_ge(rs_mm, h + 1)
                dve.tensor_tensor(r_sm[:, h, :], ps[:, 4 + h, 0:3 * P],
                                  retc[:, 2 * T + h * 3 * P:2 * T + (h + 1) * 3 * P], ALU.mult).then_inc(rsm_done, 1)
            for c in range(C_RG, C_RG + 8):
                lo(c + 4)
            for h in range(RH_):
                dve.wait_ge(rrs, h + 1)
                for t in range(TT):
                    k = 2 * h + t
                    g = r_g[:, t, h * RDV:(h + 1) * RDV]
                    dve.scalar_tensor_tensor(g, ps[:, k % 4, :], stat[:, 1, k:k + 1], g, ALU.mult, ALU.mult)\
                        .then_inc(ry, 1)
            split_stage(TR_RA, h_lo, h_hi)
            split_stage(TR_RB, y_lo, y_hi)
            for c in range(C_RO, C_RO + 7):
                lo(c + 4)

            def add_plain(y):
                for b in range(4):
                    dve.wait_ge(*y_written(y, b))
                    half = slice((b % 2) * 512, (b % 2 + 1) * 512)
                    dve.tensor_tensor(x[:, b // 2, half], x[:, b // 2, half], ps[:, b, :], ALU.add).then_inc(x_done, 1)

            add_plain(Y_ROUT)
            norm_diag(6)
            norm_split(TR_N5)
            lo(C_RO + 11)

            def ffn(layer, c0):
                def earlier_taps(g, value):
                    G = GROUPS * layer + g
                    dve.wait_ge(cv_act if value else cg_act, G + 1)
                    for back in (1, 2):
                        for f in range(2):
                            k = COL_CONV + ((layer * 2 + value) * FT + 2 * g + f) * (CONV + 1) + CONV - 1 - back
                            v = f_cv[:, g % 2, value, f, back:T]
                            src = ps[:, 4 + 2 * (g % 2) + value, f * T:(f + 1) * T - back]
                            last = dve.scalar_tensor_tensor(v, src, cols[:, k:k + 1], v, ALU.mult, ALU.add)
                        if back == 1:
                            link(last)
                    last.then_inc(cv_dve if value else cg_dve, 1)

                c = c0 + 4
                for g in range(GROUPS):
                    G = GROUPS * layer + g
                    par = g % 2
                    earlier_taps(g, 0)
                    lo(c)
                    earlier_taps(g, 1)
                    dve.wait_ge(cv_dve, G + 1)
                    dve.wait_ge(fsilu, G + 1)
                    link(dve.tensor_tensor(f_p[:, par, :, :], f_cv[:, par, 0, :, :], f_cv[:, par, 1, :, :], ALU.mult))
                    link(dve.tensor_copy(hid_hi[:, par, :, :], f_p[:, par, :, :]))
                    dve.tensor_tensor(hid_lo[:, par, :, :], f_p[:, par, :, :], hid_hi[:, par, :, :].bitcast(f32),
                                      ALU.subtract).then_inc(hid_done, 1)
                    lo(c + 1)
                    c += 2
                    if g:
                        lo(c)
                        c += 1

            ffn(0, C_F0)
            add_plain(Y_F0)
            norm_diag(7)
            norm_split(TR_N6)
            lo(C_SQ + 3)

            for c in range(C_SQ, C_SQ + 12):
                lo(c + 4)

            def s_soft(p):
                dve.wait_ge(sln, p + 1)
                if p >= 3:
                    dve.wait_ge(e_mm, p - 2)
                dve.scalar_tensor_tensor(s_b[:, p % 3, 1, :, :], ps[:, s_bank(p):s_bank(p) + 2, 0:3 * P], 0.0,
                                         s_b[:, p % 3, 0, :, :], ALU.max, ALU.add).then_inc(spm, 1)

            def s_lo(p):
                dve.wait_ge(so_hi, p + 1)
                dve.tensor_tensor(h_lo[:, p, :], ps[:, so_bank(p), 0:T], h_hi[:, p, :].bitcast(f32), ALU.subtract)\
                    .then_inc(so_lo, 1)

            s_soft(0)
            for p in range(SH_ // 2):
                if p + 1 < SH_ // 2:
                    s_soft(p + 1)
                if p >= 1:
                    s_lo(p - 1)
            s_lo(SH_ // 2 - 1)
            for c in range(C_SO, C_SO + 3):
                lo(c + 4)
            add_plain(Y_SOUT)
            norm_diag(8)
            norm_split(TR_N7)
            lo(C_SO + 7)
            ffn(1, C_F1)
            add_plain(Y_F1)
            norm_mean(9)
            dve.wait_ge(rstd_done, 10)
            dve.wait_ge(fn_in, 16)
            for t in range(TT):
                dve.scalar_tensor_tensor(xn[:, t, :], x[:, t, :], rstd[:, t:t + 1], acc[:, :], ALU.mult, ALU.mult)\
                    .then_inc(fin_done, 1)

        @block.tensor
        def _(pe):
            def chunk_ready(c):
                s, v = slot_visit(c)
                pe.wait_ge(hi_done[s], v + 1)
                pe.wait_ge(lo_done[s], v + 1)
                return s

            def rows(c, lhs_hi, lhs_lo, start, stop, bank_free=None):
                s = chunk_ready(c)

                def step(k, t, n, p):
                    first = start and k == 0 and p == 0
                    if first and bank_free:
                        pe.wait_ge(*bank_free(2 * t + n))
                    lhs = (lhs_hi, lhs_hi, lhs_lo)[p](k, t)
                    w = (w_hi, w_lo, w_hi)[p][:, s, k * D + n * 512:k * D + (n + 1) * 512]
                    return pe.matmul(ps[:, 2 * t + n, :], lhs, w, start=first, stop=stop and k == 1 and p == 2)

                if stop:
                    for t in range(TT):
                        for n in range(2):
                            for k in range(2):
                                for p in range(3):
                                    last = step(k, t, n, p)
                            if 2 * t + n < 3:
                                last.then_inc(y_part, 1)
                else:
                    for k in range(2):
                        for t in range(TT):
                            for p in range(3):
                                for n in range(2):
                                    last = step(k, t, n, p)
                last.then_inc(used[s], 1)

            def h_rows(c, i, n, bank_free=None, hb=h_hi, lb=h_lo, fresh=None):
                kt = 2 * (i % 4)
                if fresh is not None:
                    pe.wait_ge(hl_done, 4 * fresh + i % 4 + 1)
                rows(c, lambda k, t: hb[:, kt + k, t * P:(t + 1) * P], lambda k, t: lb[:, kt + k, t * P:(t + 1) * P],
                     i == 0, i == n - 1, bank_free)

            def cols_chunk(c, bank, fresh=None):
                s = chunk_ready(c)
                for f in range(2):
                    out = ps[:, bank, f * T:(f + 1) * T]
                    for kt in range(KT):
                        if fresh is not None and f == 0 and kt % 2 == 0:
                            pe.wait_ge(hl_done, 4 * fresh + kt // 2 + 1)
                        first = kt * T + f * P
                        wh, wl = w_hi[:, s, first:first + P], w_lo[:, s, first:first + P]
                        pe.matmul(out, wh, h_hi[:, kt, :], start=kt == 0, stop=False)
                        pe.matmul(out, wh, h_lo[:, kt, :], start=False, stop=False)
                        last = pe.matmul(out, wl, h_hi[:, kt, :], start=False, stop=kt == KT - 1)
                last.then_inc(used[s], 1)

            def transposes(stage, src, ready):
                for b in range(4):
                    pe.wait_ge(*ready(b))
                    if stage == TR_RB:
                        pe.wait_ge(hl_done, 4 * TR_RA + b + 1)
                    for j in range(2):
                        for t in range(TT):
                            kt = 2 * b + j
                            last = pe.transpose(ps[:, 4 + b, j * T + t * P:j * T + (t + 1) * P],
                                                src[:, t, kt * P:(kt + 1) * P], ident)
                    last.then_inc(tr_done, 1)

            def norm(n):
                pe.wait_ge(nd_done, n + 1)
                for b in range(4):
                    for j in range(2):
                        for t in range(TT):
                            kt = 2 * b + j
                            last = pe.matmul(ps[:, 4 + b, j * T + t * P:j * T + (t + 1) * P],
                                             x[:, t, kt * P:(kt + 1) * P], nd[:, t, :], start=True, stop=True)
                    last.then_inc(tr_done, 1)

            def sum_part(p, bank):
                pe.wait_ge(ada_step, (p + 1) * KT)
                if p:
                    pe.wait_ge(mod_done, p)
                for j in range(KT):
                    last = pe.matmul(ps[:, bank, j:j + 1], acc[:, j * P:(j + 1) * P], shp[:, S_ONE:S_ONE + 1],
                                     start=True, stop=True)
                last.then_inc(ada_mm, 1)

            def gate(g):
                pe.wait_ge(diag_done, g + 1)
                for j in range(2):
                    last = pe.matmul(ps[:, 6 + j, :], shp[:, S_NO:S_NO + P],
                                     diag[:, 4 * j:4 * j + 4, :].rearrange("p k n -> p (k n)"), start=True, stop=True)
                last.then_inc(gate_mm, 1)

            pe.wait_ge(shp_in, 16)
            pe.wait_ge(mask_done, 1)
            norm(0)
            sum_part(0, 0)
            sum_part(1, 0)

            pe.wait_ge(wal_done, 1)
            wa = lambda w, kt: w[:, kt * GRANK:(kt + 1) * GRANK]
            for kt in range(KT):
                out = ps[0:GRANK, 4, 0:T]
                if kt % 2 == 0:
                    pe.wait_ge(hl_done, 4 * TR_N0 + kt // 2 + 1)
                pe.matmul(out, wa(g_wah, kt), h_hi[:, kt, :], start=kt == 0, stop=False)
                pe.matmul(out, wa(g_wah, kt), h_lo[:, kt, :], start=False, stop=False)
                last = pe.matmul(out, wa(g_wal, kt), h_hi[:, kt, :], start=False, stop=kt == KT - 1)
            last.then_inc(a_mm, 1)
            h_rows(C_GV, 0, 4, lambda b: (mod_done, 2))
            pe.wait_ge(a_done, 1)
            for h in range(GH_):
                last = pe.matmul(ps[:, 6 + h // 2, (h % 2) * T:(h % 2 + 1) * T], g_w2[0:GRANK, h * GDK:(h + 1) * GDK],
                                 g_a[0:GRANK, :], start=True, stop=True)
            last.then_inc(z_mm, 1)
            for i in range(1, 4):
                h_rows(C_GV + i, i, 4)
            for n in range(2):
                cols_chunk(C_GQ + n, 4 + n)
                if n == 0:
                    pe.wait_ge(z_done, 1)
                    sum_part(2, 6)
            for n in range(2):
                pe.wait_ge(c_dve, n + 1)
                cols_chunk(C_GK + n, 4 + n)
            h_rows(C_GR, 0, 4, lambda b: y_read(Y_GV, b))
            sum_part(3, 6)
            h_rows(C_GR + 1, 1, 4)
            pe.wait_ge(c_dve, 4)
            pe.wait_ge(mod_done, 4)
            for b in range(2):
                for h in (2 * b, 2 * b + 1):
                    for t in range(TT):
                        for c in range(2):
                            o = ((h % 2) * 2 + t) * P + c * GCH
                            last = pe.matmul(ps[:, 4 + b, o:o + GCH], g_ki[:, h, t * P:(t + 1) * P],
                                             g_q[:, h, t, c, c * GCH:(c + 1) * GCH], start=True, stop=True)
                last.then_inc(sc_mm, 1)
            for b in range(2):
                for h in (2 * b, 2 * b + 1):
                    for t in range(TT):
                        o = ((h % 2) * 2 + t) * P
                        last = pe.transpose(ps[:, 6 + b, o:o + P], g_ks[:, h, t * P:(t + 1) * P], ident)
                last.then_inc(kt_mm, 1)
            h_rows(C_GR + 2, 2, 4)

            def chunk_states(h):
                if h < 2:
                    pe.wait_ge(sm_done, 2)
                    pe.wait_ge(kst_done, 2)
                    pe.wait_ge(*y_read(Y_GV, 3))
                else:
                    pe.wait_ge(st_done, h - 1)
                b = 4 + 2 * (h % 2)
                for c, out in enumerate((ps[:, b, 0:GDV], ps[:, b + 1, 0:GDV], ps[:, b, GDV:2 * GDV])):
                    part = slice((c % 2) * GCH, (c % 2 + 1) * GCH)
                    last = pe.matmul(out, g_kst[part, h, c // 2, :], g_v[part, c // 2, h * GDV:(h + 1) * GDV],
                                     start=True, stop=True)
                last.then_inc(kv_mm, 1)

            def g_output(h):
                pe.wait_ge(st_done, h + 1)
                pe.wait_ge(*y_read(Y_GR, h))
                v = lambda t: g_v[:, t, h * GDV:(h + 1) * GDV]
                o0, o1 = ps[:, h, 0:GDV], ps[:, h, GDV:2 * GDV]
                pe.matmul(o0, g_sm[:, h, 0, :], v(0), start=True, stop=False)
                pe.matmul(o0, g_q[:, h, 0, 1, :], g_st[:, h % 2, 0, :], start=False, stop=True)
                pe.matmul(o1, g_sm[:, h, 1, :], v(1), start=True, stop=False)
                pe.matmul(o1, g_q[:, h, 1, 0, :], g_st[:, h % 2, 1, :], start=False, stop=False)
                pe.matmul(o1, g_q[:, h, 1, 1, :], g_st[:, h % 2, 2, :], start=False, stop=True).then_inc(go_mm, 1)

            chunk_states(0)
            chunk_states(1)
            h_rows(C_GR + 3, 3, 4)
            for h in range(GH_):
                g_output(h)
                if h + 2 < GH_:
                    chunk_states(h + 2)
            transposes(TR_GO, g_o, lambda b: (o_done, b + 1))
            h_rows(C_GO, 0, 4, fresh=TR_GO)
            sum_part(4, 4)
            h_rows(C_GO + 1, 1, 4, fresh=TR_GO)
            h_rows(C_GO + 2, 2, 4, fresh=TR_GO)
            pe.wait_ge(hl_done, 4 * (TR_GO + 1))
            gate(0)
            h_rows(C_GO + 3, 3, 4)
            norm(1)

            def mlp(layer, c0, with_ada, stage):
                B = UNITS * layer

                def up(u, par, c, later, fresh=None):
                    if later:
                        pe.wait_ge(relu_done, u - 1)
                    cols_chunk(c, 4 + par, fresh)

                def down(u, par, c, start, stop):
                    pe.wait_ge(hid_done, u + 1)
                    rows(c, lambda k, t: hid_hi[:, par, k, t * P:(t + 1) * P],
                         lambda k, t: hid_lo[:, par, k, t * P:(t + 1) * P], start, stop)

                up(B, 0, c0, False, stage)
                up(B + 1, 1, c0 + 1, False)
                if layer == 1:
                    sum_part(11, 6)
                down(B, 0, c0 + 2, True, False)
                with pe.Fori(0, MLP_BODIES) as it:
                    for j in range(MLP_UNROLL):
                        u = it * MLP_UNROLL + (B + 2 + j)
                        c = c0 + 3 + 2 * j
                        up(u, j % 2, (c % NSLOT, it * 2 + c // NSLOT), True)
                        if with_ada and j == MLP_UNROLL - 1:
                            pe.wait_ge(ada_step, it * KT + 6 * KT)
                            pe.wait_ge(mod_done, it + 5)
                            for k in range(KT):
                                last = pe.matmul(ps[:, 6, k:k + 1], acc[:, k * P:(k + 1) * P],
                                                 shp[:, S_ONE:S_ONE + 1], start=True, stop=True)
                            last.then_inc(ada_mm, 1)
                        down(u + (-1), (j + 1) % 2, ((c + 1) % NSLOT, it * 2 + (c + 1) // NSLOT), False, False)
                c = c0 + 3 + 2 * MLP_UNROLL * MLP_BODIES
                for i in range(2 + MLP_UNROLL * MLP_BODIES, UNITS):
                    up(B + i, i % 2, c, True)
                    if i == UNITS - 1:
                        gate(2 * layer + 1)
                    down(B + i - 1, (i - 1) % 2, c + 1, False, False)
                    c += 2
                down(B + UNITS - 1, (UNITS - 1) % 2, c, False, True)

            mlp(0, C_M0, True, TR_N1)
            norm(2)

            def d_transposes(src, n):
                for b in range(4):
                    if n:
                        pe.wait_ge(dtr_act, b + 1)
                    for j in range(2):
                        for t in range(TT):
                            kt = 2 * b + j
                            last = pe.transpose(ps[:, 4 + b, j * T + t * P:j * T + (t + 1) * P],
                                                src[:, t, kt * P:(kt + 1) * P], ident)
                    last.then_inc(dtr, 1)

            for i in range(4):
                h_rows(C_DQ + i, i, 4, fresh=TR_N2)
            for i in range(4):
                h_rows(C_DK + i, i, 4, lambda b: y_read(Y_DQ, b))
                if i == 0:
                    sum_part(8, 4)
            pe.wait_ge(rope_q, 1)
            pe.wait_ge(mod_done, 9)
            d_transposes(d_q, 0)
            h_rows(C_DV, 0, 4, lambda b: y_read(Y_DK, b))
            pe.wait_ge(dtr_act, 1)
            sum_part(9, 4)
            h_rows(C_DV + 1, 1, 4)
            pe.wait_ge(rope_k, 1)
            pe.wait_ge(mod_done, 10)
            d_transposes(d_k, 4)
            h_rows(C_DV + 2, 2, 4)
            h_rows(C_DV + 3, 3, 4)

            def d_scores(h):
                if h >= 3:
                    pe.wait_ge(ds_exp, h - 2)
                for i in range(2):
                    f, b = slice(i * DDH, (i + 1) * DDH), d_bank(h) + i
                    pe.matmul(ps[:, b, 0:T], d_qt[f, h, P:T], d_kt[f, h, :], start=True, stop=True)
                    pe.matmul(ps[:, b, T:T + P], d_qt[f, h, 0:P], d_kt[f, h, 0:P], start=False, stop=True,
                              skip_group_check=True)
                    last = pe.matmul(ps[:, b, P:3 * P], maskr[:, 0:P], maskr[:, P:3 * P], start=False, stop=True,
                                     skip_group_check=True)
                last.then_inc(ds_mm, 1)

            pe.wait_ge(dtr_act, 8)
            pe.wait_ge(*y_read(Y_DV, 3))
            for h in range(3):
                d_scores(h)
            for h in range(DH_):
                par = h % 2
                pe.wait_ge(da_done, h + 1)
                if h:
                    pe.wait_ge(dat_done, h)
                for j in range(3):
                    last = pe.transpose(ps[:, 1, j * P:(j + 1) * P], d_a[:, par, j * P:(j + 1) * P], ident)
                last.then_inc(dat_mm, 1)
                if h + 3 < DH_:
                    d_scores(h + 3)
                pe.wait_ge(dat_done, h + 1)
                if h:
                    pe.wait_ge(do_act, h)
                v = lambda t: d_v[:, t, h * DDV:(h + 1) * DDV]
                o = lambda t: ps[:, 0, par * T + t * P:par * T + (t + 1) * P]
                pe.matmul(o(1), d_at[:, par, 0:P], v(0), start=True, stop=False)
                pe.matmul(o(1), d_at[:, par, P:2 * P], v(1), start=False, stop=True)
                pe.matmul(o(0), d_at[:, par, 2 * P:3 * P], v(0), start=True, stop=True).then_inc(do_mm, 1)
            transposes(TR_DO, d_o, lambda b: (o_done, GH_ + 2 * b + 2))
            h_rows(C_DO, 0, 4, fresh=TR_DO)
            sum_part(10, 4)
            h_rows(C_DO + 1, 1, 4, fresh=TR_DO)
            h_rows(C_DO + 2, 2, 4, fresh=TR_DO)
            pe.wait_ge(hl_done, 4 * (TR_DO + 1))
            gate(2)
            h_rows(C_DO + 3, 3, 4)
            norm(3)
            mlp(1, C_M1, False, TR_N3)
            norm(4)

            for n in range(2 * RH_):
                if n >= 4:
                    pe.wait_ge(c_dve, N_C_RET + n - 3)
                cols_chunk(C_RQ + n, 4 + n % 4, None if n else TR_N4)
            for i in range(4):
                h_rows(C_RV + i, i, 4)
            for i in range(4):
                h_rows(C_RV + 4 + i, i, 4, lambda b: y_read(Y_RV0, b))
            pe.wait_ge(rqk_done, 2 * RH_)
            for h in range(RH_):
                for first, keys, queries in ((0, slice(0, P), slice(0, T)), (T, slice(P, T), slice(P, T))):
                    n = queries.stop - queries.start
                    for kk in range(2):
                        last = pe.matmul(ps[:, 4 + h, first:first + n], r_k[:, 2 * h + kk, keys],
                                         r_q[:, 2 * h + kk, queries], start=kk == 0, stop=kk == 1)
                last.then_inc(rs_mm, 1)
            for i in range(4):
                h_rows(C_RG + i, i, 4, lambda b: y_read(Y_RV1, b))
            for i in range(4):
                h_rows(C_RG + 4 + i, i, 4, lambda b: y_read(Y_RG0, b))
            for h in range(RH_):
                pe.wait_ge(rsm_done, h + 1)
                v = lambda t: r_v[:, t, h * RDV:(h + 1) * RDV]
                for t in range(TT):
                    k = 2 * h + t
                    if k < 4:
                        pe.wait_ge(*y_read(Y_RG1, k))
                    else:
                        pe.wait_ge(ry, k - 3)
                    pe.matmul(ps[:, k % 4, :], r_sm[:, h, t * P:(t + 1) * P], v(0), start=True, stop=t == 0)\
                        if t else pe.matmul(ps[:, k % 4, :], r_sm[:, h, 0:P], v(0), start=True, stop=True)\
                        .then_inc(ro_mm, 1)
                    if t:
                        pe.matmul(ps[:, k % 4, :], r_sm[:, h, 2 * P:3 * P], v(1), start=False, stop=True)\
                            .then_inc(ro_mm, 1)
            transposes(TR_RA, r_g[:, :, 0:D], lambda b: (ry, 2 * (b // 2) + 2))
            transposes(TR_RB, r_g[:, :, D:2 * D], lambda b: (ry, 2 * (b // 2) + 6))
            for i in range(4):
                h_rows(C_RO + i, i, 8, fresh=TR_RA)
            for i in range(4, 8):
                h_rows(C_RO + i, i, 8, None, y_hi, y_lo, fresh=TR_RB)
            norm(5)

            def ffn(layer, c0, stage):
                B = GROUPS * layer

                def up(g, value):
                    if g >= 2:
                        pe.wait_ge(cv_dve if value else cg_dve, B + g - 1)
                    cols_chunk(ffn_chunk(c0, g, value), 4 + 2 * (g % 2) + value, None if g or value else stage)

                def down(g):
                    pe.wait_ge(hid_done, 2 * UNITS + B + g + 1)
                    rows(ffn_chunk(c0, g, 2), lambda k, t: hid_hi[:, g % 2, k, t * P:(t + 1) * P],
                         lambda k, t: hid_lo[:, g % 2, k, t * P:(t + 1) * P], g == 0, g == GROUPS - 1)

                for g in range(GROUPS):
                    up(g, 0)
                    up(g, 1)
                    if g:
                        down(g - 1)
                down(GROUPS - 1)

            ffn(0, C_F0, TR_N5)
            norm(6)

            for n in range(8):
                if n >= 4:
                    pe.wait_ge(c_act, n - 3)
                cols_chunk(C_SQ + n, 4 + n % 4, None if n else TR_N6)
            for i in range(4):
                h_rows(C_SV + i, i, 4)

            def s_scores(p):
                if p >= 3:
                    pe.wait_ge(sexp, p - 2)
                for i in range(2):
                    f, b = slice(i * SDH, (i + 1) * SDH), s_bank(p) + i
                    pe.matmul(ps[:, b, 0:T], s_k[f, p, 0:P], s_q[f, p, :], start=True, stop=True)
                    pe.matmul(ps[:, b, T:T + P], s_k[f, p, P:T], s_q[f, p, P:T], start=False, stop=True,
                              skip_group_check=True)
                    for first in (0, T):
                        last = pe.matmul(ps[:, b, first:first + P], maskr[:, 0:P], maskr[:, 3 * P:4 * P],
                                         start=False, stop=True, skip_group_check=True)
                last.then_inc(z_ready, 1)

            def s_weights(p):
                pe.wait_ge(spm, p + 1)
                for i in range(2):
                    sums, b = s_b[:, p % 3, 1, i, :], s_bank(p) + i
                    pe.matmul(ps[:, b, 0:3 * P], shp[:, S_NU:S_NU + P], sums, start=False, stop=True,
                              skip_group_check=True)
                    last = pe.matmul(ps[:, b, P:2 * P], shp[:, S_NO:S_NO + P], sums[:, 2 * P:3 * P], start=False,
                                     stop=True, skip_group_check=True)
                last.then_inc(e_mm, 1)

            def s_output(p):
                pe.wait_ge(sexp, p + 1)
                if p >= 2:
                    pe.wait_ge(so_lo, p - 1)
                for i in range(2):
                    f, h = slice(i * SDH, (i + 1) * SDH), 2 * p + i
                    a = s_b[:, p % 3, 0, i, :]
                    pe.matmul(ps[f, so_bank(p), 0:T], s_v[:, 0, h * SDH:(h + 1) * SDH], a[:, 0:T], start=True, stop=False)
                    last = pe.matmul(ps[f, so_bank(p), P:T], s_v[:, 1, h * SDH:(h + 1) * SDH], a[:, T:T + P],
                                     start=False, stop=True)
                last.then_inc(so_mm, 1)

            pe.wait_ge(c_act, 8)
            pe.wait_ge(*y_read(Y_SV, 3))
            for p in range(3):
                s_scores(p)
            s_weights(0)
            for p in range(SH_ // 2):
                if p + 1 < SH_ // 2:
                    s_weights(p + 1)
                s_output(p)
                if p + 3 < SH_ // 2:
                    s_scores(p + 3)
            pe.wait_ge(so_lo, 6)
            for i in range(4):
                pe.wait_ge(so_lo, 2 * i + 2)
                h_rows(C_SO + i, i, 4)
            norm(7)
            ffn(1, C_F1, TR_N7)


def shape_constants():
    shp = np.zeros((P, NSHP), np.float32)
    r, c = np.arange(P)[:, None], np.arange(P)[None, :]
    shp[:, S_ID:S_ID + P] = r == c
    shp[:, S_GLAM:S_GLAM + P] = (r <= c) & (r // GCH == c // GCH)
    shp[:, S_SCAN:S_SCAN + T] = np.arange(T) % GCH != 0
    shp[:, S_CAUS:S_CAUS + 2 * P] = np.tile(np.where(c <= r, 0.0, NEG), 2)
    shp[:, S_SBM:S_SBM + P] = np.where(r < c, 0.0, NEG)
    shp[:, S_NU:S_NU + P] = np.where(r >= c, -1.0, 0.0)
    shp[:, S_NO:S_NO + P] = -1.0
    shp[:, S_INVF:S_INVF + 8] = np.float32(ROPE_THETA) ** (-np.arange(0, ROPE_DIM, 2, dtype=np.float32) / ROPE_DIM)
    shp[:, S_ONE] = 1.0
    shp[:, S_HALF:S_HALF + 8] = -0.5
    retc = np.zeros((P, NRETC), np.float32)
    inv = np.float32(10000.0) ** (-np.arange(0, RDK, 2, dtype=np.float32) / RDK)
    angle = np.arange(T, dtype=np.float32)[None, :] * inv[:, None]
    retc[:, 0:T], retc[:, T:2 * T] = np.cos(angle), np.sin(angle)
    log_g = np.log(1.0 - 2.0 ** (-5.0 - np.arange(RH_)))
    for h in range(RH_):
        d = retc[:, 2 * T + h * 3 * P:2 * T + (h + 1) * 3 * P]
        now = np.where(c >= r, np.exp(np.maximum(c - r, 0) * log_g[h]), 0.0)
        d[:, 0:P] = now
        d[:, P:2 * P] = np.exp((c + P - r) * log_g[h])
        d[:, 2 * P:3 * P] = now
    retc[:, 2 * T:] *= RDK ** -0.5
    return shp, retc


def stream(inputs):
    def cols(w, first, n):
        w = w[:, first:first + n].reshape(KT, P, n // 256, 256)
        return list(w.transpose(2, 1, 0, 3).reshape(n // 256, P, CHUNK))

    def rows(w, first=0, n=D):
        w = w[:, first:first + n]
        k = w.shape[0] // 256
        return list(w.reshape(k, 2, P, n).transpose(0, 2, 1, 3).reshape(k, P, CHUNK))

    out = []
    g = inputs["gla_w_in"][0]
    hk = GH_ * GDK
    out += rows(g, 2 * hk) + cols(g, 0, hk) + cols(g, hk, hk) + rows(g, 2 * hk + D) + rows(inputs["gla_w_o"][0])

    def mlp(layer):
        up, down = cols(inputs["mlp_w1"][layer], 0, F_MLP), rows(inputs["mlp_w2"][layer])
        res = [up[0]]
        for i in range(1, UNITS):
            res += [up[i], down[i - 1]]
        return res + [down[-1]]

    out += mlp(0)
    d = inputs["diff_w_in"][0]
    out += rows(d, 0) + rows(d, D) + rows(d, 2 * D) + rows(inputs["diff_w_o"][0])
    out += mlp(1)
    r = inputs["ret_w_in_2"][0]
    qk = RH_ * RDK
    out += cols(r, 0, qk) + cols(r, qk, qk)
    for n in range(4):
        out += rows(r, 2 * qk + n * D)
    out += rows(inputs["ret_w_out_2"][0])

    def ffn(layer):
        w = inputs["ffn_w_up_2"][layer]
        gate, value, down = cols(w, 0, F_FFN), cols(w, F_FFN, F_FFN), rows(inputs["ffn_w_down_2"][layer])
        res = [gate[0], value[0]]
        for i in range(1, GROUPS):
            res += [gate[i], value[i], down[i - 1]]
        return res + [down[-1]]

    out += ffn(0)
    s = inputs["sb_w_in_2"][0]
    out += cols(s, 0, D) + cols(s, D, D) + rows(s, 2 * D) + rows(inputs["sb_w_out_2"][0])
    out += ffn(1)
    assert len(out) == NCHUNK
    return np.concatenate(out, axis=0)


def kernel(**inputs):
    import concourse.bacc as bacc
    from concourse.bass_utils import run_bass_kernel_spmd as run

    a = {k: np.asarray(v) for k, v in inputs.items()}
    per_feature = lambda v: v.reshape(-1, P).T
    on_all = lambda v: np.broadcast_to(v.reshape(1, -1), (P, v.size))
    conv = np.concatenate([a["ffn_conv_w_2"], a["ffn_conv_b_2"][:, None, :]], axis=1)
    conv = conv.reshape(DEPTH, CONV + 1, 2 * FT, P).transpose(3, 0, 2, 1).reshape(P, -1)
    cols = np.concatenate([per_feature(a[n]) for n in ("c", "ada_b", "norm_g", "ret_norm_2", "ffn_norm_2", "sb_norm_2",
                                                        "gla_b_a")] + [conv], axis=1)
    assert cols.shape == (P, NCOL)
    ada_w = a["ada_w"].reshape(DEPTH, D, 6, D).transpose(0, 2, 1, 3).reshape(ADA_PARTS * D, D)
    shp, retc = shape_constants()
    w_in = a["gla_w_in"][0]
    arrays = {
        "x": a["x"].reshape(TT, P, D).transpose(1, 0, 2),
        "positions": a["positions"].reshape(TT, P).T,
        "stream": stream(a),
        "ada_w": ada_w,
        "cols": cols,
        "shp": shp,
        "retc": retc,
        "w_a": w_in[:, w_in.shape[1] - GRANK:].reshape(KT, P, GRANK).transpose(1, 0, 2).reshape(P, KT * GRANK),
        "w_a2": a["gla_w_a2"][0],
        "b_r": on_all(a["gla_b_r"]),
        "gla_norm": on_all(a["gla_norm_g"]),
        "lam": on_all(a["diff_lambda"]),
        "subln": on_all(a["diff_subln_g"]),
        "final_g": on_all(a["final_g"]),
        "final_norm": on_all(a["final_norm_2"]),
    }
    nc = bacc.Bacc("TRN2", target_bir_lowering=False, num_devices=1)
    arrays = {f"in_{k}": np.ascontiguousarray(v) for k, v in arrays.items()}
    args = [nc.dram_tensor(k, v.shape, mybir.dt.from_np(v.dtype), kind="ExternalInput").ap() for k, v in arrays.items()]
    out = nc.dram_tensor("out", (T, D), mybir.dt.float32, kind="ExternalOutput").ap()
    build(nc, *args, out)
    r = run(nc, [arrays], core_ids=[0])
    return r.results[0]["out"].reshape(1, T, D)
```

```python
import math

import numpy as np
import concourse.bass as bass
from concourse import mybir
from contextlib import ExitStack

P = 128
T = 256
TT = T // P
D = 1024
KT = D // P
DEPTH = 2
F_MLP = 4 * D
EPS = 1e-6
GH_, GDK, GDV, GCH = 4, 128, 256, 64
GRANK, GTAU = 16, 16.0
DH_, DDH, DDV = 8, 64, 128
ROPE_DIM, ROPE_THETA = 16, 500000.0
RH_, RDK, RDV = 4, 256, 512
SH_, SDH = 16, 64
F_FFN = 2816
FT = F_FFN // P
CONV = 3
NSLOT = 4
CHUNK = 2048
LAMBDA_INIT = 0.8 - 0.6 * math.exp(-0.3)
NEG = -2.0 ** 100
ROUND = 1.5 * 2.0 ** 23
TURN = (6.28125, 0.0019350051879882812, 3.0199159819e-07)
PI32 = 3.1415925

UNITS = F_MLP // 256
MLP_UNROLL, MLP_BODIES = 4, 3
GROUPS = FT // 2
C_GV, C_GQ, C_GK, C_GR, C_GO = 0, 4, 6, 8, 12
C_M0 = 16
C_DQ = C_M0 + 2 * UNITS
C_DK, C_DV, C_DO = C_DQ + 4, C_DQ + 8, C_DQ + 12
C_M1 = C_DQ + 16
C_RQ = C_M1 + 2 * UNITS
C_RK, C_RV, C_RG, C_RO = C_RQ + 4, C_RQ + 8, C_RQ + 16, C_RQ + 24
C_F0 = C_RQ + 32
C_SQ = C_F0 + 3 * GROUPS
C_SK, C_SV, C_SO = C_SQ + 4, C_SQ + 8, C_SQ + 12
C_F1 = C_SQ + 16
NCHUNK = C_F1 + 3 * GROUPS

SH_T, SC_T, SH_C, SC_C, GA_T, GA_C = range(6)
PART_OF = [0, 1, 3, 4, 2, 5]
ROW_GATES = (GA_T, 6 + GA_T, 6 + GA_C)
ADA_PARTS = 6 * DEPTH
ADA_STEPS = ADA_PARTS * KT
ADA_RING = 4

COL_C = 0
COL_ADAB = COL_C + KT
COL_NORM = COL_ADAB + ADA_PARTS * KT
COL_RET = COL_NORM + 4 * KT
COL_FFN = COL_RET + KT
COL_SB = COL_FFN + 2 * KT
COL_BA = COL_SB + KT
COL_CONV = COL_BA + GH_
NCOL = COL_CONV + 2 * 2 * FT * (CONV + 1)

S_ID = 0
S_GLAM = S_ID + P
S_SCAN = S_GLAM + P
S_CAUS = S_SCAN + T
S_SBM = S_CAUS + 2 * P
S_NU = S_SBM + P
S_NO = S_NU + P
S_INVF = S_NO + P
S_ONE = S_INVF + ROPE_DIM // 2
S_HALF = S_ONE + 1
NSHP = S_HALF + 8
NRETC = 2 * T + RH_ * 3 * P


class Count:

    def __init__(self, sem):
        self.sem, self.n = sem, 0

    def inc(self, instruction):
        instruction.then_inc(self.sem, 1)
        self.n = self.n + 1
        return self.n


def build(nc, x_d, pos_d, stream_d, ada_d, cols_d, shp_d, retc_d, wa_d, wa2_d, br_d, gng_d, lam_d, sub_d,
          gate_d, fg_d, fn_d, out_d):
    f32, f32r, i32 = mybir.dt.float32, mybir.dt.float32r, mybir.dt.int32
    ALU = mybir.AluOpType
    ACT = mybir.ActivationFunctionType
    AX = mybir.AxisListType.X

    ctx = ExitStack()
    with ctx:
        def sb(name, shape, dt=f32):
            return ctx.enter_context(nc.sbuf_tensor(name, shape, dt))

        def sem(name):
            return ctx.enter_context(nc.semaphore(name))

        raw = sb("raw", [P, NSLOT, CHUNK])
        w_hi = sb("w_hi", [P, NSLOT, CHUNK], f32r)
        w_lo = sb("w_lo", [P, NSLOT, CHUNK], f32r)
        x = sb("x", [P, TT, D])
        h_hi = sb("h_hi", [P, KT, T], f32r)
        h_lo = sb("h_lo", [P, KT, T], f32r)
        row = sb("row", [P, D])
        acc = sb("acc", [P, D])
        ada_offset = nc.sbuf_base
        ada = sb("ada", [P, ADA_RING, D])
        cols = sb("cols", [P, NCOL])
        shp = sb("shp", [P, NSHP])
        mod = sb("mod", [P, ADA_PARTS * KT])
        gsc = sb("gsc", [P, 4 * KT])
        csil = sb("csil", [P, KT])
        maskr = sb("maskr", [P, 4 * P], f32r)
        gng = sb("gng", [P, GDV])
        sub = sb("sub", [P, DDV])
        lamc = sb("lamc", [P, 4])
        rope = sb("rope", [P, 2, TT, ROPE_DIM // 2])
        posi = sb("posi", [P, TT], i32)
        ssq = sb("ssq", [P, 16])
        rstd = sb("rstd", [P, 16])
        el = sb("el", [P, GH_ * 4])
        stat = sb("stat", [P, 2, 16])

        arena_offset = nc.sbuf_base
        arena = sb("arena", [P, 12 * 1024])
        A0 = arena_offset

        def at(name, word, shape, dt=f32):
            return nc.alloc_sbuf_tensor_at(name, [P, *shape], dt, offset=A0 + 4 * word)

        xn = at("xn", 0, [TT, D])
        h32 = at("h32", 2048, [KT, T])
        nd = at("nd", 4096, [TT, P])
        sq_out = at("sq_out", 4352, [TT, D])
        g_eb = at("g_eb", 0, [GH_, T])
        g_en = at("g_en", 1024, [GH_, T])
        g_es = at("g_es", 2048, [GH_, T])
        g_q = at("g_q", 3072, [GH_, TT, 2, P])
        g_ki = at("g_ki", 5120, [GH_, T])
        g_ks = at("g_ks", 6144, [GH_, T])
        g_w2 = at("g_w2", 6144, [GH_ * GDK])
        g_a = at("g_a", 6656, [T])
        g_wa = at("g_wa", 5120, [KT * GRANK])
        g_wah = at("g_wah", 5248, [KT * GRANK], f32r)
        g_wal = at("g_wal", 5376, [KT * GRANK], f32r)
        srow = at("srow", 7168, [D])
        g_v = at("g_v", 7168, [TT, D])
        g_r = at("g_r", 9216, [TT, D])
        g_z = at("g_z", 9216, [GH_, T])
        g_t = at("g_t", 10240, [GH_, T])
        g_b = at("g_b", 11264, [GH_, T])
        g_kst = at("g_kst", 11264, [GH_, TT, P])
        g_sm = at("g_sm", 0, [GH_, TT, P])
        g_st = at("g_st", 1024, [2, 3, GDV])
        g_o = at("g_o", 5120, [TT, D])
        m_r = at("m_r", 4096, [2, 512])
        m_sq = at("m_sq", 5120, [2, 512])
        hid_hi = at("hid_hi", 7168, [2, 2, T], f32r)
        hid_lo = at("hid_lo", 8192, [2, 2, T], f32r)
        f_cv = at("f_cv", 4096, [2, 2, 2, T])
        f_p = at("f_p", 6144, [2, 2, T])
        diag = at("diag", 9216, [KT, P])
        d_q = at("d_q", 0, [TT, D])
        d_k = at("d_k", 2048, [TT, D])
        d_v = at("d_v", 4096, [TT, D])
        d_qt = at("d_qt", 6144, [KT, T])
        d_kt = at("d_kt", 8192, [KT, T])
        d_rt = at("d_rt", 10240, [4, TT, 16, 8])
        d_p = at("d_p", 0, [3, 2, 3 * P])
        d_a = at("d_a", 2304, [2, 3 * P])
        d_at = at("d_at", 3072, [2, 3 * P])
        d_st = at("d_st", 3840, [3, 3, 4])
        d_o = at("d_o", 10240, [TT, D])
        lamv = at("lamv", 10240, [256])
        lamp = at("lamp", 10496, [2, 64])
        ang = at("ang", 10752, [4, TT, 8])
        r_q = at("r_q", 0, [KT, T])
        r_k = at("r_k", 2048, [KT, T])
        r_v = at("r_v", 4096, [TT, RH_ * RDV])
        r_g = at("r_g", 8192, [TT, RH_ * RDV])
        y_hi = at("y_hi", 0, [KT, T], f32r)
        y_lo = at("y_lo", 2048, [KT, T], f32r)
        A1 = ada_offset

        def in_ada(name, word, shape):
            return nc.alloc_sbuf_tensor_at(name, [P, *shape], f32, offset=A1 + 4 * word)

        retc = in_ada("retc", 0, [NRETC])
        r_t = in_ada("r_t", NRETC, [2, 2, T])
        r_sm = in_ada("r_sm", NRETC, [RH_, 3 * P])
        r_sq = in_ada("r_sq", NRETC + RH_ * 3 * P, [RDV])
        s_q = at("s_q", 0, [KT, T])
        s_k = at("s_k", 2048, [KT, T])
        s_v = at("s_v", 4096, [TT, D])
        s_b = at("s_b", 6144, [3, 2, 2, 3 * P])

        ps = ctx.enter_context(nc.psum_tensor("ps", [P, 8, 512], f32))
        ident = shp[:, S_ID:S_ID + P]

        raw_in = [sem(f"raw_in{i}") for i in range(NSLOT)]
        hi_done = [sem(f"hi_done{i}") for i in range(NSLOT)]
        lo_done = [sem(f"lo_done{i}") for i in range(NSLOT)]
        used = [sem(f"used{i}") for i in range(NSLOT)]
        ada_in = [sem(f"ada_in{i}") for i in range(ADA_RING)]
        early_in = [sem(f"early_in{i}") for i in range(2 * NSLOT)]
        ada_more = [sem(f"ada_more{i}") for i in range(ADA_RING)]
        ada_half = sem("ada_half")
        ada_step = sem("ada_step")
        ada_pe = sem("ada_pe")
        srow_done = sem("srow_done")
        ada_mm = sem("ada_mm")
        mod_done = sem("mod_done")
        cols_in = sem("cols_in")
        shp_in = sem("shp_in")
        x_in = sem("x_in")
        small_in = sem("small_in")
        retc_in = sem("retc_in")
        fg_in = sem("fg_in")
        fn_in = sem("fn_in")
        out_in = sem("out_in")
        csil_done = sem("csil_done")
        ssq_done = sem("ssq_done")
        mean_done = sem("mean_done")
        rstd_done = sem("rstd_done")
        nd_done = sem("nd_done")
        y_part = sem("y_part")
        tr_done = sem("tr_done")
        hh_done = sem("hh_done")
        hl_done = sem("hl_done")
        x_done = sem("x_done")
        y_act = sem("y_act")
        y_dve = sem("y_dve")
        diag_done = sem("diag_done")
        gate_mm = sem("gate_mm")
        gate_done = sem("gate_done")
        gate_in = sem("gate_in")
        act_chain = sem("act_chain")
        dve_chain = sem("dve_chain")
        pool_chain = sem("pool_chain")
        wah_done = sem("wah_done")
        a_mm = sem("a_mm")
        a_done = sem("a_done")
        z_mm = sem("z_mm")
        z_done = sem("z_done")
        abs_done = sem("abs_done")
        ln_done = sem("ln_done")
        rel_done = sem("rel_done")
        eb_done = sem("eb_done")
        qzero = sem("qzero")
        c_dve = sem("c_dve")
        c_act = sem("c_act")
        sc_mm = sem("sc_mm")
        sm_done = sem("sm_done")
        kt_mm = sem("kt_mm")
        kst_done = sem("kst_done")
        kv_mm = sem("kv_mm")
        st_done = sem("st_done")
        go_mm = sem("go_mm")
        gsq_done = sem("gsq_done")
        grs_done = sem("grs_done")
        silu_done = sem("silu_done")
        o_done = sem("o_done")
        relu_done = sem("relu_done")
        sqh_done = sem("sqh_done")
        hid_done = sem("hid_done")
        cg_act = sem("cg_act")
        cv_act = sem("cv_act")
        cg_dve = sem("cg_dve")
        cv_dve = sem("cv_dve")
        fsilu = sem("fsilu")
        rope_q = sem("rope_q")
        rope_k = sem("rope_k")
        dtr = sem("dtr")
        dtr_act = sem("dtr_act")
        ds_mm = sem("ds_mm")
        ds_max = sem("ds_max")
        ds_exp = sem("ds_exp")
        da_done = sem("da_done")
        dat_mm = sem("dat_mm")
        dat_done = sem("dat_done")
        do_mm = sem("do_mm")
        do_act = sem("do_act")
        drs = sem("drs")
        rs_mm = sem("rs_mm")
        rsm_done = sem("rsm_done")
        ro_mm = sem("ro_mm")
        rsq = sem("rsq")
        rrs = sem("rrs")
        ry = sem("ry")
        z_ready = sem("z_ready")
        sln = sem("sln")
        mask_done = sem("mask_done")
        spm = sem("spm")
        e_mm = sem("e_mm")
        sexp = sem("sexp")
        so_mm = sem("so_mm")
        so_hi = sem("so_hi")
        so_lo = sem("so_lo")
        ang_done = sem("ang_done")
        rope_done = sem("rope_done")
        lam_sum = sem("lam_sum")
        lam_exp = sem("lam_exp")
        gsc_done = sem("gsc_done")
        wal_done = sem("wal_done")
        fin_done = sem("fin_done")
        sq_done = sem("sq_done")
        rqk_done = sem("rqk_done")


        block = ctx.enter_context(nc.Block())

        (TR_N0, TR_GO, TR_N1, TR_N2, TR_DO, TR_N3, TR_N4, TR_RA, TR_RB, TR_N5, TR_N6, TR_N7) = range(12)
        (Y_GV, Y_GR, Y_GOUT, Y_M0, Y_DQ, Y_DK, Y_DV, Y_DOUT, Y_M1, Y_RV0, Y_RV1, Y_RG0, Y_RG1, Y_ROUT, Y_F0,
         Y_SV, Y_SOUT, Y_F1) = range(18)
        BY_ACT = [Y_GV, Y_DQ, Y_DK, Y_DV, Y_RV0, Y_RV1, Y_RG0, Y_RG1, Y_SV]
        BY_DVE = [Y_GR, Y_GOUT, Y_M0, Y_DOUT, Y_M1, Y_ROUT, Y_F0, Y_SOUT, Y_F1]
        X_GLA, X_M0, X_DIFF, X_M1, X_FG, X_RET, X_F0, X_SB, X_F1 = 4, 8, 12, 16, 18, 22, 26, 30, 34
        N_C_RET = 4
        Y_LAST = [C_GQ - 1, C_GO - 1, C_M0 - 1, C_DQ - 1, C_DK - 1, C_DV - 1, C_DO - 1, C_M1 - 1, C_RQ - 1,
                  C_RV + 3, C_RG - 1, C_RG + 3, C_RO - 1, C_F0 - 1, C_SQ - 1, C_SO - 1, C_F1 - 1, NCHUNK - 1]

        def y_read(y, bank):
            if y in BY_ACT:
                return y_act, 4 * BY_ACT.index(y) + bank + 1
            return y_dve, 4 * BY_DVE.index(y) + bank + 1

        def y_written(y, bank):
            return (y_part, 3 * y + bank + 1) if bank < 3 else multiplied(Y_LAST[y])

        def so_bank(p):
            return p - 2 if p >= 6 else p % 2

        def early_slot(s):
            r = s - ADA_RING
            if 0 <= r < 2 * NSLOT:
                return raw[:, r // 2, (r % 2) * D:(r % 2 + 1) * D], early_in[r], 16
            return ada[:, s % ADA_RING, :], ada_in[s % ADA_RING], 16 if s < ADA_RING else 32

        def slot_visit(c):
            return c if isinstance(c, tuple) else (c % NSLOT, c // NSLOT)

        def multiplied(c):
            s, v = slot_visit(c)
            return used[s], v + 1

        def ffn_chunk(c0, g, part):
            if part == 2:
                return c0 + 3 * GROUPS - 1 if g == GROUPS - 1 else ffn_chunk(c0, g + 1, 1) + 1
            return c0 + (part if g == 0 else 3 * g - 1 + part)

        def d_bank(h):
            return (2, 4, 6)[h % 3]

        def s_bank(p):
            return (4, 6, 2)[p % 3]

        def bcast(ap, n):
            k = ap.shape[1]
            return ap.rearrange("p (o k) -> p o k", o=1).to_broadcast([P, n, k])

        @block.sync
        def _(sp):
            sp.dma_start(cols[:, :], cols_d).then_inc(cols_in, 16)
            for s in range(2 * KT):
                part, k = s % 2, s // 2
                if s >= ADA_RING + 2 * NSLOT:
                    if part:
                        sp.wait_ge(ada_pe, (s - 2 * NSLOT - ADA_RING) // 2 + 1)
                    else:
                        sp.wait_ge(ada_step, s - 2 * NSLOT - ADA_RING + 2)
                if s == 2:
                    sp.dma_start(x[:, :, :], x_d).then_inc(x_in, 16)
                if s == 3:
                    sp.dma_start(shp[:, :], shp_d).then_inc(shp_in, 16)
                first = (part * KT + k) * P
                place, landed, _ = early_slot(s)
                sp.dma_start(place, ada_d[first:first + P, :]).then_inc(landed, 16)
            for c in range(NSLOT):
                sp.wait_ge(ada_step, ADA_RING + 2 * c + 2)
                sp.wait_ge(ada_pe, ADA_RING // 2 + c + 1)
                sp.dma_start(raw[:, c, :], stream_d[c * P:(c + 1) * P, :]).then_inc(raw_in[c], 16)
            with sp.Fori(1, NCHUNK // NSLOT) as i:
                for s in range(NSLOT):
                    sp.wait_ge(lo_done[s], i)
                    sp.dma_start(raw[:, s, :], stream_d[bass.ds((i * NSLOT + s) * P, P), :]).then_inc(raw_in[s], 16)
            for c in range(NCHUNK - NCHUNK % NSLOT, NCHUNK):
                s, v = slot_visit(c)
                sp.wait_ge(lo_done[s], v)
                sp.dma_start(raw[:, s, :], stream_d[c * P:(c + 1) * P, :]).then_inc(raw_in[s], 16)
            for t in range(TT):
                sp.wait_ge(fin_done, 1 + t)
                sp.dma_start(out_d[t * P:(t + 1) * P, :], xn[:, t, :]).then_inc(out_in, 16)
            sp.wait_ge(out_in, 16 * TT)

        @block.gpsimd
        def _(pool):
            pc = Count(pool_chain)
            for dst, src in ((posi[:, :], pos_d), (lamv[:, :], lam_d), (gng[:, :], gng_d), (sub[:, :], sub_d),
                             (g_wa[:, :], wa_d), (g_w2[0:GRANK, :], wa2_d), (row[:, :], br_d)):
                pool.dma_start(dst, src).then_inc(small_in, 16)

            def gate_bias(n):
                pool.dma_start(row[:, :], gate_d[n * P:(n + 1) * P, :]).then_inc(gate_in, 16)

            def inverse_rms(out, sums, n, width):
                pc.inc(pool.tensor_scalar(sums, sums, 1.0 / width, EPS, ALU.mult, ALU.add))
                pool.wait_ge(pool_chain, pc.n)
                return pool.tensor_tensor(out, sums, shp[:, S_HALF:S_HALF + n], ALU.pow)

            def norm(k):
                for t in range(TT):
                    pool.wait_ge(mean_done, TT * k + t + 1)
                    pool.tensor_tensor(rstd[:, t:t + 1], ssq[:, 4 + t:5 + t], shp[:, S_HALF:S_HALF + 1], ALU.pow)\
                        .then_inc(rstd_done, 1)

            def ada_load(s):
                pool.wait_ge(ada_step, s - ADA_RING + 1)
                pool.dma_start(ada[:, s % ADA_RING, :], ada_d[s * P:(s + 1) * P, :]).then_inc(ada_more[s % ADA_RING], 16)

            pool.wait_ge(shp_in, 16)
            norm(0)
            pool.wait_ge(ada_pe, KT)
            for s in range(2 * KT, 2 * KT + ADA_RING):
                ada_load(s)
            pool.wait_ge(hl_done, 4)
            pool.memset(g_q[:, :, :, :, :], 0.0).then_inc(qzero, 1)
            for s in range(2 * KT + ADA_RING, 5 * KT):
                ada_load(s)
            pool.wait_ge(*y_read(Y_GR, 3))
            gate_bias(0)
            for h in range(GH_):
                pool.wait_ge(gsq_done, 2 * h + 2)
                inverse_rms(stat[:, 1, 2 * h:2 * h + 2], stat[:, 0, 2 * h:2 * h + 2], 2, GDV).then_inc(grs_done, 1)
            norm(1)
            with pool.Fori(0, MLP_BODIES) as i:
                for k in range(KT):
                    pool.wait_ge(ada_step, i * KT + (5 * KT + k - ADA_RING + 1))
                    pool.dma_start(ada[:, k % ADA_RING, :], ada_d[bass.ds((i * KT + (5 * KT + k)) * P, P), :])\
                        .then_inc(ada_more[k % ADA_RING], 16)
            norm(2)
            gate_bias(1)
            for s in range(8 * KT, 10 * KT + 6 + ADA_RING):
                ada_load(s)
            for h in range(DH_):
                pool.wait_ge(do_act, h + 1)
                inverse_rms(stat[:, 1, 2 * h:2 * h + 2], stat[:, 0, 2 * h:2 * h + 2], 2, DDV).then_inc(drs, 1)
            for s in range(10 * KT + 6 + ADA_RING, 11 * KT + ADA_RING):
                ada_load(s)
            norm(3)
            gate_bias(2)
            for s in range(11 * KT + ADA_RING, ADA_STEPS):
                ada_load(s)
            pool.wait_ge(ada_step, ADA_STEPS)
            pool.dma_start(retc[:, :], retc_d).then_inc(retc_in, 16)
            pool.wait_ge(ada_mm, ADA_PARTS)
            pool.dma_start(acc[:, :], fg_d).then_inc(fg_in, 16)
            norm(4)
            norm(5)
            pool.dma_start(acc[:, :], fn_d).then_inc(fn_in, 16)
            for h in range(RH_):
                pool.wait_ge(rsq, 2 * h + 2)
                inverse_rms(stat[:, 1, 2 * h:2 * h + 2], stat[:, 0, 2 * h:2 * h + 2], 2, RDV).then_inc(rrs, 1)
            for k in range(6, 10):
                norm(k)

        @block.scalar
        def _(act):
            ac = Count(act_chain)

            def hi(c):
                if not isinstance(c, tuple) and c >= NCHUNK:
                    return
                s, v = slot_visit(c)
                act.wait_ge(raw_in[s], v * 16 + 16)
                if isinstance(c, tuple) or v:
                    act.wait_ge(used[s], v)
                act.activation(w_hi[:, s, :], raw[:, s, :], ACT.Copy).then_inc(hi_done[s], 1)

            def squares(k, x_count, dst=sq_out):
                for n in range(4):
                    t, half = n // 2, n % 2
                    if x_count == X_FG:
                        act.wait_ge(x_done, X_FG - 1 + t)
                    elif x_count is not None:
                        act.wait_ge(x_done, x_count - 3 + n)
                    part = slice(half * 512, (half + 1) * 512)
                    act.activation(dst[:, t, part], x[:, t, part], ACT.Square, scale=D ** -0.5,
                                   accum_out=ssq[:, 2 * half + t:2 * half + t + 1]).then_inc(ssq_done, 1)

            def norm(k, x_count, stage, late, scale_col, bias_col):
                squares(k, x_count)
                hi(late)
                norm_rows(stage, scale_col, bias_col)

            def norm_rows(stage, scale_col, bias_col):
                for b in range(4):
                    act.wait_ge(tr_done, 4 * stage + b + 1)
                    for j in range(2):
                        kt = 2 * b + j
                        last = act.activation(h32[:, kt, :], ps[:, 4 + b, j * T:(j + 1) * T], ACT.Identity,
                                              bias=bias_col(kt) if bias_col else 0.0, scale=scale_col(kt))
                    if b == 3:
                        ac.inc(last)
                        act.wait_ge(act_chain, ac.n)
                        last = act.activation(h_hi[:, 2 * b:2 * b + 2, :], h32[:, 2 * b:2 * b + 2, :], ACT.Copy)
                    last.then_inc(hh_done, 1)

            def split_stage(stage, dst):
                for b in range(4):
                    act.wait_ge(tr_done, 4 * stage + b + 1)
                    act.activation(dst[:, 2 * b:2 * b + 2, :].rearrange("p k t -> p (k t)"), ps[:, 4 + b, :],
                                   ACT.Copy).then_inc(hh_done, 1)

            def read_y(y, dst, scale=1.0, func=ACT.Copy):
                for b in range(4):
                    act.wait_ge(*y_written(y, b))
                    act.activation(dst[:, b // 2, (b % 2) * 512:(b % 2 + 1) * 512], ps[:, b, :], func, scale=scale)\
                        .then_inc(y_act, 1)

            def gate_row():
                act.wait_ge(gate_mm, 1)
                for j in range(2):
                    last = act.activation(row[:, j * 512:(j + 1) * 512], ps[:, 6 + j, :], ACT.Copy, scale=-1.0)
                last.then_inc(gate_done, 1)

            act.wait_ge(cols_in, 16)
            act.activation(csil[:, :], cols[:, COL_C:COL_C + KT], ACT.Silu).then_inc(csil_done, 1)
            act.wait_ge(x_in, 16)
            squares(0, None, xn)
            act.wait_ge(small_in, 16 * 7)
            act.activation(g_wah[:, :], g_wa[:, :], ACT.Copy).then_inc(wah_done, 1)
            act.wait_ge(ang_done, 2)
            act.activation(rope[:, :, :, :].rearrange("p a t k -> p (a t k)"),
                           ang[:, 2:4, :, :].rearrange("p a t k -> p (a t k)"), ACT.Sin).then_inc(rope_done, 1)
            act.preload_act_table_set("natural_log_exp_and_others")
            act.wait_ge(lam_sum, 1)
            act.activation(lamc[:, 2:4], lamc[:, 0:2], ACT.Exp).then_inc(lam_exp, 1)
            act.activation(maskr[:, 0:P], ident, ACT.Copy)
            act.activation(maskr[:, P:4 * P], shp[:, S_CAUS:S_CAUS + 3 * P], ACT.Copy).then_inc(mask_done, 1)
            act.wait_ge(ada_pe, KT)
            for j in range(2):
                act.activation(srow[0:1, j * 512:(j + 1) * 512], ps[0:1, 2 + j, :], ACT.Copy).then_inc(srow_done, 1)
            hi(0)
            act.wait_ge(gsc_done, 1)
            norm_rows(TR_N0, lambda kt: gsc[:, kt:kt + 1], lambda kt: mod[:, SH_T * KT + kt:SH_T * KT + kt + 1])
            for c in range(1, NSLOT):
                hi(c)

            act.wait_ge(abs_done, 1)
            ac.inc(act.activation(g_t[:, :, :], g_t[:, :, :], ACT.Exp, scale=-1.0))
            act.wait_ge(act_chain, ac.n)
            act.activation(g_t[:, :, :], g_t[:, :, :], ACT.Ln, bias=shp[:, S_ONE:S_ONE + 1]).then_inc(ln_done, 1)
            hi(C_GV + 4)
            hi(C_GV + 5)
            act.wait_ge(rel_done, 1)
            act.activation(g_eb[:, :, :], g_b[:, :, :], ACT.Exp, scale=1.0 / GTAU)
            act.activation(g_en[:, :, :], g_b[:, :, :], ACT.Exp, scale=-1.0 / GTAU)
            act.activation(el[:, :], g_b[:, :, :].rearrange("p h (c j) -> p (h c) j", j=GCH)[:, :, GCH - 1],
                           ACT.Exp, scale=1.0 / GTAU)
            act.activation(g_es[:, :, :], g_t[:, :, :], ACT.Exp, scale=1.0 / GTAU).then_inc(eb_done, 1)
            hi(C_GV + 6)
            read_y(Y_GV, g_v)
            for c in range(C_GV + 3, C_GR + 2):
                hi(c + 4)
            for b in range(2):
                act.wait_ge(kt_mm, b + 1)
                act.activation(g_kst[:, 2 * b:2 * b + 2, :, :].rearrange("p h t k -> p (h t k)"), ps[:, 6 + b, :],
                               ACT.Copy).then_inc(kst_done, 1)
            for c in range(C_GR + 2, C_GO):
                hi(c + 4)
            for b in range(4):
                act.wait_ge(*y_read(Y_GR, b))
                g = g_r[:, b // 2, (b % 2) * 512:(b % 2 + 1) * 512]
                act.activation(g, g, ACT.Silu).then_inc(silu_done, 1)
            for h in range(GH_):
                act.wait_ge(go_mm, h + 1)
                for t in range(TT):
                    k = 2 * h + t
                    act.activation(h_hi[:, k, :], ps[:, h, t * GDV:(t + 1) * GDV], ACT.Square,
                                   accum_out=stat[:, 0, k:k + 1]).then_inc(gsq_done, 1)
            split_stage(TR_GO, h_hi)
            for c in range(C_GO, C_GO + 3):
                hi(c + 4)
            act.wait_ge(gsc_done, 2)
            norm(1, X_GLA, TR_N1, C_GO + 7, lambda kt: gsc[:, KT + kt:KT + kt + 1],
                 lambda kt: mod[:, SH_C * KT + kt:SH_C * KT + kt + 1])

            def mlp(layer, c0):
                B = UNITS * layer

                def unit(u, par, later, c):
                    act.wait_ge(*multiplied(c))
                    if later:
                        act.wait_ge(hid_done, u - 1)
                    act.activation(m_r[:, par, :], ps[:, 4 + par, :], ACT.Relu).then_inc(relu_done, 1)
                    act.wait_ge(relu_done, u + 1)
                    act.activation(hid_hi[:, par, :, :].rearrange("p f t -> p (f t)"), m_r[:, par, :], ACT.Square)\
                        .then_inc(sqh_done, 1)

                unit(B, 0, False, c0)
                hi(c0 + 4)
                unit(B + 1, 1, False, c0 + 1)
                hi(c0 + 5)
                hi(c0 + 6)
                with act.Fori(0, MLP_BODIES) as it:
                    for j in range(MLP_UNROLL):
                        c = c0 + 3 + 2 * j
                        unit(it * MLP_UNROLL + (B + 2 + j), j % 2, True, (c % NSLOT, it * 2 + c // NSLOT))
                        for c in (c + 4, c + 5):
                            hi((c % NSLOT, it * 2 + c // NSLOT))
                c = c0 + 7 + 2 * MLP_UNROLL * MLP_BODIES
                for i in range(2 + MLP_UNROLL * MLP_BODIES, UNITS):
                    unit(B + i, i % 2, True, c - 4)
                    if layer == 0 and i == UNITS - 1:
                        gate_row()
                    hi(c)
                    hi(c + 1)
                    c += 2

            mlp(0, C_M0)
            act.wait_ge(gsc_done, 3)
            norm(2, X_M0, TR_N2, C_DQ + 3, lambda kt: gsc[:, 2 * KT + kt:2 * KT + kt + 1],
                 lambda kt: mod[:, (6 + SH_T) * KT + kt:(6 + SH_T) * KT + kt + 1])

            def d_features(dst, n):
                for b in range(4):
                    act.wait_ge(dtr, n + b + 1)
                    act.activation(dst[:, 2 * b:2 * b + 2, :].rearrange("p k t -> p (k t)"), ps[:, 4 + b, :],
                                   ACT.Copy).then_inc(dtr_act, 1)

            for c in range(C_DQ, C_DQ + 3):
                hi(c + 4)
            read_y(Y_DQ, d_q, DDH ** -0.5)
            for c in range(C_DQ + 3, C_DK + 3):
                hi(c + 4)
            read_y(Y_DK, d_k)
            hi(C_DK + 7)
            d_features(d_qt, 0)
            hi(C_DV + 4)
            hi(C_DV + 5)
            d_features(d_kt, 4)
            hi(C_DV + 6)
            act.preload_act_table_set("natural_log_exp_and_others")
            read_y(Y_DV, d_v)

            def d_exp(h):
                act.wait_ge(ds_max, h + 1)
                r = h % 3
                for i in range(2):
                    for t, first, n in ((1, 0, 2 * P), (0, 2 * P, P)):
                        k = 2 * i + t
                        last = act.activation(d_p[:, r, i, first:first + n], ps[:, d_bank(h) + i, first:first + n],
                                              ACT.Exp, bias=d_st[:, r, 0, k:k + 1], accum_out=d_st[:, r, 1, k:k + 1])
                last.then_inc(ds_exp, 1)

            def d_out(h):
                act.wait_ge(do_mm, h + 1)
                out = ps[:, 0, (h % 2) * T:(h % 2 + 1) * T].rearrange("p (t k) -> p t k", t=TT)
                for t in range(TT):
                    act.activation(h_lo[:, 2 * (h % 2) + t, 0:DDV], out[:, t, :], ACT.Square,
                                   accum_out=stat[:, 0, 2 * h + t:2 * h + t + 1])
                act.activation(d_o[:, :, h * DDV:(h + 1) * DDV], out, ACT.Copy).then_inc(do_act, 1)

            for h in range(3):
                d_exp(h)
            hi(C_DV + 7)
            for h in range(DH_):
                d_out(h)
                if h + 3 < DH_:
                    act.wait_ge(da_done, h + 1)
                    d_exp(h + 3)
            split_stage(TR_DO, h_hi)
            for c in range(C_DO, C_DO + 3):
                hi(c + 4)
            act.wait_ge(gsc_done, 4)
            norm(3, X_DIFF, TR_N3, C_DO + 7, lambda kt: gsc[:, 3 * KT + kt:3 * KT + kt + 1],
                 lambda kt: mod[:, (6 + SH_C) * KT + kt:(6 + SH_C) * KT + kt + 1])
            mlp(1, C_M1)
            squares(4, X_M1)
            norm(5, X_FG, TR_N4, C_RQ + 3, lambda kt: cols[:, COL_RET + kt:COL_RET + kt + 1], None)

            for c in range(C_RQ, C_RV + 3):
                hi(c + 4)
            read_y(Y_RV0, r_v[:, :, 0:D])
            for c in range(C_RV + 3, C_RV + 7):
                hi(c + 4)
            read_y(Y_RV1, r_v[:, :, D:2 * D])
            for c in range(C_RV + 7, C_RG + 3):
                hi(c + 4)
            read_y(Y_RG0, r_g[:, :, 0:D], 1.0, ACT.Silu)
            def r_squares(first):
                for k in range(first, first + 4):
                    act.wait_ge(ro_mm, k + 1)
                    if k:
                        act.wait_ge(rsq, k)
                    act.activation(r_sq[:, :], ps[:, 4 + k % 4, :], ACT.Square, accum_out=stat[:, 0, k:k + 1])\
                        .then_inc(rsq, 1)

            hi(C_RG + 7)
            r_squares(0)
            hi(C_RG + 8)
            split_stage(TR_RA, y_hi)
            hi(C_RG + 9)
            r_squares(4)
            hi(C_RG + 10)
            read_y(Y_RG1, r_g[:, :, D:2 * D], 1.0, ACT.Silu)
            hi(C_RO + 3)
            hi(C_RO + 4)
            split_stage(TR_RB, h_hi)
            for c in range(C_RO + 1, C_RO + 7):
                hi(c + 4)
            norm(6, X_RET, TR_N5, C_RO + 11, lambda kt: cols[:, COL_FFN + kt:COL_FFN + kt + 1], None)

            def ffn(layer, c0):
                def last_tap(g, value):
                    G = GROUPS * layer + g
                    act.wait_ge(*multiplied(ffn_chunk(c0, g, value)))
                    if g >= 2:
                        act.wait_ge(hid_done, 2 * UNITS + G - 1)
                    for f in range(2):
                        k = COL_CONV + ((layer * 2 + value) * FT + 2 * g + f) * (CONV + 1)
                        last = act.activation(f_cv[:, g % 2, value, f, :],
                                              ps[:, 4 + 2 * (g % 2) + value, f * T:(f + 1) * T],
                                              ACT.Identity, bias=cols[:, k + 3:k + 4], scale=cols[:, k + 2:k + 3])
                    last.then_inc(cv_act if value else cg_act, 1)

                c = c0 + 4
                for g in range(GROUPS):
                    last_tap(g, 0)
                    hi(c)
                    act.wait_ge(cg_dve, GROUPS * layer + g + 1)
                    act.activation(f_cv[:, g % 2, 0, :, :], f_cv[:, g % 2, 0, :, :], ACT.Silu).then_inc(fsilu, 1)
                    last_tap(g, 1)
                    hi(c + 1)
                    c += 2
                    if g:
                        hi(c)
                        c += 1

            ffn(0, C_F0)
            norm(7, X_F0, TR_N6, C_SQ + 3, lambda kt: cols[:, COL_SB + kt:COL_SB + kt + 1], None)

            for n in range(2 * KT // 2):
                act.wait_ge(*multiplied(C_SQ + n))
                dst, m = (s_q, n) if n < 4 else (s_k, n - 4)
                act.activation(dst[:, 2 * m:2 * m + 2, :].rearrange("p k t -> p (k t)"), ps[:, 4 + n % 4, :], ACT.Copy,
                               scale=SDH ** -0.5 if n < 4 else 1.0).then_inc(c_act, 1)
                hi(C_SQ + n + 4)
            for c in range(C_SV, C_SV + 2):
                hi(c + 4)

            act.preload_act_table_set("natural_log_exp_and_others")

            def s_log(p):
                act.wait_ge(z_ready, p + 1)
                ln = s_b[:, p % 3, 0, :, :]
                if p >= 3:
                    act.wait_ge(so_mm, p - 2)
                ac.inc(act.activation(ln, ps[:, s_bank(p):s_bank(p) + 2, 0:3 * P], ACT.Abs))
                act.wait_ge(act_chain, ac.n)
                ac.inc(act.activation(ln, ln, ACT.Exp, scale=-1.0))
                act.wait_ge(act_chain, ac.n)
                act.activation(ln, ln, ACT.Ln, bias=shp[:, S_ONE:S_ONE + 1]).then_inc(sln, 1)

            def s_exp(p):
                act.wait_ge(e_mm, p + 1)
                act.activation(s_b[:, p % 3, 0, :, :], ps[:, s_bank(p):s_bank(p) + 2, 0:3 * P], ACT.Exp)\
                    .then_inc(sexp, 1)

            def s_out(p):
                act.wait_ge(so_mm, p + 1)
                act.activation(h_hi[:, p, :], ps[:, so_bank(p), 0:T], ACT.Copy).then_inc(so_hi, 1)

            s_log(0)
            s_log(1)
            read_y(Y_SV, s_v)
            for p in range(SH_ // 2):
                s_exp(p)
                if p >= 1:
                    s_out(p - 1)
                if p + 2 < SH_ // 2:
                    s_log(p + 2)
            s_out(SH_ // 2 - 1)
            hi(C_SV + 6)
            hi(C_SV + 7)
            for c in range(C_SO, C_SO + 3):
                hi(c + 4)
            norm(8, X_SB, TR_N7, C_SO + 7, lambda kt: cols[:, COL_FFN + KT + kt:COL_FFN + KT + kt + 1], None)
            ffn(1, C_F1)
            squares(9, X_F1)

        @block.vector
        def _(dve):
            dc = Count(dve_chain)

            def link(instruction):
                dc.inc(instruction)
                dve.wait_ge(dve_chain, dc.n)

            def lo(c):
                if not isinstance(c, tuple) and c >= NCHUNK:
                    return
                s, v = slot_visit(c)
                dve.wait_ge(hi_done[s], v + 1)
                dve.tensor_tensor(w_lo[:, s, :], raw[:, s, :], w_hi[:, s, :].bitcast(f32), ALU.subtract)\
                    .then_inc(lo_done[s], 1)

            def add_step(s, k, place, landed, fill, inc=1):
                dve.wait_ge(landed, fill)
                for half, done in ((slice(0, 512), ada_half), (slice(512, D), ada_step)):
                    rows, ck = place[:, half], csil[:, k:k + 1]
                    if k == 0:
                        dve.tensor_scalar(acc[:, half], rows, ck, None, ALU.mult).then_inc(done, inc)
                    else:
                        dve.wait_ge(done, s)
                        dve.scalar_tensor_tensor(acc[:, half], rows, ck, acc[:, half], ALU.mult, ALU.add)\
                            .then_inc(done, inc)

            def steps(first, n):
                for s in range(first, first + n):
                    if s % KT == 0:
                        dve.wait_ge(ada_mm, s // KT)
                    add_step(s, s % KT, ada[:, s % ADA_RING, :], ada_more[s % ADA_RING], 16 * ((s - 2 * KT) // ADA_RING + 1))

            def finish_part(p, bank):
                dve.wait_ge(ada_mm, p + 1)
                dve.tensor_tensor(mod[:, p * KT:(p + 1) * KT], ps[:, bank, 0:KT],
                                  cols[:, COL_ADAB + p * KT:COL_ADAB + (p + 1) * KT], ALU.add).then_inc(mod_done, 1)

            def norm_scale(n, p):
                dve.wait_ge(mod_done, p + 1)
                dve.scalar_tensor_tensor(gsc[:, n * KT:(n + 1) * KT], mod[:, p * KT:(p + 1) * KT], 1.0,
                                         cols[:, COL_NORM + n * KT:COL_NORM + (n + 1) * KT], ALU.add, ALU.mult)\
                    .then_inc(gsc_done, 1)
                dve.wait_ge(gsc_done, n + 1)

            def norm_mean(k, t):
                dve.wait_ge(ssq_done, 4 * k + 2 * t + 2)
                dve.scalar_tensor_tensor(ssq[:, 4 + t:5 + t], ssq[:, t:t + 1], EPS, ssq[:, 2 + t:3 + t],
                                         ALU.add, ALU.add).then_inc(mean_done, 1)

            def norm_diag(k, t):
                dve.wait_ge(rstd_done, TT * k + t + 1)
                dve.tensor_scalar(nd[:, t, :], ident, rstd[:, t:t + 1], None, ALU.mult).then_inc(nd_done, 1)

            def norm_split(stage):
                for b in range(4):
                    pair = slice(2 * b, 2 * b + 2)
                    dve.wait_ge(hh_done, 4 * stage + b + 1)
                    if b < 3:
                        link(dve.tensor_copy(h_hi[:, pair, :], h32[:, pair, :]))
                    dve.tensor_tensor(h_lo[:, pair, :], h32[:, pair, :], h_hi[:, pair, :].bitcast(f32), ALU.subtract)\
                        .then_inc(hl_done, 1)

            def split_stage(stage, dst, src_hi):
                for b in range(4):
                    dve.wait_ge(hh_done, 4 * stage + b + 1)
                    dve.tensor_tensor(dst[:, 2 * b:2 * b + 2, :].rearrange("p k t -> p (k t)"), ps[:, 4 + b, :],
                                      src_hi[:, 2 * b:2 * b + 2, :].rearrange("p k t -> p (k t)").bitcast(f32),
                                      ALU.subtract).then_inc(hl_done, 1)

            def norm_end(norm, t):
                if norm not in (4, 9):
                    norm_diag(norm, t)

            def make_diag(p):
                dve.wait_ge(mod_done, p + 1)
                for kt in range(KT):
                    last = dve.tensor_scalar(diag[:, kt, :], ident, mod[:, p * KT + kt:p * KT + kt + 1], None, ALU.mult)
                last.then_inc(diag_done, 1)

            def row_gate(n):
                dve.wait_ge(ada_mm, ROW_GATES[n] + 1)
                dve.wait_ge(gate_in, 16 * (n + 1))
                for j in range(2):
                    half = slice(j * 512, (j + 1) * 512)
                    last = dve.tensor_tensor(row[:, half], row[:, half], ps[:, 6 + j, :], ALU.subtract)
                last.then_inc(mod_done, 1)

            def add_gated(y, gate, norm):
                dve.wait_ge(*gate)
                for b in range(4):
                    dve.wait_ge(*y_written(y, b))
                    half = slice((b % 2) * 512, (b % 2 + 1) * 512)
                    dve.tensor_tensor(xn[:, b // 2, half], ps[:, b, :], row[:, half], ALU.mult).then_inc(y_dve, 1)
                    if b == 2:
                        norm_mean(norm, 0)
                    dve.wait_ge(*y_read(y, b))
                    dve.tensor_tensor(x[:, b // 2, half], x[:, b // 2, half], xn[:, b // 2, half], ALU.add)\
                        .then_inc(x_done, 1)
                    if b == 2:
                        norm_end(norm, 0)
                norm_mean(norm, 1)
                norm_end(norm, 1)

            def early_step(k):
                add_step(2 * k, k, *early_slot(2 * k), 2)

            def angles():
                dve.wait_ge(small_in, 16 * 7)
                link(dve.tensor_copy(stat[:, 0, 0:TT], posi[:, :]))
                for t in range(TT):
                    last = dve.tensor_scalar(ang[:, 0, t, :], shp[:, S_INVF:S_INVF + 8], stat[:, 0, t:t + 1], None,
                                             ALU.mult)
                link(last)

            def reduce_angle(n, quarter):
                turns, whole, rest = ang[:, 1, :, :], ang[:, 0, :, :], ang[:, n, :, :]
                link(dve.tensor_scalar(turns, whole, 1.0 / (2 * math.pi), quarter, ALU.mult, ALU.add))
                link(dve.tensor_scalar(turns, turns, ROUND, -ROUND, ALU.add, ALU.add))
                link(dve.scalar_tensor_tensor(rest, turns, -TURN[0], whole, ALU.mult, ALU.add))
                link(dve.scalar_tensor_tensor(rest, turns, -TURN[1], rest, ALU.mult, ALU.add))
                link(dve.scalar_tensor_tensor(rest, turns, -TURN[2], rest, ALU.mult, ALU.add))
                if quarter:
                    link(dve.tensor_scalar(rest, rest, math.pi / 2, None, ALU.add))
                dve.tensor_scalar(rest, rest, PI32, -PI32, ALU.min, ALU.max).then_inc(ang_done, 1)

            dve.wait_ge(csil_done, 1)
            early_step(0)
            early_step(1)
            dve.wait_ge(shp_in, 16)
            norm_mean(0, 0)
            norm_mean(0, 1)
            early_step(2)
            norm_diag(0, 0)
            norm_diag(0, 1)
            early_step(3)
            angles()
            early_step(4)
            reduce_angle(2, 0.25)
            early_step(5)
            reduce_angle(3, 0.0)
            early_step(6)
            lv = lamv[:, :].rearrange("p (a b k) -> p a b k", a=2, b=2)
            link(dve.tensor_tensor(lamp[:, :, :], lv[:, :, 0, :], lv[:, :, 1, :], ALU.mult))
            dve.tensor_reduce(lamc[:, 0:2], lamp[:, :, :], AX, ALU.add).then_inc(lam_sum, 1)
            dve.tensor_scalar(sub[:, :], sub[:, :], 1.0 - LAMBDA_INIT, None, ALU.mult)
            early_step(7)
            dve.wait_ge(wah_done, 1)
            dve.tensor_tensor(g_wal[:, :], g_wa[:, :], g_wah[:, :].bitcast(f32), ALU.subtract).then_inc(wal_done, 1)
            finish_part(0, 0)
            finish_part(1, 1)
            norm_scale(0, SC_T)
            norm_split(TR_N0)
            lo(0)
            dve.wait_ge(lam_exp, 1)
            link(dve.tensor_tensor(lamc[:, 0:1], lamc[:, 3:4], lamc[:, 2:3], ALU.subtract))
            dve.tensor_scalar(lamc[:, 0:1], lamc[:, 0:1], -LAMBDA_INIT, None, ALU.add)
            dve.wait_ge(rope_done, 1)

            dve.wait_ge(a_mm, 1)
            dve.tensor_copy(g_a[0:GRANK, :], ps[0:GRANK, 4, 0:T]).then_inc(a_done, 1)
            for c in range(1, NSLOT):
                lo(c)
            dve.wait_ge(z_mm, 1)
            for h in range(GH_):
                last = dve.tensor_scalar(g_z[:, h, :], ps[:, 6 + h // 2, (h % 2) * T:(h % 2 + 1) * T],
                                         cols[:, COL_BA + h:COL_BA + h + 1], None, ALU.add)
            last.then_inc(z_done, 1)
            dve.wait_ge(z_done, 1)
            dve.scalar_tensor_tensor(g_t[:, :, :], g_z[:, :, :], -1.0, g_z[:, :, :], ALU.mult, ALU.max)\
                .then_inc(abs_done, 1)
            dve.wait_ge(abs_done, 1)
            lo(4)
            link(dve.tensor_scalar(g_z[:, :, :], g_z[:, :, :], 0.0, None, ALU.min))
            dve.wait_ge(ln_done, 1)
            link(dve.scalar_tensor_tensor(g_t[:, :, :], g_t[:, :, :], -1.0, g_z[:, :, :], ALU.mult, ALU.add))
            for h in range(GH_):
                last = dve.tensor_tensor_scan(g_b[:, h, :], shp[:, S_SCAN:S_SCAN + T], g_t[:, h, :], 0.0,
                                              ALU.mult, ALU.add)
            link(last)
            bv = g_b[:, :, :].rearrange("p h (c j) -> p (h c) j", j=GCH)
            dve.tensor_tensor(g_t[:, :, :].rearrange("p h (c j) -> p (h c) j", j=GCH),
                              bv[:, :, GCH - 1:GCH].to_broadcast([P, GH_ * 4, GCH]), bv, ALU.subtract)\
                .then_inc(rel_done, 1)
            lo(5)
            steps(2 * KT, 4)
            lo(6)
            lo(7)
            dve.wait_ge(eb_done, 1)
            dve.wait_ge(qzero, 1)
            for n in range(2):
                dve.wait_ge(*multiplied(C_GQ + n))
                for f in range(2):
                    h = 2 * n + f
                    src = ps[:, 4 + n, f * T:(f + 1) * T].rearrange("p (t c j) -> p t c j", t=TT, c=2)
                    dec = g_eb[:, h, :].rearrange("p (t c j) -> p t c j", t=TT, c=2)
                    for c in range(2):
                        last = dve.scalar_tensor_tensor(g_q[:, h, :, c, c * GCH:(c + 1) * GCH], src[:, :, c, :],
                                                        GDK ** -0.5, dec[:, :, c, :], ALU.mult, ALU.mult)
                last.then_inc(c_dve, 1)
                lo(C_GQ + n + 4)
                if n == 0:
                    steps(2 * KT + 4, 4)
            for n in range(2):
                dve.wait_ge(*multiplied(C_GK + n))
                flat = lambda a: a[:, 2 * n:2 * n + 2, :].rearrange("p h t -> p (h t)")
                dve.tensor_tensor(flat(g_ki), ps[:, 4 + n, :], flat(g_en), ALU.mult)
                dve.tensor_tensor(flat(g_ks), ps[:, 4 + n, :], flat(g_es), ALU.mult).then_inc(c_dve, 1)
                lo(C_GK + n + 4)
                if n == 0:
                    finish_part(2, 6)
                steps(3 * KT + 3 * n, 3)
            lo(C_GR + 4)
            steps(3 * KT + 6, 2)
            finish_part(3, 6)
            lo(C_GR + 5)
            steps(4 * KT, 2)
            for b in range(2):
                dve.wait_ge(sc_mm, b + 1)
                dve.tensor_tensor(g_sm[:, 2 * b:2 * b + 2, :, :].rearrange("p h t k -> p (h t) k"),
                                  ps[:, 4 + b, :].rearrange("p (a k) -> p a k", a=4),
                                  bcast(shp[:, S_GLAM:S_GLAM + P], 4), ALU.mult).then_inc(sm_done, 1)
            def state(h):
                dve.wait_ge(kv_mm, h + 1)
                if h >= 2:
                    dve.wait_ge(go_mm, h - 1)
                kv = (ps[:, 4 + 2 * (h % 2), 0:GDV], ps[:, 5 + 2 * (h % 2), 0:GDV], ps[:, 4 + 2 * (h % 2), GDV:2 * GDV])
                st = g_st[:, h % 2, :, :]
                link(dve.tensor_copy(st[:, 0, :], kv[0]))
                link(dve.scalar_tensor_tensor(st[:, 1, :], st[:, 0, :], el[:, 4 * h + 1:4 * h + 2], kv[1],
                                              ALU.mult, ALU.add))
                dve.scalar_tensor_tensor(st[:, 2, :], st[:, 1, :], el[:, 4 * h + 2:4 * h + 3], kv[2],
                                         ALU.mult, ALU.add).then_inc(st_done, 1)

            steps(4 * KT + 2, 2)
            state(0)
            state(1)
            for b in range(4):
                dve.wait_ge(*y_written(Y_GR, b))
                half = slice((b % 2) * 512, (b % 2 + 1) * 512)
                dve.tensor_tensor(g_r[:, b // 2, half], ps[:, b, :], row[:, half], ALU.add).then_inc(y_dve, 1)
            lo(C_GR + 6)
            for b in range(4):
                dve.wait_ge(silu_done, b + 1)
                g = g_r[:, b // 2, (b % 2) * 512:(b % 2 + 1) * 512].rearrange("p (h k) -> p h k", k=GDV)
                last = dve.tensor_tensor(g, g, bcast(gng[:, :], 2), ALU.mult)
            link(last)
            for h in range(GH_):
                if h + 2 < GH_:
                    state(h + 2)
                dve.wait_ge(grs_done, h + 1)
                for t in range(TT):
                    last = dve.scalar_tensor_tensor(g_o[:, t, h * GDV:(h + 1) * GDV], ps[:, h, t * GDV:(t + 1) * GDV],
                                                    stat[:, 1, 2 * h + t:2 * h + t + 1],
                                                    g_r[:, t, h * GDV:(h + 1) * GDV], ALU.mult, ALU.mult)
                last.then_inc(o_done, 1)
            split_stage(TR_GO, h_lo, h_hi)
            lo(C_GR + 7)
            steps(4 * KT + 4, 4)
            lo(C_GO + 4)
            norm_scale(1, SC_C)
            lo(C_GO + 5)
            row_gate(0)
            add_gated(Y_GOUT, (mod_done, GA_T + 1), 1)
            norm_split(TR_N1)
            lo(C_GO + 6)
            lo(C_GO + 7)

            def mlp(layer, c0, with_ada):
                B = UNITS * layer

                def unit(u, par):
                    dve.wait_ge(relu_done, u + 1)
                    dve.tensor_tensor(m_sq[:, par, :], m_r[:, par, :], m_r[:, par, :], ALU.mult).then_inc(sq_done, 1)
                    dve.wait_ge(sq_done, u + 1)
                    dve.wait_ge(sqh_done, u + 1)
                    dve.tensor_tensor(hid_lo[:, par, :, :].rearrange("p f t -> p (f t)"), m_sq[:, par, :],
                                      hid_hi[:, par, :, :].rearrange("p f t -> p (f t)").bitcast(f32), ALU.subtract)\
                        .then_inc(hid_done, 1)

                unit(B, 0)
                lo(c0 + 4)
                if layer == 1:
                    steps(11 * KT, 2)
                unit(B + 1, 1)
                lo(c0 + 5)
                if layer == 1:
                    steps(11 * KT + 2, 3)
                lo(c0 + 6)
                if layer == 1:
                    steps(11 * KT + 5, 3)
                with dve.Fori(0, MLP_BODIES) as it:
                    for j in range(MLP_UNROLL):
                        unit(it * MLP_UNROLL + (B + 2 + j), j % 2)
                        for q in range(2):
                            c = c0 + 7 + 2 * j + q
                            lo((c % NSLOT, it * 2 + c // NSLOT))
                            if with_ada and j < 2:
                                for k in (4 * j + 2 * q, 4 * j + 2 * q + 1):
                                    if k == 0:
                                        dve.wait_ge(ada_mm, it + 5)
                                    add_step(it * KT + (5 * KT + k), k, ada[:, k % ADA_RING, :],
                                             ada_more[k % ADA_RING],
                                             it * 32 + 16 * ((3 * KT + k) // ADA_RING + 1))
                    if with_ada:
                        dve.wait_ge(ada_mm, it + 6)
                        dve.tensor_tensor(mod[:, bass.ds(it * KT + 5 * KT, KT)], ps[:, 6, 0:KT],
                                          cols[:, bass.ds(it * KT + (COL_ADAB + 5 * KT), KT)], ALU.add)\
                            .then_inc(mod_done, 1)
                c = c0 + 7 + 2 * MLP_UNROLL * MLP_BODIES
                if layer == 0:
                    make_diag(GA_C)
                for i in range(2 + MLP_UNROLL * MLP_BODIES, UNITS):
                    unit(B + i, i % 2)
                    if layer == 1 and i == UNITS - 1:
                        row_gate(2)
                    lo(c)
                    if i < UNITS - 1:
                        lo(c + 1)
                    c += 2

            mlp(0, C_M0, True)
            norm_scale(2, 6 + SC_T)
            add_gated(Y_M0, (gate_done, 1), 2)
            norm_split(TR_N2)
            lo(C_DQ + 2)
            lo(C_DQ + 3)

            def rotate(q, done):
                v = q[:, :, :].rearrange("p t (g k) -> p t g k", k=DDH)
                x1, x2 = v[:, :, :, 0:8], v[:, :, :, 8:16]

                def each(op, out, a, b):
                    for t in range(TT):
                        last = dve.tensor_tensor(out(t), a(t), b(t), op)
                    return last

                cos = lambda t: bcast(rope[:, 0, t, :], 16)
                sin = lambda t: bcast(rope[:, 1, t, :], 16)
                r = [lambda t, n=n: d_rt[:, n, t, :, :] for n in range(4)]
                a1, a2 = (lambda t: x1[:, t]), (lambda t: x2[:, t])
                each(ALU.mult, r[0], a1, cos)
                each(ALU.mult, r[1], a2, sin)
                each(ALU.mult, r[2], a2, cos)
                link(each(ALU.mult, r[3], a1, sin))
                each(ALU.subtract, a1, r[0], r[1])
                each(ALU.add, a2, r[2], r[3]).then_inc(done, 1)
                dve.wait_ge(done, 1)

            for e in range(3):
                lo(C_DQ + e + 4)
                steps(8 * KT + 2 * e, 2)
            lo(C_DQ + 7)
            steps(8 * KT + 6, 2)
            dve.wait_ge(rope_done, 1)
            dve.wait_ge(*(y_read(Y_DQ, 3)))
            rotate(d_q, rope_q)
            for e in range(4):
                lo(C_DK + e + 4)
                if e == 1:
                    finish_part(8, 4)
                    steps(9 * KT, 4)
                if e > 1:
                    steps(9 * KT + 2 * e, 2)
            dve.wait_ge(*(y_read(Y_DK, 3)))
            rotate(d_k, rope_k)
            for e in range(4):
                if e < 3:
                    lo(C_DV + e + 4)
                if e == 0:
                    finish_part(9, 4)
                if e < 2:
                    steps(10 * KT + 3 * e, 3)

            def d_maxima(h):
                dve.wait_ge(ds_mm, h + 1)
                b, r = d_bank(h), h % 3
                m = d_st[:, r, 0, :].rearrange("p (i t) -> p i t", i=2)
                dve.tensor_reduce(m[:, :, 1], ps[:, b:b + 2, 0:2 * P], AX, ALU.max, negate=True)
                dve.tensor_reduce(m[:, :, 0], ps[:, b:b + 2, 2 * P:3 * P], AX, ALU.max, negate=True).then_inc(ds_max, 1)

            def d_combine(h):
                r, par = h % 3, h % 2
                dve.wait_ge(ds_exp, h + 1)
                link(dve.reciprocal(d_st[:, r, 2, :], d_st[:, r, 1, :]))
                dve.tensor_scalar(d_st[:, r, 2, 2:4], d_st[:, r, 2, 2:4], lamc[:, 0:1], None, ALU.mult)
                if h >= 2:
                    dve.wait_ge(dat_mm, h - 1)
                parts = ((1, 0, 2 * P), (0, 2 * P, P))
                for t, a, n in parts:
                    last = dve.tensor_scalar(d_a[:, par, a:a + n], d_p[:, r, 0, a:a + n],
                                             d_st[:, r, 2, t:t + 1], None, ALU.mult)
                link(last)
                for t, a, n in parts:
                    last = dve.scalar_tensor_tensor(d_a[:, par, a:a + n], d_p[:, r, 1, a:a + n],
                                                    d_st[:, r, 2, 2 + t:3 + t], d_a[:, par, a:a + n],
                                                    ALU.mult, ALU.add)
                last.then_inc(da_done, 1)

            def d_transposed(h):
                dve.wait_ge(dat_mm, h + 1)
                if h >= 2:
                    dve.wait_ge(do_mm, h - 1)
                dve.tensor_copy(d_at[:, h % 2, :], ps[:, 1, 0:3 * P]).then_inc(dat_done, 1)

            def d_scale(h):
                dve.wait_ge(drs, h + 1)
                for t in range(TT):
                    o = d_o[:, t, h * DDV:(h + 1) * DDV]
                    last = dve.scalar_tensor_tensor(o, o, stat[:, 1, 2 * h + t:2 * h + t + 1], sub[:, :],
                                                    ALU.mult, ALU.mult)
                last.then_inc(o_done, 1)

            d_maxima(0)
            d_maxima(1)
            d_combine(0)
            d_maxima(2)
            for h in range(DH_):
                d_transposed(h)
                if h + 1 < DH_:
                    d_combine(h + 1)
                if h + 3 < DH_:
                    d_maxima(h + 3)
                if h >= 1:
                    d_scale(h - 1)
            d_scale(DH_ - 1)
            split_stage(TR_DO, h_lo, h_hi)
            lo(C_DV + 7)
            steps(10 * KT + 6, 2)
            lo(C_DO + 4)
            norm_scale(3, 6 + SC_C)
            lo(C_DO + 5)
            row_gate(1)
            add_gated(Y_DOUT, (mod_done, 6 + GA_T + 1), 3)
            norm_split(TR_N3)
            lo(C_DO + 6)
            lo(C_DO + 7)
            mlp(1, C_M1, False)
            add_gated(Y_M1, (mod_done, 6 + GA_C + 1), 4)
            dve.wait_ge(fg_in, 16)
            for t in range(TT):
                dve.wait_ge(rstd_done, TT * 4 + t + 1)
                dve.scalar_tensor_tensor(x[:, t, :], x[:, t, :], rstd[:, t:t + 1], acc[:, :], ALU.mult, ALU.mult)\
                    .then_inc(x_done, 1)
            for t in range(TT):
                norm_mean(5, t)
                norm_diag(5, t)
            norm_split(TR_N4)
            lo(C_RQ + 2)
            lo(C_RQ + 3)

            dve.wait_ge(retc_in, 16)
            for n in range(2 * RH_):
                dst, h = (r_q, n) if n < RH_ else (r_k, n - RH_)
                dve.wait_ge(*multiplied(C_RQ + n))
                src = ps[:, 4 + n % 4, :].rearrange("p (a t) -> p a t", a=2)
                dve.tensor_tensor(r_t[:, 0, :, :], src, bcast(retc[:, 0:T], 2), ALU.mult)
                dve.tensor_tensor(r_t[:, 1, :, :], src, bcast(retc[:, T:2 * T], 2), ALU.mult).then_inc(c_dve, 1)
                dve.wait_ge(c_dve, N_C_RET + n + 1)
                dve.tensor_tensor(dst[:, 2 * h, :], r_t[:, 0, 0, :], r_t[:, 1, 1, :], ALU.subtract)
                dve.tensor_tensor(dst[:, 2 * h + 1, :], r_t[:, 1, 0, :], r_t[:, 0, 1, :], ALU.add)\
                    .then_inc(rqk_done, 1)
                dve.wait_ge(rqk_done, n + 1)
                lo(C_RQ + n + 4)
            for c in range(C_RV, C_RV + 8):
                lo(c + 4)
            for h in range(RH_):
                dve.wait_ge(rs_mm, h + 1)
                dve.tensor_tensor(r_sm[:, h, :], ps[:, 4 + h, 0:3 * P],
                                  retc[:, 2 * T + h * 3 * P:2 * T + (h + 1) * 3 * P], ALU.mult).then_inc(rsm_done, 1)
            for c in range(C_RG, C_RG + 4):
                lo(c + 4)

            def r_gated(h):
                dve.wait_ge(rrs, h + 1)
                for t in range(TT):
                    k = 2 * h + t
                    dve.wait_ge(*y_read((Y_RG0, Y_RG1)[h // 2], 2 * t + h % 2))
                    g = r_g[:, t, h * RDV:(h + 1) * RDV]
                    dve.scalar_tensor_tensor(g, ps[:, 4 + k % 4, :], stat[:, 1, k:k + 1], g, ALU.mult, ALU.mult)\
                        .then_inc(ry, 1)

            r_gated(0)
            r_gated(1)
            lo(C_RG + 8)
            split_stage(TR_RA, y_lo, y_hi)
            lo(C_RG + 9)
            lo(C_RG + 10)
            r_gated(2)
            r_gated(3)
            lo(C_RO + 3)
            lo(C_RO + 4)
            split_stage(TR_RB, h_lo, h_hi)
            for c in range(C_RO + 1, C_RO + 6):
                lo(c + 4)

            def add_plain(y, norm):
                for b in range(4):
                    dve.wait_ge(*y_written(y, b))
                    half = slice((b % 2) * 512, (b % 2 + 1) * 512)
                    dve.tensor_tensor(x[:, b // 2, half], x[:, b // 2, half], ps[:, b, :], ALU.add).then_inc(x_done, 1)
                    if b == 2:
                        norm_mean(norm, 0)
                        norm_end(norm, 0)
                norm_mean(norm, 1)
                norm_end(norm, 1)

            add_plain(Y_ROUT, 6)
            norm_split(TR_N5)
            lo(C_RO + 10)
            lo(C_RO + 11)

            def ffn(layer, c0):
                def earlier_taps(g, value):
                    G = GROUPS * layer + g
                    dve.wait_ge(cv_act if value else cg_act, G + 1)
                    for back in (1, 2):
                        for f in range(2):
                            k = COL_CONV + ((layer * 2 + value) * FT + 2 * g + f) * (CONV + 1) + CONV - 1 - back
                            v = f_cv[:, g % 2, value, f, back:T]
                            src = ps[:, 4 + 2 * (g % 2) + value, f * T:(f + 1) * T - back]
                            last = dve.scalar_tensor_tensor(v, src, cols[:, k:k + 1], v, ALU.mult, ALU.add)
                        if back == 1:
                            link(last)
                    last.then_inc(cv_dve if value else cg_dve, 1)

                c = c0 + 4
                for g in range(GROUPS):
                    G = GROUPS * layer + g
                    par = g % 2
                    earlier_taps(g, 0)
                    lo(c)
                    earlier_taps(g, 1)
                    dve.wait_ge(cv_dve, G + 1)
                    dve.wait_ge(fsilu, G + 1)
                    link(dve.tensor_tensor(f_p[:, par, :, :], f_cv[:, par, 0, :, :], f_cv[:, par, 1, :, :], ALU.mult))
                    link(dve.tensor_copy(hid_hi[:, par, :, :], f_p[:, par, :, :]))
                    dve.tensor_tensor(hid_lo[:, par, :, :], f_p[:, par, :, :], hid_hi[:, par, :, :].bitcast(f32),
                                      ALU.subtract).then_inc(hid_done, 1)
                    lo(c + 1)
                    c += 2
                    if 0 < g < GROUPS - 1:
                        lo(c)
                        c += 1

            ffn(0, C_F0)
            add_plain(Y_F0, 7)
            norm_split(TR_N6)
            lo(C_SQ + 2)
            lo(C_SQ + 3)

            for c in range(C_SQ, C_SQ + 10):
                lo(c + 4)

            def s_soft(p):
                dve.wait_ge(sln, p + 1)
                if p >= 3:
                    dve.wait_ge(e_mm, p - 2)
                dve.scalar_tensor_tensor(s_b[:, p % 3, 1, :, :], ps[:, s_bank(p):s_bank(p) + 2, 0:3 * P], 0.0,
                                         s_b[:, p % 3, 0, :, :], ALU.max, ALU.add).then_inc(spm, 1)

            def s_lo(p):
                dve.wait_ge(so_hi, p + 1)
                dve.tensor_tensor(h_lo[:, p, :], ps[:, so_bank(p), 0:T], h_hi[:, p, :].bitcast(f32), ALU.subtract)\
                    .then_inc(so_lo, 1)

            s_soft(0)
            for p in range(SH_ // 2):
                if p + 1 < SH_ // 2:
                    s_soft(p + 1)
                if p >= 1:
                    s_lo(p - 1)
            s_lo(SH_ // 2 - 1)
            lo(C_SV + 6)
            lo(C_SV + 7)
            for c in range(C_SO, C_SO + 2):
                lo(c + 4)
            add_plain(Y_SOUT, 8)
            norm_split(TR_N7)
            lo(C_SO + 6)
            lo(C_SO + 7)
            ffn(1, C_F1)
            add_plain(Y_F1, 9)
            dve.wait_ge(fn_in, 16)
            for t in range(TT):
                dve.wait_ge(rstd_done, TT * 9 + t + 1)
                dve.scalar_tensor_tensor(xn[:, t, :], x[:, t, :], rstd[:, t:t + 1], acc[:, :], ALU.mult, ALU.mult)\
                    .then_inc(fin_done, 1)

        @block.tensor
        def _(pe):
            def chunk_ready(c):
                s, v = slot_visit(c)
                pe.wait_ge(hi_done[s], v + 1)
                pe.wait_ge(lo_done[s], v + 1)
                return s

            def rows(c, lhs_hi, lhs_lo, start, stop, bank_free=None):
                s = chunk_ready(c)

                def step(k, t, n, p):
                    first = start and k == 0 and p == 0
                    if first and bank_free:
                        pe.wait_ge(*bank_free(2 * t + n))
                    lhs = (lhs_hi, lhs_hi, lhs_lo)[p](k, t)
                    w = (w_hi, w_lo, w_hi)[p][:, s, k * D + n * 512:k * D + (n + 1) * 512]
                    return pe.matmul(ps[:, 2 * t + n, :], lhs, w, start=first, stop=stop and k == 1 and p == 2)

                if stop:
                    for t in range(TT):
                        for n in range(2):
                            for k in range(2):
                                for p in range(3):
                                    last = step(k, t, n, p)
                            if 2 * t + n < 3:
                                last.then_inc(y_part, 1)
                else:
                    for k in range(2):
                        for t in range(TT):
                            for p in range(3):
                                for n in range(2):
                                    last = step(k, t, n, p)
                last.then_inc(used[s], 1)

            def h_rows(c, i, n, bank_free=None, hb=h_hi, lb=h_lo, fresh=None):
                kt = 2 * (i % 4)
                if fresh is not None:
                    pe.wait_ge(hl_done, 4 * fresh + i % 4 + 1)
                rows(c, lambda k, t: hb[:, kt + k, t * P:(t + 1) * P], lambda k, t: lb[:, kt + k, t * P:(t + 1) * P],
                     i == 0, i == n - 1, bank_free)

            def cols_chunk(c, bank, fresh=None):
                s = chunk_ready(c)
                for f in range(2):
                    out = ps[:, bank, f * T:(f + 1) * T]
                    for kt in range(KT):
                        if fresh is not None and f == 0 and kt % 2 == 0:
                            pe.wait_ge(hl_done, 4 * fresh + kt // 2 + 1)
                        first = kt * T + f * P
                        wh, wl = w_hi[:, s, first:first + P], w_lo[:, s, first:first + P]
                        pe.matmul(out, wh, h_hi[:, kt, :], start=kt == 0, stop=False)
                        pe.matmul(out, wh, h_lo[:, kt, :], start=False, stop=False)
                        last = pe.matmul(out, wl, h_hi[:, kt, :], start=False, stop=kt == KT - 1)
                last.then_inc(used[s], 1)

            def transposes(stage, src, ready):
                for b in range(4):
                    pe.wait_ge(*ready(b))
                    if stage == TR_RB:
                        pe.wait_ge(hl_done, 4 * TR_RA + b + 1)
                    for j in range(2):
                        for t in range(TT):
                            kt = 2 * b + j
                            last = pe.transpose(ps[:, 4 + b, j * T + t * P:j * T + (t + 1) * P],
                                                src[:, t, kt * P:(kt + 1) * P], ident)
                    last.then_inc(tr_done, 1)

            def norm(n):
                for t in range(TT):
                    pe.wait_ge(nd_done, TT * n + t + 1)
                    for kt in range(KT):
                        b, j = kt // 2, kt % 2
                        last = pe.matmul(ps[:, 4 + b, j * T + t * P:j * T + (t + 1) * P],
                                         x[:, t, kt * P:(kt + 1) * P], nd[:, t, :], start=True, stop=True)
                        if t == TT - 1 and j == 1:
                            last.then_inc(tr_done, 1)

            def sum_part(p, bank):
                pe.wait_ge(ada_step, max(p + 1, 2) * KT)
                if p:
                    pe.wait_ge(mod_done, p)
                for j in range(KT):
                    last = pe.matmul(ps[:, bank, j:j + 1], acc[:, j * P:(j + 1) * P], shp[:, S_ONE:S_ONE + 1],
                                     start=True, stop=True)
                last.then_inc(ada_mm, 1)

            def gate():
                pe.wait_ge(diag_done, 1)
                for j in range(2):
                    last = pe.matmul(ps[:, 6 + j, :], shp[:, S_NO:S_NO + P],
                                     diag[:, 4 * j:4 * j + 4, :].rearrange("p k n -> p (k n)"), start=True, stop=True)
                last.then_inc(gate_mm, 1)

            def row_gate(n):
                pe.wait_ge(ada_step, (ROW_GATES[n] + 1) * KT)
                for j in range(2):
                    last = pe.matmul(ps[:, 6 + j, :], shp[:, S_NO:S_NO + P], acc[:, j * 512:(j + 1) * 512],
                                     start=True, stop=True)
                last.then_inc(ada_mm, 1)

            pe.wait_ge(csil_done, 1)
            for k in range(KT):
                place, landed, fill = early_slot(2 * k + 1)
                pe.wait_ge(landed, fill)
                for j in range(2):
                    last = pe.matmul(ps[0:1, 2 + j, :], csil[:, k:k + 1], place[:, j * 512:(j + 1) * 512],
                                     start=k == 0, stop=k == KT - 1)
                last.then_inc(ada_pe, 1)
                if k == 2:
                    pe.wait_ge(shp_in, 16)
                    norm(0)
            sum_part(0, 0)
            for j in range(KT):
                pe.wait_ge(srow_done, j // 4 + 1)
                last = pe.matmul(ps[:, 1, j:j + 1], srow[0:1, j * P:(j + 1) * P], shp[0:1, S_ONE:S_ONE + 1],
                                 start=True, stop=True)
            last.then_inc(ada_mm, 1)

            pe.wait_ge(wal_done, 1)
            wa = lambda w, kt: w[:, kt * GRANK:(kt + 1) * GRANK]
            for kt in range(KT):
                out = ps[0:GRANK, 4, 0:T]
                if kt % 2 == 0:
                    pe.wait_ge(hl_done, 4 * TR_N0 + kt // 2 + 1)
                pe.matmul(out, wa(g_wah, kt), h_hi[:, kt, :], start=kt == 0, stop=False)
                pe.matmul(out, wa(g_wah, kt), h_lo[:, kt, :], start=False, stop=False)
                last = pe.matmul(out, wa(g_wal, kt), h_hi[:, kt, :], start=False, stop=kt == KT - 1)
            last.then_inc(a_mm, 1)
            h_rows(C_GV, 0, 4, lambda b: (mod_done, 2))
            pe.wait_ge(a_done, 1)
            for h in range(GH_):
                last = pe.matmul(ps[:, 6 + h // 2, (h % 2) * T:(h % 2 + 1) * T], g_w2[0:GRANK, h * GDK:(h + 1) * GDK],
                                 g_a[0:GRANK, :], start=True, stop=True)
            last.then_inc(z_mm, 1)
            for i in range(1, 4):
                h_rows(C_GV + i, i, 4)
            for n in range(2):
                cols_chunk(C_GQ + n, 4 + n)
            for n in range(2):
                pe.wait_ge(c_dve, n + 1)
                cols_chunk(C_GK + n, 4 + n)
                if n == 0:
                    pe.wait_ge(z_done, 1)
                    sum_part(2, 6)
            h_rows(C_GR, 0, 4, lambda b: y_read(Y_GV, b))
            h_rows(C_GR + 1, 1, 4)
            pe.wait_ge(c_dve, 4)
            for b in range(2):
                for h in (2 * b, 2 * b + 1):
                    for t in range(TT):
                        for c in range(2):
                            o = ((h % 2) * 2 + t) * P + c * GCH
                            last = pe.matmul(ps[:, 4 + b, o:o + GCH], g_ki[:, h, t * P:(t + 1) * P],
                                             g_q[:, h, t, c, c * GCH:(c + 1) * GCH], start=True, stop=True)
                last.then_inc(sc_mm, 1)
            sum_part(3, 6)
            pe.wait_ge(mod_done, 4)
            for b in range(2):
                for h in (2 * b, 2 * b + 1):
                    for t in range(TT):
                        o = ((h % 2) * 2 + t) * P
                        last = pe.transpose(ps[:, 6 + b, o:o + P], g_ks[:, h, t * P:(t + 1) * P], ident)
                last.then_inc(kt_mm, 1)
            h_rows(C_GR + 2, 2, 4)

            def chunk_states(h):
                if h < 2:
                    pe.wait_ge(sm_done, 2)
                    pe.wait_ge(kst_done, 2)
                    pe.wait_ge(*y_read(Y_GV, 3))
                else:
                    pe.wait_ge(st_done, h - 1)
                b = 4 + 2 * (h % 2)
                for c, out in enumerate((ps[:, b, 0:GDV], ps[:, b + 1, 0:GDV], ps[:, b, GDV:2 * GDV])):
                    part = slice((c % 2) * GCH, (c % 2 + 1) * GCH)
                    last = pe.matmul(out, g_kst[part, h, c // 2, :], g_v[part, c // 2, h * GDV:(h + 1) * GDV],
                                     start=True, stop=True)
                last.then_inc(kv_mm, 1)

            def g_output(h):
                pe.wait_ge(st_done, h + 1)
                pe.wait_ge(*y_read(Y_GR, h))
                v = lambda t: g_v[:, t, h * GDV:(h + 1) * GDV]
                o0, o1 = ps[:, h, 0:GDV], ps[:, h, GDV:2 * GDV]
                pe.matmul(o0, g_sm[:, h, 0, :], v(0), start=True, stop=False)
                pe.matmul(o0, g_q[:, h, 0, 1, :], g_st[:, h % 2, 0, :], start=False, stop=True)
                pe.matmul(o1, g_sm[:, h, 1, :], v(1), start=True, stop=False)
                pe.matmul(o1, g_q[:, h, 1, 0, :], g_st[:, h % 2, 1, :], start=False, stop=False)
                pe.matmul(o1, g_q[:, h, 1, 1, :], g_st[:, h % 2, 2, :], start=False, stop=True).then_inc(go_mm, 1)

            chunk_states(0)
            chunk_states(1)
            h_rows(C_GR + 3, 3, 4)
            for h in range(GH_):
                g_output(h)
                if h + 2 < GH_:
                    chunk_states(h + 2)
            transposes(TR_GO, g_o, lambda b: (o_done, b + 1))
            h_rows(C_GO, 0, 4, fresh=TR_GO)
            h_rows(C_GO + 1, 1, 4, fresh=TR_GO)
            h_rows(C_GO + 2, 2, 4, fresh=TR_GO)
            pe.wait_ge(hl_done, 4 * (TR_GO + 1))
            pe.wait_ge(mod_done, GA_T)
            row_gate(0)
            h_rows(C_GO + 3, 3, 4)
            norm(1)

            def mlp(layer, c0, with_ada, stage):
                B = UNITS * layer

                def up(u, par, c, later, fresh=None):
                    if later:
                        pe.wait_ge(relu_done, u - 1)
                    cols_chunk(c, 4 + par, fresh)

                def down(u, par, c, start, stop):
                    pe.wait_ge(hid_done, u + 1)
                    rows(c, lambda k, t: hid_hi[:, par, k, t * P:(t + 1) * P],
                         lambda k, t: hid_lo[:, par, k, t * P:(t + 1) * P], start, stop)

                up(B, 0, c0, False, stage)
                up(B + 1, 1, c0 + 1, False)
                down(B, 0, c0 + 2, True, False)
                with pe.Fori(0, MLP_BODIES) as it:
                    for j in range(MLP_UNROLL):
                        u = it * MLP_UNROLL + (B + 2 + j)
                        c = c0 + 3 + 2 * j
                        up(u, j % 2, (c % NSLOT, it * 2 + c // NSLOT), True)
                        if with_ada and j == MLP_UNROLL - 1:
                            pe.wait_ge(ada_step, it * KT + 6 * KT)
                            pe.wait_ge(mod_done, it + 5)
                            for k in range(KT):
                                last = pe.matmul(ps[:, 6, k:k + 1], acc[:, k * P:(k + 1) * P],
                                                 shp[:, S_ONE:S_ONE + 1], start=True, stop=True)
                            last.then_inc(ada_mm, 1)
                        down(u + (-1), (j + 1) % 2, ((c + 1) % NSLOT, it * 2 + (c + 1) // NSLOT), False, False)
                c = c0 + 3 + 2 * MLP_UNROLL * MLP_BODIES
                for i in range(2 + MLP_UNROLL * MLP_BODIES, UNITS):
                    up(B + i, i % 2, c, True)
                    if i == UNITS - 1:
                        gate() if layer == 0 else row_gate(2)
                    down(B + i - 1, (i - 1) % 2, c + 1, False, False)
                    c += 2
                down(B + UNITS - 1, (UNITS - 1) % 2, c, False, True)

            mlp(0, C_M0, True, TR_N1)
            norm(2)

            def d_transposes(src, n):
                for b in range(4):
                    if n:
                        pe.wait_ge(dtr_act, b + 1)
                    for j in range(2):
                        for t in range(TT):
                            kt = 2 * b + j
                            last = pe.transpose(ps[:, 4 + b, j * T + t * P:j * T + (t + 1) * P],
                                                src[:, t, kt * P:(kt + 1) * P], ident)
                    last.then_inc(dtr, 1)

            for i in range(4):
                h_rows(C_DQ + i, i, 4, fresh=TR_N2)
            for i in range(4):
                h_rows(C_DK + i, i, 4, lambda b: y_read(Y_DQ, b))
                if i == 1:
                    sum_part(8, 4)
            pe.wait_ge(rope_q, 1)
            pe.wait_ge(mod_done, 9)
            d_transposes(d_q, 0)
            h_rows(C_DV, 0, 4, lambda b: y_read(Y_DK, b))
            pe.wait_ge(dtr_act, 1)
            sum_part(9, 4)
            h_rows(C_DV + 1, 1, 4)
            pe.wait_ge(rope_k, 1)
            pe.wait_ge(mod_done, 10)
            d_transposes(d_k, 4)
            h_rows(C_DV + 2, 2, 4)
            h_rows(C_DV + 3, 3, 4)

            def d_scores(h):
                if h >= 3:
                    pe.wait_ge(ds_exp, h - 2)
                for i in range(2):
                    f, b = slice(i * DDH, (i + 1) * DDH), d_bank(h) + i
                    pe.matmul(ps[:, b, 0:T], d_qt[f, h, P:T], d_kt[f, h, :], start=True, stop=True)
                    pe.matmul(ps[:, b, T:T + P], d_qt[f, h, 0:P], d_kt[f, h, 0:P], start=False, stop=True,
                              skip_group_check=True)
                    last = pe.matmul(ps[:, b, P:3 * P], maskr[:, 0:P], maskr[:, P:3 * P], start=False, stop=True,
                                     skip_group_check=True)
                last.then_inc(ds_mm, 1)

            pe.wait_ge(mask_done, 1)
            pe.wait_ge(dtr_act, 8)
            pe.wait_ge(*y_read(Y_DV, 3))
            for h in range(3):
                d_scores(h)
            for h in range(DH_):
                par = h % 2
                pe.wait_ge(da_done, h + 1)
                if h:
                    pe.wait_ge(dat_done, h)
                for j in range(3):
                    last = pe.transpose(ps[:, 1, j * P:(j + 1) * P], d_a[:, par, j * P:(j + 1) * P], ident)
                last.then_inc(dat_mm, 1)
                if h + 3 < DH_:
                    d_scores(h + 3)
                pe.wait_ge(dat_done, h + 1)
                if h:
                    pe.wait_ge(do_act, h)
                v = lambda t: d_v[:, t, h * DDV:(h + 1) * DDV]
                o = lambda t: ps[:, 0, par * T + t * P:par * T + (t + 1) * P]
                pe.matmul(o(1), d_at[:, par, 0:P], v(0), start=True, stop=False)
                pe.matmul(o(1), d_at[:, par, P:2 * P], v(1), start=False, stop=True)
                pe.matmul(o(0), d_at[:, par, 2 * P:3 * P], v(0), start=True, stop=True).then_inc(do_mm, 1)
            transposes(TR_DO, d_o, lambda b: (o_done, GH_ + 2 * b + 2))
            h_rows(C_DO, 0, 4, fresh=TR_DO)
            h_rows(C_DO + 1, 1, 4, fresh=TR_DO)
            h_rows(C_DO + 2, 2, 4, fresh=TR_DO)
            pe.wait_ge(hl_done, 4 * (TR_DO + 1))
            row_gate(1)
            h_rows(C_DO + 3, 3, 4)
            norm(3)
            mlp(1, C_M1, False, TR_N3)
            norm(4)

            for n in range(2 * RH_):
                if n >= 4:
                    pe.wait_ge(c_dve, N_C_RET + n - 3)
                cols_chunk(C_RQ + n, 4 + n % 4, None if n else TR_N4)
            for i in range(4):
                h_rows(C_RV + i, i, 4)
            for i in range(4):
                h_rows(C_RV + 4 + i, i, 4, lambda b: y_read(Y_RV0, b))
            pe.wait_ge(rqk_done, 2 * RH_)
            for h in range(RH_):
                for first, keys, queries in ((0, slice(0, P), slice(0, T)), (T, slice(P, T), slice(P, T))):
                    n = queries.stop - queries.start
                    for kk in range(2):
                        last = pe.matmul(ps[:, 4 + h, first:first + n], r_k[:, 2 * h + kk, keys],
                                         r_q[:, 2 * h + kk, queries], start=kk == 0, stop=kk == 1)
                last.then_inc(rs_mm, 1)
            for i in range(4):
                h_rows(C_RG + i, i, 4, lambda b: y_read(Y_RV1, b))

            def r_outputs(first):
                for k in range(first, first + 4):
                    h, t = k // 2, k % 2
                    v = lambda t: r_v[:, t, h * RDV:(h + 1) * RDV]
                    out = ps[:, 4 + k % 4, :]
                    last = pe.matmul(out, r_sm[:, h, t * P:(t + 1) * P], v(0), start=True, stop=t == 0)
                    if t:
                        last = pe.matmul(out, r_sm[:, h, 2 * P:3 * P], v(1), start=False, stop=True)
                    last.then_inc(ro_mm, 1)

            g_rows = lambda i: h_rows(C_RG + 4 + i, i, 4, lambda b: y_read(Y_RG0, b))
            pe.wait_ge(rsm_done, RH_)
            r_outputs(0)
            g_rows(0)
            g_rows(1)
            transposes(TR_RA, r_g[:, :, 0:D], lambda b: (ry, 4))
            g_rows(2)
            pe.wait_ge(hl_done, 4 * (TR_RA + 1))
            r_outputs(4)
            g_rows(3)
            for i in range(2):
                h_rows(C_RO + i, i, 8, lambda b: y_read(Y_RG1, b), y_hi, y_lo)
            transposes(TR_RB, r_g[:, :, D:2 * D], lambda b: (ry, 2 * (b // 2) + 6))
            for i in range(2, 4):
                h_rows(C_RO + i, i, 8, None, y_hi, y_lo)
            for i in range(4, 8):
                h_rows(C_RO + i, i, 8, fresh=TR_RB)
            norm(5)

            def ffn(layer, c0, stage):
                B = GROUPS * layer

                def up(g, value):
                    if g >= 2:
                        pe.wait_ge(cv_dve if value else cg_dve, B + g - 1)
                    cols_chunk(ffn_chunk(c0, g, value), 4 + 2 * (g % 2) + value, None if g or value else stage)

                def down(g):
                    pe.wait_ge(hid_done, 2 * UNITS + B + g + 1)
                    rows(ffn_chunk(c0, g, 2), lambda k, t: hid_hi[:, g % 2, k, t * P:(t + 1) * P],
                         lambda k, t: hid_lo[:, g % 2, k, t * P:(t + 1) * P], g == 0, g == GROUPS - 1)

                for g in range(GROUPS):
                    up(g, 0)
                    up(g, 1)
                    if g:
                        down(g - 1)
                down(GROUPS - 1)

            ffn(0, C_F0, TR_N5)
            norm(6)

            for n in range(8):
                if n >= 4:
                    pe.wait_ge(c_act, n - 3)
                cols_chunk(C_SQ + n, 4 + n % 4, None if n else TR_N6)
            for i in range(3):
                h_rows(C_SV + i, i, 4)

            def s_scores(p):
                if p >= 3:
                    pe.wait_ge(sexp, p - 2)
                for i in range(2):
                    f, b = slice(i * SDH, (i + 1) * SDH), s_bank(p) + i
                    pe.matmul(ps[:, b, 0:T], s_k[f, p, 0:P], s_q[f, p, :], start=True, stop=True)
                    pe.matmul(ps[:, b, T:T + P], s_k[f, p, P:T], s_q[f, p, P:T], start=False, stop=True,
                              skip_group_check=True)
                    for first in (0, T):
                        last = pe.matmul(ps[:, b, first:first + P], maskr[:, 0:P], maskr[:, 3 * P:4 * P],
                                         start=False, stop=True, skip_group_check=True)
                last.then_inc(z_ready, 1)

            def s_weights(p):
                pe.wait_ge(spm, p + 1)
                for i in range(2):
                    sums, b = s_b[:, p % 3, 1, i, :], s_bank(p) + i
                    pe.matmul(ps[:, b, 0:3 * P], shp[:, S_NU:S_NU + P], sums, start=False, stop=True,
                              skip_group_check=True)
                    last = pe.matmul(ps[:, b, P:2 * P], shp[:, S_NO:S_NO + P], sums[:, 2 * P:3 * P], start=False,
                                     stop=True, skip_group_check=True)
                last.then_inc(e_mm, 1)

            def s_output(p):
                pe.wait_ge(sexp, p + 1)
                if p >= 2:
                    pe.wait_ge(so_lo, p - 1)
                for i in range(2):
                    f, h = slice(i * SDH, (i + 1) * SDH), 2 * p + i
                    a = s_b[:, p % 3, 0, i, :]
                    pe.matmul(ps[f, so_bank(p), 0:T], s_v[:, 0, h * SDH:(h + 1) * SDH], a[:, 0:T], start=True, stop=False)
                    last = pe.matmul(ps[f, so_bank(p), P:T], s_v[:, 1, h * SDH:(h + 1) * SDH], a[:, T:T + P],
                                     start=False, stop=True)
                last.then_inc(so_mm, 1)

            pe.wait_ge(c_act, 8)
            s_scores(0)
            s_scores(1)
            h_rows(C_SV + 3, 3, 4)
            s_weights(0)
            pe.wait_ge(*y_read(Y_SV, 3))
            s_scores(2)
            for p in range(SH_ // 2):
                if p + 1 < SH_ // 2:
                    s_weights(p + 1)
                s_output(p)
                if p + 3 < SH_ // 2:
                    s_scores(p + 3)
            pe.wait_ge(so_lo, 6)
            for i in range(4):
                pe.wait_ge(so_lo, 2 * i + 2)
                h_rows(C_SO + i, i, 4)
            norm(7)
            ffn(1, C_F1, TR_N7)


def shape_constants():
    shp = np.zeros((P, NSHP), np.float32)
    r, c = np.arange(P)[:, None], np.arange(P)[None, :]
    shp[:, S_ID:S_ID + P] = r == c
    shp[:, S_GLAM:S_GLAM + P] = (r <= c) & (r // GCH == c // GCH)
    shp[:, S_SCAN:S_SCAN + T] = np.arange(T) % GCH != 0
    shp[:, S_CAUS:S_CAUS + 2 * P] = np.tile(np.where(c <= r, 0.0, NEG), 2)
    shp[:, S_SBM:S_SBM + P] = np.where(r < c, 0.0, NEG)
    shp[:, S_NU:S_NU + P] = np.where(r >= c, -1.0, 0.0)
    shp[:, S_NO:S_NO + P] = -1.0
    shp[:, S_INVF:S_INVF + 8] = np.float32(ROPE_THETA) ** (-np.arange(0, ROPE_DIM, 2, dtype=np.float32) / ROPE_DIM)
    shp[:, S_ONE] = 1.0
    shp[:, S_HALF:S_HALF + 8] = -0.5
    retc = np.zeros((P, NRETC), np.float32)
    inv = np.float32(10000.0) ** (-np.arange(0, RDK, 2, dtype=np.float32) / RDK)
    angle = np.arange(T, dtype=np.float32)[None, :] * inv[:, None]
    retc[:, 0:T], retc[:, T:2 * T] = np.cos(angle), np.sin(angle)
    log_g = np.log(1.0 - 2.0 ** (-5.0 - np.arange(RH_)))
    for h in range(RH_):
        d = retc[:, 2 * T + h * 3 * P:2 * T + (h + 1) * 3 * P]
        now = np.where(c >= r, np.exp(np.maximum(c - r, 0) * log_g[h]), 0.0)
        d[:, 0:P] = now
        d[:, P:2 * P] = np.exp((c + P - r) * log_g[h])
        d[:, 2 * P:3 * P] = now
    retc[:, 2 * T:] *= RDK ** -0.5
    return shp, retc


def stream(inputs):
    def cols(w, first, n):
        w = w[:, first:first + n].reshape(KT, P, n // 256, 256)
        return list(w.transpose(2, 1, 0, 3).reshape(n // 256, P, CHUNK))

    def rows(w, first=0, n=D):
        w = w[:, first:first + n]
        k = w.shape[0] // 256
        return list(w.reshape(k, 2, P, n).transpose(0, 2, 1, 3).reshape(k, P, CHUNK))

    out = []
    g = inputs["gla_w_in"][0]
    hk = GH_ * GDK
    out += rows(g, 2 * hk) + cols(g, 0, hk) + cols(g, hk, hk) + rows(g, 2 * hk + D) + rows(inputs["gla_w_o"][0])

    def mlp(layer):
        up, down = cols(inputs["mlp_w1"][layer], 0, F_MLP), rows(inputs["mlp_w2"][layer])
        res = [up[0]]
        for i in range(1, UNITS):
            res += [up[i], down[i - 1]]
        return res + [down[-1]]

    out += mlp(0)
    d = inputs["diff_w_in"][0]
    out += rows(d, 0) + rows(d, D) + rows(d, 2 * D) + rows(inputs["diff_w_o"][0])
    out += mlp(1)
    r = inputs["ret_w_in_2"][0]
    qk = RH_ * RDK
    out += cols(r, 0, qk) + cols(r, qk, qk)
    for n in range(4):
        out += rows(r, 2 * qk + n * D)
    out += rows(inputs["ret_w_out_2"][0])

    def ffn(layer):
        w = inputs["ffn_w_up_2"][layer]
        gate, value, down = cols(w, 0, F_FFN), cols(w, F_FFN, F_FFN), rows(inputs["ffn_w_down_2"][layer])
        res = [gate[0], value[0]]
        for i in range(1, GROUPS):
            res += [gate[i], value[i], down[i - 1]]
        return res + [down[-1]]

    out += ffn(0)
    s = inputs["sb_w_in_2"][0]
    out += cols(s, 0, D) + cols(s, D, D) + rows(s, 2 * D) + rows(inputs["sb_w_out_2"][0])
    out += ffn(1)
    assert len(out) == NCHUNK
    return np.concatenate(out, axis=0)


def kernel(**inputs):
    import concourse.bacc as bacc
    from concourse.bass_utils import run_bass_kernel_spmd as run

    a = {k: np.asarray(v) for k, v in inputs.items()}
    per_feature = lambda v: v.reshape(-1, P).T
    on_all = lambda v: np.broadcast_to(v.reshape(1, -1), (P, v.size))
    conv = np.concatenate([a["ffn_conv_w_2"], a["ffn_conv_b_2"][:, None, :]], axis=1)
    conv = conv.reshape(DEPTH, CONV + 1, 2 * FT, P).transpose(3, 0, 2, 1).reshape(P, -1)
    ada_b = a["ada_b"].reshape(DEPTH, 6, D)[:, PART_OF].reshape(ADA_PARTS, D)
    a["ada_b"] = ada_b
    cols = np.concatenate([per_feature(a[n]) for n in ("c", "ada_b", "norm_g", "ret_norm_2", "ffn_norm_2", "sb_norm_2",
                                                        "gla_b_a")] + [conv], axis=1)
    assert cols.shape == (P, NCOL)
    ada_w = a["ada_w"].reshape(DEPTH, D, 6, D).transpose(0, 2, 1, 3)[:, PART_OF].reshape(ADA_PARTS * D, D)
    shp, retc = shape_constants()
    w_in = a["gla_w_in"][0]
    arrays = {
        "x": a["x"].reshape(TT, P, D).transpose(1, 0, 2),
        "positions": a["positions"].reshape(TT, P).T,
        "stream": stream(a),
        "ada_w": ada_w,
        "cols": cols,
        "shp": shp,
        "retc": retc,
        "w_a": w_in[:, w_in.shape[1] - GRANK:].reshape(KT, P, GRANK).transpose(1, 0, 2).reshape(P, KT * GRANK),
        "w_a2": a["gla_w_a2"][0],
        "b_r": on_all(a["gla_b_r"]),
        "gla_norm": on_all(a["gla_norm_g"]),
        "lam": on_all(a["diff_lambda"]),
        "subln": on_all(a["diff_subln_g"]),
        "gate_b": np.repeat(ada_b[list(ROW_GATES)], P, axis=0),
        "final_g": on_all(a["final_g"]),
        "final_norm": on_all(a["final_norm_2"]),
    }
    nc = bacc.Bacc("TRN2", target_bir_lowering=False, num_devices=1)
    arrays = {f"in_{k}": np.ascontiguousarray(v) for k, v in arrays.items()}
    args = [nc.dram_tensor(k, v.shape, mybir.dt.from_np(v.dtype), kind="ExternalInput").ap() for k, v in arrays.items()]
    out = nc.dram_tensor("out", (T, D), mybir.dt.float32, kind="ExternalOutput").ap()
    build(nc, *args, out)
    r = run(nc, [arrays], core_ids=[0])
    return r.results[0]["out"].reshape(1, T, D)
```
